# Optimizing a Trainium2 kernel written in Bass

```python
import jax, jax.numpy as jnp
from jax import lax
import numpy as np

D_MODEL = 1024
BATCH = 1
SEQ = 256
DEPTH = 2

CHUNK = 64
PLE_DIM = 256
D_FF = 2752
EPS = 1e-6
N_EVEN = (DEPTH + 1) // 2
N_ODD = DEPTH // 2

GDN_HEADS = 4
GDN_DK = 128
GDN_DV = 128
GDN_CONV = 4
GDN_QK = GDN_HEADS * GDN_DK
GDN_VW = GDN_HEADS * GDN_DV

MLA_HEADS = 4
MLA_Q_LORA = 384
MLA_KV_LORA = 256
MLA_NOPE = 128
MLA_ROPE = 64
MLA_V = 128
MLA_QBLOCK = 128
ROPE_THETA = 10000.0

SWA_HEADS = 16
SWA_KV_HEADS = 4
SWA_HEAD_DIM = 64
SWA_WINDOW = 128
SWA_WIN_CHUNKS = SWA_WINDOW // CHUNK
SWA_QKV = (SWA_HEADS + 2 * SWA_KV_HEADS) * SWA_HEAD_DIM

IN0_SIZES = (GDN_QK, GDN_QK, GDN_VW, GDN_VW, GDN_HEADS, GDN_HEADS, MLA_Q_LORA, MLA_KV_LORA, MLA_ROPE)
IN0_WIDTH = sum(IN0_SIZES)
MIX0_WIDTH = GDN_VW + MLA_HEADS * MLA_V

kernel_name = 'hybrid_streaming_encoder_block'

def _rms(x):
    xf = x.astype(jnp.float32)
    return (xf * lax.rsqrt(jnp.mean(xf * xf, axis=-1, keepdims=True) + EPS)).astype(x.dtype)

def rmsnorm(x, w):
    return _rms(x) * w

def l2norm(x):
    xf = x.astype(jnp.float32)
    return xf * lax.rsqrt(jnp.sum(xf * xf, axis=-1, keepdims=True) + EPS)

def swiglu(x, w_gu, w_down):
    g, u = jnp.split(x @ w_gu, 2, axis=-1)
    return (jax.nn.silu(g) * u) @ w_down

def causal_dwconv(x, w):
    k_w, c = w.shape
    return lax.conv_general_dilated(x, w[:, None, :], window_strides=(1,), padding=[(k_w - 1, 0)],
                                    dimension_numbers=('NWC', 'WIO', 'NWC'), feature_group_count=c)

def rope(x, pos):
    half = x.shape[-1] // 2
    inv = ROPE_THETA ** (-jnp.arange(half, dtype=jnp.float32) / half)
    ang = pos.astype(jnp.float32)[:, None] * inv[None, :]
    cos, sin = jnp.cos(ang)[:, None, :], jnp.sin(ang)[:, None, :]
    xf = x.astype(jnp.float32)
    x1, x2 = xf[..., :half], xf[..., half:]
    return jnp.concatenate([x1 * cos - x2 * sin, x2 * cos + x1 * sin], axis=-1).astype(x.dtype)

def gated_delta_rule(q, k, v, g, beta):
    b_, s_, h_, dk = q.shape
    dv = v.shape[-1]
    n = s_ // CHUNK

    def blk(t):
        return jnp.moveaxis(t.reshape((b_, n, CHUNK, h_) + t.shape[3:]), 3, 1)

    q, k, v, g, beta = blk(q) * dk ** -0.5, blk(k), blk(v), blk(g), blk(beta)
    gc = jnp.cumsum(g, axis=-1)
    idx = jnp.arange(CHUNK)
    lower = idx[:, None] >= idx[None, :]
    strict = idx[:, None] > idx[None, :]
    decay = jnp.exp(jnp.where(lower, gc[..., :, None] - gc[..., None, :], -jnp.inf))
    kb = k * beta[..., None]
    l_mat = jnp.where(strict, jnp.einsum('bhncd,bhnjd->bhncj', kb, k) * decay, 0.0)
    rhs = jnp.concatenate([v * beta[..., None], kb * jnp.exp(gc)[..., None]], axis=-1)
    sol = lax.linalg.triangular_solve(l_mat + jnp.eye(CHUNK, dtype=l_mat.dtype), rhs,
                                      left_side=True, lower=True, unit_diagonal=True)
    u, w = sol[..., :dv], sol[..., dv:]
    attn = jnp.einsum('bhncd,bhnjd->bhncj', q, k) * decay
    g_last = gc[..., -1]
    q_dec = q * jnp.exp(gc)[..., None]
    k_dec = k * jnp.exp(g_last[..., None] - gc)[..., None]

    def step(state, xs):
        qd, kd, uu, ww, at, gl = xs
        v_new = uu - jnp.einsum('bhcd,bhde->bhce', ww, state)
        o = jnp.einsum('bhcd,bhde->bhce', qd, state) + jnp.einsum('bhcj,bhje->bhce', at, v_new)
        state = state * jnp.exp(gl)[..., None, None] + jnp.einsum('bhcd,bhce->bhde', kd, v_new)
        return state, o

    xs = tuple(jnp.moveaxis(t, 2, 0) for t in (q_dec, k_dec, u, w, attn, g_last))
    state0 = jnp.zeros((b_, h_, dk, dv), q.dtype)
    _, o = lax.scan(step, state0, xs)
    return jnp.transpose(o, (1, 0, 3, 2, 4)).reshape(b_, s_, h_, dv)

def mla_attention(q, k, v):
    b_, s_, h_, dqk = q.shape
    nb = s_ // MLA_QBLOCK
    scale = dqk ** -0.5
    kpos = jnp.arange(s_)
    qb = jnp.swapaxes(q.reshape(b_, nb, MLA_QBLOCK, h_, dqk), 0, 1)
    starts = jnp.arange(nb) * MLA_QBLOCK

    def block(args):
        qi, s0 = args
        qpos = s0 + jnp.arange(MLA_QBLOCK)
        limit = (qpos // CHUNK + 1) * CHUNK
        mask = kpos[None, :] < limit[:, None]
        s = jnp.einsum('bqhd,bkhd->bhqk', qi, k).astype(jnp.float32) * scale
        s = jnp.where(mask[None, None], s, -jnp.inf)
        pr = jax.nn.softmax(s, axis=-1).astype(v.dtype)
        return jnp.einsum('bhqk,bkhd->bqhd', pr, v)

    o = lax.map(block, (qb, starts))
    return jnp.swapaxes(o, 0, 1).reshape(b_, s_, h_, v.shape[-1])

def swa_sink_attention(q, k, v, sinks):
    b_, s_, hq, d = q.shape
    hkv = k.shape[2]
    grp = hq // hkv
    n = s_ // CHUNK
    qc = q.reshape(b_, n, CHUNK, hkv, grp, d)

    def band(t):
        tc = t.reshape(b_, n, CHUNK, hkv, d)
        parts = [jnp.pad(tc, ((0, 0), (sh, 0), (0, 0), (0, 0), (0, 0)))[:, :n]
                 for sh in range(SWA_WIN_CHUNKS - 1, -1, -1)]
        return jnp.concatenate(parts, axis=2)

    kb, vb = band(k), band(v)
    key_chunk = jnp.arange(n)[:, None] - jnp.arange(SWA_WIN_CHUNKS - 1, -1, -1)[None, :]
    valid = jnp.repeat(key_chunk >= 0, CHUNK, axis=1)
    s = jnp.einsum('bnqhgd,bnkhd->bnhgqk', qc, kb).astype(jnp.float32) * d ** -0.5
    s = jnp.where(valid[None, :, None, None, None, :], s, -jnp.inf)
    sink = jnp.broadcast_to(sinks.astype(jnp.float32).reshape(hkv, grp)[None, None, :, :, None, None],
                            s.shape[:-1] + (1,))
    pr = jax.nn.softmax(jnp.concatenate([s, sink], axis=-1), axis=-1)[..., :-1].astype(v.dtype)
    o = jnp.einsum('bnhgqk,bnkhd->bnqhgd', pr, vb)
    return o.reshape(b_, s_, hq, d)

def even_mixer(h, pos, w_in, conv_w, a_log, dt_bias, out_norm, q_norm, w_uq, kv_norm, w_ukv, w_out):
    b_, s_, _ = h.shape
    points = np.cumsum(IN0_SIZES)[:-1].tolist()
    q, k, v, z, a, bt, cq, ckv, kr = jnp.split(h @ w_in, points, axis=-1)
    qkv = jax.nn.silu(causal_dwconv(jnp.concatenate([q, k, v], axis=-1), conv_w))
    q, k, v = jnp.split(qkv, [GDN_QK, 2 * GDN_QK], axis=-1)
    qa = l2norm(q.reshape(b_, s_, GDN_HEADS, GDN_DK))
    ka = l2norm(k.reshape(b_, s_, GDN_HEADS, GDN_DK))
    va = v.reshape(b_, s_, GDN_HEADS, GDN_DV).astype(jnp.float32)
    g = -jnp.exp(a_log.astype(jnp.float32)) * jax.nn.softplus(a.astype(jnp.float32) + dt_bias.astype(jnp.float32))
    beta = jax.nn.sigmoid(bt.astype(jnp.float32))
    o_a = gated_delta_rule(qa, ka, va, g, beta).astype(h.dtype)
    o_a = (rmsnorm(o_a, out_norm) * jax.nn.silu(z.reshape(b_, s_, GDN_HEADS, GDN_DV))).reshape(b_, s_, GDN_VW)
    qm = (rmsnorm(cq, q_norm) @ w_uq).reshape(b_, s_, MLA_HEADS, MLA_NOPE + MLA_ROPE)
    q_nope, q_rope = qm[..., :MLA_NOPE], rope(qm[..., MLA_NOPE:], pos)
    kvm = (rmsnorm(ckv, kv_norm) @ w_ukv).reshape(b_, s_, MLA_HEADS, MLA_NOPE + MLA_V)
    k_nope, v_b = kvm[..., :MLA_NOPE], kvm[..., MLA_NOPE:]
    k_rope = jnp.broadcast_to(rope(kr[:, :, None, :], pos), (b_, s_, MLA_HEADS, MLA_ROPE))
    o_b = mla_attention(jnp.concatenate([q_nope, q_rope], axis=-1),
                        jnp.concatenate([k_nope, k_rope], axis=-1), v_b).reshape(b_, s_, MLA_HEADS * MLA_V)
    return jnp.concatenate([o_a, o_b], axis=-1) @ w_out

def odd_mixer(h, w_qkv, b_qkv, sinks, w_o, b_o):
    b_, s_, _ = h.shape
    qkv = h @ w_qkv + b_qkv
    nq = SWA_HEADS * SWA_HEAD_DIM
    nk = SWA_KV_HEADS * SWA_HEAD_DIM
    q, k, v = jnp.split(qkv, [nq, nq + nk], axis=-1)
    o = swa_sink_attention(q.reshape(b_, s_, SWA_HEADS, SWA_HEAD_DIM),
                           k.reshape(b_, s_, SWA_KV_HEADS, SWA_HEAD_DIM),
                           v.reshape(b_, s_, SWA_KV_HEADS, SWA_HEAD_DIM), sinks)
    return o.reshape(b_, s_, nq) @ w_o + b_o

def setup_inputs(seed: int = 0) -> dict:
    key = jax.random.key(seed)
    ks = list(jax.random.split(key, 40))

    def nk():
        return ks.pop()

    def w(shape, fan_in):
        return jax.random.normal(nk(), shape, jnp.float32) * fan_in ** -0.5

    def gain(shape):
        return 1.0 + 0.02 * jax.random.normal(nk(), shape, jnp.float32)

    def small(shape, s=0.02):
        return s * jax.random.normal(nk(), shape, jnp.float32)

    dt = jnp.exp(jax.random.uniform(nk(), (N_EVEN, GDN_HEADS), jnp.float32, np.log(1e-3), np.log(1e-1)))
    dt_bias = dt + jnp.log(-jnp.expm1(-dt))
    return {
        'x': jax.random.normal(nk(), (BATCH, SEQ, D_MODEL), jnp.float32),
        'p': jax.random.normal(nk(), (DEPTH, BATCH, SEQ, PLE_DIM), jnp.float32),
        'ffn1_pre': gain((DEPTH, D_MODEL)),
        'ffn1_wgu': w((DEPTH, D_MODEL, 2 * D_FF), D_MODEL),
        'ffn1_wd': w((DEPTH, D_FF, D_MODEL), D_FF),
        'ffn1_post': gain((DEPTH, D_MODEL)),
        'mix_pre': gain((DEPTH, D_MODEL)),
        'mix_post': gain((DEPTH, D_MODEL)),
        'ffn2_pre': gain((DEPTH, D_MODEL)),
        'ffn2_wgu': w((DEPTH, D_MODEL, 2 * D_FF), D_MODEL),
        'ffn2_wd': w((DEPTH, D_FF, D_MODEL), D_FF),
        'ffn2_post': gain((DEPTH, D_MODEL)),
        'ple_gate_w': w((DEPTH, D_MODEL, D_MODEL), D_MODEL),
        'ple_gate_b': small((DEPTH, D_MODEL)),
        'ple_proj': w((DEPTH, PLE_DIM, D_MODEL), PLE_DIM),
        'ple_norm': gain((DEPTH, D_MODEL)),
        'ab_w_in': w((N_EVEN, D_MODEL, IN0_WIDTH), D_MODEL),
        'gdn_conv': w((N_EVEN, GDN_CONV, 2 * GDN_QK + GDN_VW), GDN_CONV),
        'gdn_a_log': jnp.log(jax.random.uniform(nk(), (N_EVEN, GDN_HEADS), jnp.float32, 1.0, 16.0)),
        'gdn_dt_bias': dt_bias,
        'gdn_out_norm': gain((N_EVEN, GDN_DV)),
        'mla_q_norm': gain((N_EVEN, MLA_Q_LORA)),
        'mla_w_uq': w((N_EVEN, MLA_Q_LORA, MLA_HEADS * (MLA_NOPE + MLA_ROPE)), MLA_Q_LORA),
        'mla_kv_norm': gain((N_EVEN, MLA_KV_LORA)),
        'mla_w_ukv': w((N_EVEN, MLA_KV_LORA, MLA_HEADS * (MLA_NOPE + MLA_V)), MLA_KV_LORA),
        'ab_w_out': w((N_EVEN, MIX0_WIDTH, D_MODEL), MIX0_WIDTH),
        'swa_w_qkv': w((N_ODD, D_MODEL, SWA_QKV), D_MODEL),
        'swa_b_qkv': small((N_ODD, SWA_QKV)),
        'swa_sinks': small((N_ODD, SWA_HEADS), 0.5),
        'swa_w_o': w((N_ODD, SWA_HEADS * SWA_HEAD_DIM, D_MODEL), SWA_HEADS * SWA_HEAD_DIM),
        'swa_b_o': small((N_ODD, D_MODEL)),
    }

def reference(x, p, ffn1_pre, ffn1_wgu, ffn1_wd, ffn1_post, mix_pre, mix_post, ffn2_pre, ffn2_wgu, ffn2_wd,
              ffn2_post, ple_gate_w, ple_gate_b, ple_proj, ple_norm, ab_w_in, gdn_conv, gdn_a_log, gdn_dt_bias,
              gdn_out_norm, mla_q_norm, mla_w_uq, mla_kv_norm, mla_w_ukv, ab_w_out, swa_w_qkv, swa_b_qkv,
              swa_sinks, swa_w_o, swa_b_o):
    pos = jnp.arange(x.shape[1])
    for i in range(DEPTH):
        j = i // 2
        x = x + 0.5 * rmsnorm(swiglu(rmsnorm(x, ffn1_pre[i]), ffn1_wgu[i], ffn1_wd[i]), ffn1_post[i])
        h = rmsnorm(x, mix_pre[i])
        if i % 2 == 0:
            m = even_mixer(h, pos, ab_w_in[j], gdn_conv[j], gdn_a_log[j], gdn_dt_bias[j], gdn_out_norm[j],
                           mla_q_norm[j], mla_w_uq[j], mla_kv_norm[j], mla_w_ukv[j], ab_w_out[j])
        else:
            m = odd_mixer(h, swa_w_qkv[j], swa_b_qkv[j], swa_sinks[j], swa_w_o[j], swa_b_o[j])
        x = x + rmsnorm(m, mix_post[i])
        x = x + 0.5 * rmsnorm(swiglu(rmsnorm(x, ffn2_pre[i]), ffn2_wgu[i], ffn2_wd[i]), ffn2_post[i])
        gate = jax.nn.sigmoid(_rms(x) @ ple_gate_w[i] + ple_gate_b[i])
        x = x + gate * rmsnorm(p[i] @ ple_proj[i], ple_norm[i])
    return x


_drawn_inputs = setup_inputs


def setup_inputs(seed=0):
    import zlib

    import numpy as np

    out = dict(_drawn_inputs(seed))
    spreads = {}
    factors = {'ffn1_pre': 2.761,
     'ffn1_post': 3.975,
     'mix_post': 3.116,
     'ffn2_pre': 4.833,
     'ffn2_post': 7.102,
     'ple_gate_b': 8.0,
     'ple_norm': 6.616,
     'gdn_out_norm': 4.132,
     'mla_q_norm': 8.0,
     'mla_kv_norm': 7.987,
     'swa_sinks': 8.0}
    for name, (base, spread) in spreads.items():
        noise = np.random.default_rng([zlib.crc32(name.encode()), seed]).standard_normal(out[name].shape)
        drawn = base * np.exp(spread * noise) if base else spread * noise
        out[name] = __import__('jax').numpy.asarray(drawn.astype(out[name].dtype))
    for name, factor in factors.items():
        out[name] = (out[name] * factor).astype(out[name].dtype)
    return out
```

```python
from contextlib import ExitStack

import numpy as np

import concourse.bass as bass
from concourse import mybir

F32 = mybir.dt.float32
F32R = mybir.dt.float32r
I32 = mybir.dt.int32
ALU = mybir.AluOpType
ACT = mybir.ActivationFunctionType
AX = mybir.AxisListType

P = 128
SEQ = 256
TT = SEQ // P
D = 1024
KD = D // P
BANK = 512
D_FF = 2752
FULL = D_FF // P
HALF = D_FF - FULL * P
TILES = FULL + 1
PLE = 256
KP = PLE // P
CHUNK = 64
EPS = 1e-6
RSQRT_MAGIC = float(0x5F3759DF)

RING = 6
AHEAD = 4
SLAB = 1024

COL_FFN1, COL_MIX, COL_FFN2, COL_CONV = 0, 16, 32, 48
COL_QN, COL_KVN, COL_BQK, COL_ONE = 96, 99, 101, 111
CONSTS = ["ident", "upto", "same", "first", "second", "add_upto", "add_before"]
C_AT = {name: P * i for i, name in enumerate(CONSTS)}
LEVELS = 6
C_LEVEL = P * len(CONSTS)
C_COS = C_LEVEL + P * LEVELS
C_SIN = C_COS + 64
C_ALL = C_SIN + 64


def shape_constants():
    r = np.arange(P)
    row, col = r[:, None], r[None, :]
    same = (row // CHUNK) == (col // CHUNK)
    blocks = {
        "ident": row == col,
        "upto": same & (row <= col),
        "same": same,
        "first": (row < CHUNK) & (col >= 0),
        "second": (row >= CHUNK) & (col >= 0),
        "add_upto": np.where(same & (row <= col), 0.0, -1e30),
        "add_before": np.where(same & (col < row), 0.0, 1e30),
    }
    out = [np.asarray(blocks[n], np.float32) for n in CONSTS]
    for level in range(LEVELS):
        b = 1 << level
        pair = (row // (2 * b) == col // (2 * b)) & ((row // b) % 2 == 0) & ((col // b) % 2 == 1)
        out.append(np.where(pair, -1.0, 0.0).astype(np.float32))
    half = 32
    inv = np.float32(10000.0) ** (-np.arange(half, dtype=np.float32) / np.float32(half))
    ang = np.arange(SEQ, dtype=np.float32)[:, None] * inv[None, :].astype(np.float32)
    for fn in (np.cos, np.sin):
        out.append(fn(ang).astype(np.float32).reshape(TT, P, half).transpose(1, 0, 2).reshape(P, TT * half))
    return np.ascontiguousarray(np.concatenate(out, axis=1))


class Slabs:

    def __init__(self):
        self.load = []
        self.size = []
        self.loaded = []
        self.total = [0] * RING

    def add(self, parts, width, pieces):
        n = len(self.load)
        self.load.append(pieces)
        self.size.append((parts, width))
        self.total[n % RING] += 16 * len(pieces)
        self.loaded.append(self.total[n % RING])
        return n


def k_rows(w, k, c0=0, c1=None):
    return w[k * P:(k + 1) * P, c0:(w.shape[1] if c1 is None else c1)]


def encoder(nc, io, out, phases):
    ctx = ExitStack()
    with ctx:
        def sem(name):
            return ctx.enter_context(nc.semaphore(name))

        origin = -(-nc.sbuf_base // 32) * 32
        ctx.enter_context(nc.sbuf_tensor("fence", [P, 207 * 256], F32))

        def at_kb(name, kb, shape, dt=F32):
            return nc.alloc_sbuf_tensor_at(name, shape, dt, offset=origin + int(kb * 1024))

        raw = at_kb("raw", 0, [P, RING, SLAB])
        hi = at_kb("hi", 24, [P, RING, SLAB], F32R)
        lo = at_kb("lo", 48, [P, RING, SLAB], F32R)
        x = at_kb("x", 72, [P, TT, D])
        xn = at_kb("xn", 80, [P, TT, D])
        xT_hi = at_kb("xT_hi", 88, [P, KD, SEQ], F32R)
        xT_lo = at_kb("xT_lo", 96, [P, KD, SEQ], F32R)
        gain = at_kb("gain", 104, [P, 2, D])
        tmp = at_kb("tmp", 112, [P, TT, D])
        const = at_kb("const", 120, [P, C_ALL])
        bias_hi = at_kb("bias_hi", 128, [P, D], F32R)
        bias_lo = at_kb("bias_lo", 132, [P, D], F32R)
        ones = at_kb("ones", 136, [P, P])
        ones_r = at_kb("ones_r", 136.5, [P, P], F32R)
        rows = at_kb("rows", 137, [P, P])
        cols = at_kb("cols", 137.5, [P, P])
        st = at_kb("st", 138, [P, 192])
        SCOPE = 139
        sil = at_kb("sil", SCOPE, [P, 2, SEQ])
        h = at_kb("h", SCOPE + 2, [P, 2, SEQ])
        h_hi = at_kb("h_hi", SCOPE + 4, [P, 2, SEQ], F32R)
        h_lo = at_kb("h_lo", SCOPE + 6, [P, 2, SEQ], F32R)
        p_in = at_kb("p_in", SCOPE + 8, [P, TT, PLE])
        pT_hi = at_kb("pT_hi", SCOPE + 10, [P, KP, SEQ], F32R)
        pT_lo = at_kb("pT_lo", SCOPE + 12, [P, KP, SEQ], F32R)
        pn = at_kb("pn", SCOPE + 14, [P, TT, D])
        bias = at_kb("bias", SCOPE + 22, [P, D])
        qkT = at_kb("qkT", SCOPE, [P, 10, SEQ])
        val = at_kb("val", SCOPE + 10, [P, TT, 256])
        prob = at_kb("prob", SCOPE + 12, [P, 2, 2048])
        probT = at_kb("probT", SCOPE + 28, [P, 2, 2048])
        sink = at_kb("sink", SCOPE + 44, [P, 16])
        soft = at_kb("soft", SCOPE + 44.5, [P, 6, 32])
        GH = 4
        convT = at_kb("convT", SCOPE, [P, 3 * GH, SEQ])
        knT = at_kb("knT", SCOPE, [P, GH, SEQ])
        qnT = at_kb("qnT", SCOPE + 4, [P, GH, SEQ])
        qdT = at_kb("qdT", SCOPE + 8, [P, GH, SEQ])
        wT = at_kb("wT", SCOPE, [P, TT * GH, P])
        k_tok = at_kb("k_tok", SCOPE + 12, [P, TT, BANK])
        o_tok = at_kb("o_tok", SCOPE + 12, [P, TT, BANK])
        q_tok = at_kb("q_tok", SCOPE + 16, [P, TT, BANK])
        u_tok = at_kb("u_tok", SCOPE + 16, [P, TT, BANK])
        k_dec = at_kb("k_dec", SCOPE + 20, [P, TT, BANK])
        rhs = at_kb("rhs", SCOPE + 24, [P, TT * GH, 2 * P])
        attnT = at_kb("attnT", SCOPE + 32, [P, TT * GH, P])
        lmat = at_kb("lmat", SCOPE + 36, [P, TT * GH, P])
        inv_u = at_kb("inv_u", SCOPE + 40, [P, TT * GH, P])
        inv_t = at_kb("inv_t", SCOPE + 44, [P, TT * GH, P])
        cross = at_kb("cross", SCOPE + 48, [P, TT * GH, P])
        v_new = at_kb("v_new", SCOPE + 48, [P, TT, BANK])
        z_gate = at_kb("z_gate", SCOPE + 52, [P, TT, BANK])
        states = [at_kb("state0", SCOPE + 40, [P, GH, P]), at_kb("state1", SCOPE + 56, [P, GH, P])]
        gs = at_kb("gs", SCOPE + 58, [P, 256])
        o_gain = at_kb("o_gain", SCOPE + 59, [P, P])
        Q_LORA, KV_LORA, ROPE = 384, 256, 64
        KL = (Q_LORA + KV_LORA) // P
        lat = at_kb("lat", 80, [P, TT, Q_LORA + KV_LORA])
        rope_in = at_kb("rope_in", 85, [P, TT, 5, ROPE])
        m_prob = at_kb("m_prob", 80, [P, 12 * P])
        latT_hi = at_kb("latT_hi", 112, [P, KL, SEQ], F32R)
        rope_out = at_kb("rope_out", SCOPE + 12, [P, TT, 8, ROPE])
        m_probT = at_kb("m_probT", 112, [P, 12 * P])
        latT_lo = at_kb("latT_lo", SCOPE + 60, [P, KL, SEQ], F32R)
        rope_tmp = at_kb("rope_tmp", SCOPE + 65, [P, TT, 5, ROPE // 2])
        m_soft = at_kb("m_soft", SCOPE + 66.5, [P, 4, 8])
        q_nopeT = at_kb("q_nopeT", 88, [P, GH, SEQ])
        k_nopeT = at_kb("k_nopeT", 92, [P, GH, SEQ])
        m_val = at_kb("m_val", 96, [P, TT, BANK])
        ropeT = at_kb("ropeT", 100, [P, 4, SEQ])
        y = ctx.enter_context(nc.psum_tensor("y", [P, TT, D], F32))
        q = ctx.enter_context(nc.psum_tensor("q", [P, 4, BANK], F32))
        y_flat = y[:, :, :].rearrange("p t d -> p (t d)")
        q_flat = q[:, :, :].rearrange("p b c -> p (b c)")
        ident = const[:, 0:P]

        slabs = Slabs()

        def view(n, k=None):
            parts, width = slabs.size[n]
            v = raw[0:parts, n % RING, 0:width]
            return v if k is None else v.rearrange("p (k c) -> p k c", k=k)

        def add_rows(w, k, parts=P, c0=0, c1=None):
            c1 = w.shape[1] if c1 is None else c1
            return slabs.add(parts, c1 - c0, [lambda n: (view(n), w[k * P:k * P + parts, c0:c1])])

        def add_cols(w, at):
            wk = w.rearrange("(k p) c -> p k c", p=P)
            pieces, done = [], 0
            for c, m in at:
                pieces.append(lambda n, c=c, m=m, done=done:
                              (view(n, KD)[:, :, done:done + m], wk[:, :, c:c + m]))
                done += m
            return slabs.add(P, KD * P, pieces)

        SWA_H, SWA_KV, HD = 16, 4, 64
        KV0 = SWA_H * HD
        V0 = KV0 + SWA_KV * HD

        def odd_tiles():
            return [[(KV0 + a * P, P)] for a in range(2)] + \
                   [[((8 * a + i) * HD, HD), ((8 * a + 4 + i) * HD, HD)] for a in range(2) for i in range(4)]

        def plan_odd():
            w = io["swa_w_qkv"][0]
            wk = w.rearrange("(k p) c -> p k c", p=P)
            for cols_ in odd_tiles()[:2]:
                add_cols(w, cols_)
            for j in range(2):
                slabs.add(P, SLAB, [lambda n, j=j: (view(n, 4), wk[:, 4 * j:4 * j + 4, V0:V0 + 256])])
            for cols_ in odd_tiles()[2:]:
                add_cols(w, cols_)
            for k in range(KD):
                add_rows(io["swa_w_o"][0], k)

        Z0, A0, KV_IN = 1536, 2048, 2048 + 8 + Q_LORA
        W_A, W_KV = 8 + Q_LORA, KV_LORA + ROPE

        def plan_even():
            w = io["ab_w_in"][0]
            wk = w.rearrange("(k p) c -> p k c", p=P)

            def pairs(c0, width):
                for j in range(KD // 2):
                    slabs.add(P, 2 * width, [lambda n, j=j: (view(n, 2), wk[:, 2 * j:2 * j + 2, c0:c0 + width])])

            pairs(A0, W_A)
            pairs(KV_IN, W_KV)
            for c in (512, 0, 1024):
                for hd in range(GH):
                    add_cols(w, [(c + hd * P, P)])
            pairs(Z0, BANK)
            for k in range(Q_LORA // P):
                add_rows(io["mla_w_uq"][0], k)
            for k in range(KV_LORA // P):
                add_rows(io["mla_w_ukv"][0], k)
            for k in range(KD):
                add_rows(io["ab_w_out"][0], k)

        N_A, N_KV, N_TILE, N_Z, N_UQ, N_UKV, N_OUT = 0, 4, 8, 20, 24, 27, 29

        def ffn_slab(wgu, wd, kind, f):
            if kind == "d":
                return add_rows(wd, f, P if f < FULL else HALF)
            if f == FULL:
                return add_cols(wgu, [(f * P, HALF), (D_FF + f * P, HALF)])
            return add_cols(wgu, [((kind == "u") * D_FF + f * P, P)])

        ffns, toks = {}, {}
        y_of, squares_of, gain_of, norm_of = {}, {}, {}, {}
        y_last = {}
        n_row_loads = 3 + 6
        n_bias_loads = 4
        for name in phases:
            kind, layer = name[:-1], int(name[-1])
            if kind in ("ffn1_", "ffn2_"):
                wgu, wd = io[kind + "wgu"][layer], io[kind + "wd"][layer]
                seq = [("g", 0)] + [("p", k) for k in range(KP) if kind == "ffn2_"] + [("u", 0)]
                for f in range(1, FULL):
                    seq += [("g", f), ("u", f), ("d", f - 1)]
                seq += [("g", FULL), ("d", FULL - 1), ("d", FULL)]
                ffns[name] = (len(slabs.load), len(ffns), wgu, wd)
                for kd, f in seq:
                    if kd == "p":
                        add_rows(io["ple_proj"][layer], f)
                    else:
                        ffn_slab(wgu, wd, kd, f)
                if kind == "ffn2_":
                    y_of["p" + name] = len(y_of)
                    y_last["p" + name] = ffns[name][0] + KP
                    gain_of["p" + name] = (len(gain_of), "ple_norm", layer)
                    squares_of["p" + name] = len(squares_of)
            elif kind == "mix":
                toks[name] = len(slabs.load)
                plan_odd() if layer else plan_even()
            elif kind == "gate":
                toks[name] = len(slabs.load)
                for k in range(KD):
                    add_rows(io["ple_gate_w"][layer], k)
            y_last[name] = len(slabs.load) - 1
            y_of[name] = len(y_of)
            norm_of[name] = len(norm_of)
            if kind != "gate":
                squares_of[name] = len(squares_of)
                gain_of[name] = (len(gain_of), {"ffn1_": "ffn1_post", "ffn2_": "ffn2_post",
                                                "mix": "mix_post"}[kind], layer)
        N = len(slabs.load)

        mains = phases
        norm_col = {"ffn1_": COL_FFN1, "ffn2_": COL_FFN2, "mix": COL_MIX}

        def gain_col(name, k):
            kind, layer = name[:-1], int(name[-1])
            c = COL_ONE + k if kind == "gate" else norm_col[kind] + 8 * layer + k
            return cols[:, c:c + 1]

        loaded = [sem(f"loaded{i}") for i in range(RING)]
        hi_ready, lo_ready, slab_used = sem("hi_ready"), sem("lo_ready"), sem("slab_used")
        x_loaded, p_loaded, const_loaded, rows_loaded, bias_loaded = (
            sem(n) for n in ("x_loaded", "p_loaded", "const_loaded", "rows_loaded", "bias_loaded"))
        rows_clear, bias_clear, ones_set, ones_r_set = (
            sem(n) for n in ("rows_clear", "bias_clear", "ones_set", "ones_r_set"))
        cols_turned, cols_ready = sem("cols_turned"), sem("cols_ready")
        bias_hi_ready, bias_ready = sem("bias_hi_ready"), sem("bias_ready")
        gain_loaded = [sem("gain_loaded0"), sem("gain_loaded1")]
        y_first, y_sq, p_scaled = sem("y_first"), sem("y_sq"), sem("p_scaled")
        x_ready, x_sq, x_rms, xn_ready = sem("x_ready"), sem("x_sq"), sem("x_rms"), sem("xn_ready")
        xn_turned, xT_hi_ready, xT_ready = sem("xn_turned"), sem("xT_hi_ready"), sem("xT_ready")
        p_turned, pT_hi_ready, pT_ready = sem("p_turned"), sem("pT_hi_ready"), sem("pT_ready")
        sil_ready, h_ready, h_hi_ready, h_lo_ready = (
            sem(n) for n in ("sil_ready", "h_ready", "h_hi_ready", "h_lo_ready"))
        gate_ready = sem("gate_ready")
        sinks_loaded, qk_kept, val_kept, scores_ready, max_ready, exp_done, prob_ready, zero_set = (
            sem(n) for n in ("sinks_loaded", "qk_kept", "val_kept", "scores_ready", "max_ready", "exp_done",
                             "prob_ready", "zero_set"))
        prob_turned, probT_act, probT_dve, mixed, mixT_hi_ready, mixT_ready = (
            sem(n) for n in ("prob_turned", "probT_act", "probT_dve", "mixed", "mixT_hi_ready", "mixT_ready"))
        dve_step = sem("dve_step")
        gate_rows, gates_in, lat_sq, lat_rms, lat_ready, rope_key = (
            sem(n) for n in ("gate_rows", "gates_in", "lat_sq", "lat_rms", "lat_ready", "rope_key"))
        gates_raw, gates_exp, gates_set, beta_set, conv_first, conv_done, conv_ready = (
            sem(n) for n in ("gates_raw", "gates_exp", "gates_set", "beta_set", "conv_first", "conv_done",
                             "conv_ready"))
        lat_turned, latT_hi_ready, latT_ready = sem("lat_turned"), sem("latT_hi_ready"), sem("latT_ready")
        sums_ready, sums_kept, dec_args, dec_ready, wide_sums, decay_args, grown, decay_ready = (
            sem(n) for n in ("sums_ready", "sums_kept", "dec_args", "dec_ready", "wide_sums", "decay_args",
                             "grown", "decay_ready"))
        z_in, z_ready, qn_made, q_nope_kept, rope_kept, kn_made, k_nope_kept, m_val_kept = (
            sem(n) for n in ("z_in", "z_ready", "qn_made", "q_nope_kept", "rope_kept", "kn_made", "k_nope_kept",
                             "m_val_kept"))
        rope_ready, rope_turned, ropeT_kept, m_scores, m_max, m_exp, m_prob_ready, m_turned, m_probT_act, \
            m_probT_dve, m_mixed = (sem(n) for n in (
                "rope_ready", "rope_turned", "ropeT_kept", "m_scores", "m_max", "m_exp", "m_prob_ready",
                "m_turned", "m_probT_act", "m_probT_dve", "m_mixed"))
        tok_turned, tok_sq, tok_ready, back_turned, back_kept, qd_ready = (
            sem(n) for n in ("tok_turned", "tok_sq", "tok_ready", "back_turned", "back_kept", "qd_ready"))
        rhs_ready, grams, l_ready, cross_made, cross_ready, inv_made, inv_ready = (
            sem(n) for n in ("rhs_ready", "grams", "l_ready", "cross_made", "cross_ready", "inv_made", "inv_ready"))
        solved, solved_kept, read_out, v_new_ready, kv_made, state_ready, o_made, o_sq, o_ready, o_turned = (
            sem(n) for n in ("solved", "solved_kept", "read_out", "v_new_ready", "kv_made", "state_ready",
                             "o_made", "o_sq", "o_ready", "o_turned"))
        emix_hi, emix_ready = sem("emix_hi"), sem("emix_ready")
        stored = sem("stored")

        def conv_col(j):
            return (GH, 0, 2 * GH)[j // GH] + j % GH

        def lat_bank(k):
            t, c = ((0, BANK), (0, BANK + SEQ), (1, BANK), (1, BANK + SEQ), (0, 0))[k]
            return y[:, t, c:c + SEQ]

        M_SCALE = 192 ** -0.5

        def m_scores_of(t):
            w = (t + 1) * P
            return y[:, t, 0:GH * w].rearrange("p (h k) -> p h k", h=GH)

        def m_prob_of(t):
            w = (t + 1) * P
            return m_prob[:, t * GH * P:t * GH * P + GH * w].rearrange("p (h k) -> p h k", h=GH)

        def k_dec_free(t):
            return inv_t[:, 4 * t:4 * t + 4, :].rearrange("p h c -> p (h c)")

        BATCHES = [(0, 0, 16, y_flat, 0, 128), (1, 0, 8, q_flat, 64, 256), (1, 8, 8, y_flat, 64, 256)]

        def scores_of(b):
            t, h0, heads, place, key0, wide = BATCHES[b]
            return place[:, 0:heads * wide].rearrange("p (h k) -> p h k", h=heads)[:, :, key0:wide]

        def prob_of(b):
            t, h0, heads, place, key0, wide = BATCHES[b]
            return prob[:, b % 2, 0:heads * wide].rearrange("p (h k) -> p h k", h=heads)[:, :, key0:wide]

        def soft_of(b, row):
            t, h0, heads, place, key0, wide = BATCHES[b]
            s0 = 16 * t + h0
            return soft[:, row, s0:s0 + heads]

        MIXED = [(0, 0, slice(0, 4), 0), (0, 1, slice(4, 8), 0), (1, 2, slice(0, 4), 1), (2, 3, slice(4, 8), 1)]

        def at(i, base, step):
            return base if i is None else i * step + base

        LOOP0, LOOP1 = 3, 19
        TURNS = (LOOP1 - LOOP0) // 2

        def slab_of(name, f):
            return ffns[name][0] + (0 if f == 0 else 2 + extra(name) + 3 * (f - 1))

        def extra(name):
            return KP if name.startswith("ffn2_") else 0

        block = ctx.enter_context(nc.Block())

        @block.sync
        def _(sp):
            sp.dma_start(x[:, :, :], io["x"][0].rearrange("(t p) d -> p t d", p=P)).then_inc(x_loaded, 16)
            sp.dma_start(const[:, :], io["const"]).then_inc(const_loaded, 16)

            def load(n):
                if n >= RING:
                    sp.wait_ge(lo_ready, n - RING + 1)
                for piece in slabs.load[n]:
                    dst, src = piece(n)
                    sp.dma_start(dst, src).then_inc(loaded[n % RING], 16)

            def load_ffn(name, base, wgu, wd):
                for n in range(base, slab_of(name, LOOP0)):
                    load(n)
                wk = wgu.rearrange("(k p) c -> p k c", p=P)
                with sp.Fori(0, TURNS) as i:
                    for j in range(2):
                        n = slab_of(name, LOOP0 + j)
                        f = LOOP0 + j
                        for m, (c0, stride) in enumerate([(f * P, 2 * P), (D_FF + f * P, 2 * P)]):
                            src = wk[:, :, bass.ds(i * stride + c0, P)]
                            sp.wait_ge(lo_ready, i * 6 + (n + m - RING + 1))
                            sp.dma_start(view(n + m, KD), src).then_inc(loaded[(n + m) % RING], 16)
                        src = wd[bass.ds(i * (2 * P) + (f - 1) * P, P), :]
                        sp.wait_ge(lo_ready, i * 6 + (n + 2 - RING + 1))
                        sp.dma_start(view(n + 2), src).then_inc(loaded[(n + 2) % RING], 16)
                for n in range(slab_of(name, LOOP1), base + 65 + extra(name)):
                    load(n)

            n = 0
            while n < N:
                hit = [(name, v) for name, v in ffns.items() if v[0] == n]
                if hit:
                    name, (base, _, wgu, wd) = hit[0]
                    load_ffn(name, base, wgu, wd)
                    n += 65 + extra(name)
                else:
                    load(n)
                    n += 1
            for t in range(TT):
                sp.wait_ge(x_ready, TT * (len(mains) - 1) + t + 1)
                sp.dma_start(out[0, t * P:(t + 1) * P, :], x[:, t, :]).then_inc(stored, 16)
            sp.wait_ge(stored, 16 * TT)

        @block.gpsimd
        def _(pool):
            uses = list(gain_of)
            for u, name, layer in gain_of.values():
                if u >= 2:
                    before = uses[u - 2]
                    if before.startswith("p"):
                        pool.wait_ge(p_scaled, TT * (int(before[-1]) + 1))
                    else:
                        pool.wait_ge(x_ready, TT * (norm_of[before] + 1))
                pool.dma_start(gain[:, u % 2, :], io[name][layer:layer + 1, :].to_broadcast([P, D])) \
                    .then_inc(gain_loaded[u % 2], 16)
                if name == "mix_post" and not layer:
                    pool.wait_ge(x_ready, TT * norm_of["mix0"])
                    for c, src in ((128, "gdn_dt_bias"), (132, "gdn_a_log")):
                        pool.dma_start(gs[:, c:c + 4], io[src].to_broadcast([P, 4])).then_inc(gate_rows, 16)
                    pool.dma_start(o_gain[:, :], io["gdn_out_norm"].to_broadcast([P, P])).then_inc(gate_rows, 16)
                    pool.wait_ge(gate_rows, 48)
                    pool.wait_ge(z_in, 1)
                    v = z_gate[:, :, :].rearrange("p t (h c) -> p (t h) c", c=P)
                    pool.tensor_tensor(v, v, o_gain[:, :].unsqueeze(1).to_broadcast([P, TT * GH, P]), ALU.mult) \
                        .then_inc(z_ready, 1)
                if name == "mix_post" and layer:
                    pool.wait_ge(x_ready, TT * norm_of["mix1"])
                    pool.dma_start(sink[:, :], io["swa_sinks"].to_broadcast([P, SWA_H])).then_inc(sinks_loaded, 16)
                    for b in (1, 2):
                        if b == 2:
                            pool.wait_ge(prob_turned, 2)
                        v = prob[:, b % 2, :].rearrange("p (h k) -> p h k", h=8)[:, :, 0:CHUNK]
                        pool.memset(v, 0.0).then_inc(zero_set, 1)
                if name == "ple_norm":
                    if layer:
                        pool.wait_ge(p_turned, 1)
                    pool.wait_ge(x_ready, TT * norm_of[f"ffn2_{layer}"])
                    pool.dma_start(p_in[:, :, :], io["p"][layer, 0].rearrange("(t p) c -> p t c", p=P)) \
                        .then_inc(p_loaded, 16)

        @block.scalar
        def _(act):
            act.wait_ge(rows_clear, 1)
            for c, name in ((COL_FFN1, "ffn1_pre"), (COL_MIX, "mix_pre"), (COL_FFN2, "ffn2_pre")):
                act.dma_start(rows[c:c + 2 * KD, :], io[name].rearrange("l (k p) -> (l k) p", p=P)) \
                    .then_inc(rows_loaded, 16)
            for row, name in ((COL_QN, "mla_q_norm"), (COL_KVN, "mla_kv_norm")):
                v = io[name][0].rearrange("(k p) -> k p", p=P)
                act.dma_start(rows[row:row + v.shape[0], :], v).then_inc(rows_loaded, 16)
            act.dma_start(rows[COL_CONV:COL_CONV + 48, :], io["gdn_conv"][0].rearrange("j (c p) -> (j c) p", p=P)) \
                .then_inc(rows_loaded, 16)
            b_qkv = io["swa_b_qkv"]
            q_bias = b_qkv[0, 0:KV0].rearrange("(a b r) -> b a r", a=2, b=2)
            for b in range(2):
                act.dma_start(rows[COL_BQK + 2:COL_BQK + 10, b * HD:(b + 1) * HD],
                              q_bias[b].rearrange("a (i d) -> a i d", d=HD)).then_inc(rows_loaded, 16)
            act.dma_start(rows[COL_BQK:COL_BQK + 2, :], b_qkv[0, KV0:V0].rearrange("(k p) -> k p", p=P)) \
                .then_inc(rows_loaded, 16)
            act.wait_ge(bias_clear, 1)
            for l in range(2):
                act.dma_start(bias[32 * l:32 * l + 1, :], io["ple_gate_b"][l:l + 1, :]).then_inc(bias_loaded, 16)
            act.dma_start(bias[64:65, :], io["swa_b_o"]).then_inc(bias_loaded, 16)
            act.dma_start(bias[96:97, 0:256], b_qkv[0:1, V0:]).then_inc(bias_loaded, 16)

            def split_hi(m, i=None):
                parts, width = slabs.size[m]
                act.wait_ge(loaded[m % RING], at(i, slabs.loaded[m], 16))
                if m >= RING:
                    act.wait_ge(slab_used, at(i, m - RING + 1, 6))
                nc.scalar.activation(hi[0:parts, m % RING, 0:width], raw[0:parts, m % RING, 0:width],
                                     ACT.Copy).then_inc(hi_ready, 1)

            def ahead(n, i=None):
                if n + AHEAD < N:
                    split_hi(n + AHEAD, i)

            def wait_y(name, t):
                if t == 0:
                    act.wait_ge(y_first, y_of[name] + 1)
                else:
                    act.wait_ge(slab_used, y_last[name] + 1)

            def squares_y(name):
                for t in range(TT):
                    wait_y(name, t)
                    nc.scalar.activation(xn[:, t, :], y[:, t, :], ACT.Square,
                                         accum_out=st[:, t:t + 1]).then_inc(y_sq, 1)

            def norm(name):
                b = norm_of[name]
                for t in range(TT):
                    if b == 0:
                        act.wait_ge(x_loaded, 16)
                    else:
                        act.wait_ge(x_ready, TT * (b - 1) + t + 1)
                    nc.scalar.activation(xn[:, t, :], x[:, t, :], ACT.Square,
                                         accum_out=st[:, 2 + t:3 + t]).then_inc(x_sq, 1)
                for t in range(TT):
                    act.wait_ge(x_rms, TT * b + t + 1)
                    nc.scalar.activation(xn[:, t, :], x[:, t, :], ACT.Copy,
                                         scale=st[:, 6 + t:7 + t]).then_inc(xn_ready, 1)

            def turned(name):
                b = norm_of[name]
                if b == 0:
                    act.wait_ge(cols_ready, 1)
                for k in range(KD):
                    act.wait_ge(xn_turned, (KD * b + k) // 2 + 1)
                    nc.scalar.activation(xT_hi[:, k, :], q[:, k // 2, (k % 2) * SEQ:(k % 2 + 1) * SEQ], ACT.Copy,
                                         scale=gain_col(name, k)).then_inc(xT_hi_ready, 1)

            def unit(name, number, f, i=None):
                n, F = slab_of(name, f), TILES * number + f
                m = P if f < FULL else HALF
                ahead(n, i)
                if f == 0 and extra(name):
                    embeddings(name)
                    n += KP
                if f < FULL:
                    ahead(n + 1, i)
                act.wait_ge(slab_used, at(i, n + (2 if f < FULL else 1), 6))
                if F >= 2:
                    act.wait_ge(h_ready, at(i, F - 1, 2))
                nc.scalar.activation(sil[0:m, f % 2, :], q[0:m, f % 2, 0:SEQ], ACT.Silu).then_inc(sil_ready, 1)
                if f == FULL:
                    ahead(n + 1, i)
                elif f > 0:
                    ahead(n + 2, i)
                act.wait_ge(h_ready, at(i, F + 1, 2))
                if f >= 2:
                    act.wait_ge(slab_used, at(i, slab_of(name, f - 1) + 3, 6))
                nc.scalar.activation(h_hi[0:m, f % 2, :], h[0:m, f % 2, :], ACT.Copy).then_inc(h_hi_ready, 1)
                if f == FULL:
                    ahead(n + 2, i)

            def ffn(name):
                number = ffns[name][1]
                for f in range(LOOP0):
                    unit(name, number, f)
                with act.Fori(0, TURNS) as i:
                    unit(name, number, LOOP0, i)
                    unit(name, number, LOOP0 + 1, i)
                for f in range(LOOP1, TILES):
                    unit(name, number, f)
                squares_y(name)

            def embeddings(name):
                act.wait_ge(p_turned, int(name[-1]) + 1)
                nc.scalar.activation(pT_hi[:, :, :], y[:, 0, 0:BANK], ACT.Copy).then_inc(pT_hi_ready, 1)
                for k in range(KP):
                    ahead(ffns[name][0] + 1 + k)
                squares_y("p" + name)

            def gate(name):
                for k in range(KD):
                    ahead(toks[name] + k)
                for t in range(TT):
                    wait_y(name, t)
                    nc.scalar.activation(xn[:, t, :], y[:, t, :], ACT.Tanh, scale=0.5).then_inc(gate_ready, 1)

            def mixed_hi(piece):
                b, bank, blocks, t = MIXED[piece]
                act.wait_ge(mixed, b + 1)
                nc.scalar.activation(xT_hi[:, blocks, t * P:(t + 1) * P],
                                     q[:, bank, :].rearrange("p (m c) -> p m c", m=4), ACT.Copy) \
                    .then_inc(mixT_hi_ready, 1)

            def odd(name):
                n0 = toks[name]

                def keep(j, n):
                    act.wait_ge(slab_used, n + 1)
                    nc.scalar.activation(qkT[:, j, :], q[:, j % 4, 0:SEQ], ACT.Identity,
                                         bias=cols[:, COL_BQK + j:COL_BQK + j + 1]).then_inc(qk_kept, 1)

                for j in range(2):
                    ahead(n0 + j)
                    keep(j, n0 + j)
                ahead(n0 + 2)
                ahead(n0 + 3)
                act.wait_ge(slab_used, n0 + 4)
                nc.scalar.activation(val[:, :, :], y[:, :, 0:256], ACT.Copy).then_inc(val_kept, 1)
                for j in range(2, 10):
                    ahead(n0 + 2 + j)
                    keep(j, n0 + 2 + j)

                def exps(b):
                    act.wait_ge(max_ready, b + 1)
                    for j in range(BATCHES[b][2]):
                        nc.scalar.activation(prob_of(b)[:, j, :], scores_of(b)[:, j, :], ACT.Exp,
                                             bias=soft_of(b, 2)[:, j:j + 1], scale=HD ** -0.5,
                                             accum_out=soft_of(b, 3)[:, j:j + 1])
                    nc.scalar.activation(soft_of(b, 4), soft_of(b, 1), ACT.Exp).then_inc(exp_done, 1)

                def keep_turned(b):
                    act.wait_ge(prob_turned, 2 * b + 1)
                    nc.scalar.activation(probT[:, b % 2, 0:1024], BATCHES[b][3][:, 0:1024], ACT.Copy) \
                        .then_inc(probT_act, 1)

                exps(0)
                exps(1)
                keep_turned(0)
                keep_turned(1)
                exps(2)
                for piece in range(3):
                    mixed_hi(piece)
                keep_turned(2)
                mixed_hi(3)
                for k in range(KD):
                    ahead(n0 + 12 + k)
                squares_y(name)

            def even(name):
                n0 = toks[name]

                def used(n):
                    act.wait_ge(slab_used, n0 + n)

                for n in range(N_TILE):
                    ahead(n0 + n)
                used(N_TILE)
                for t in range(TT):
                    nc.scalar.activation(lat[:, t, 0:Q_LORA], y[:, t, 8:W_A], ACT.Square,
                                         accum_out=st[:, 64 + t:65 + t])
                    ins = nc.scalar.activation(lat[:, t, Q_LORA:], y[:, t, BANK:BANK + KV_LORA], ACT.Square,
                                               accum_out=st[:, 66 + t:67 + t])
                ins.then_inc(lat_sq, 1)
                act.wait_ge(gate_rows, 48)
                nc.scalar.activation(gs[:, 0:16].rearrange("p (t c) -> p t c", t=TT), y[:, :, 0:8], ACT.Copy) \
                    .then_inc(gates_in, 1)
                nc.scalar.activation(rope_in[:, :, 4, :], y[:, :, BANK + KV_LORA:BANK + W_KV], ACT.Copy) \
                    .then_inc(rope_key, 1)
                act.wait_ge(gates_raw, 1)
                nc.scalar.activation(gs[:, 32:40], gs[:, 24:32], ACT.Exp, scale=-1.0).then_inc(gates_exp, 1)
                nc.scalar.activation(gs[:, 136:140], gs[:, 132:136], ACT.Exp)
                act.wait_ge(gates_in, 1)
                nc.scalar.activation(gs[:, 48:56].rearrange("p (t c) -> p t c", t=TT),
                                     gs[:, 0:16].rearrange("p (t c) -> p t c", t=TT)[:, :, 4:8], ACT.Exp, scale=-1.0)
                act.wait_ge(gates_exp, 1)
                nc.scalar.activation(gs[:, 40:48], gs[:, 32:40], ACT.Ln, bias=1.0).then_inc(gates_exp, 1)
                act.wait_ge(lat_rms, 1)
                for t in range(TT):
                    nc.scalar.activation(lat[:, t, 0:Q_LORA], y[:, t, 8:W_A], ACT.Copy, scale=st[:, 68 + t:69 + t])
                    ins = nc.scalar.activation(lat[:, t, Q_LORA:], y[:, t, BANK:BANK + KV_LORA], ACT.Copy,
                                               scale=st[:, 70 + t:71 + t])
                ins.then_inc(lat_ready, 1)
                for j in range(3 * GH):
                    ahead(n0 + N_TILE + j)
                    used(N_TILE + j + 1)
                    c = COL_CONV + 36 + conv_col(j)
                    nc.scalar.activation(convT[:, j, :], q[:, j % 4, 0:SEQ], ACT.Copy, scale=cols[:, c:c + 1]) \
                        .then_inc(conv_first, 1)
                    if j:
                        act.wait_ge(conv_done, j)
                        nc.scalar.activation(convT[:, j - 1, :], convT[:, j - 1, :], ACT.Silu).then_inc(conv_ready, 1)
                act.wait_ge(conv_done, 3 * GH)
                nc.scalar.activation(convT[:, 3 * GH - 1, :], convT[:, 3 * GH - 1, :], ACT.Silu) \
                    .then_inc(conv_ready, 1)
                for k in range(KL):
                    act.wait_ge(lat_turned, k // 2 + 1)
                    nc.scalar.activation(latT_hi[:, k, :], lat_bank(k), ACT.Copy,
                                         scale=cols[:, COL_QN + k:COL_QN + k + 1]).then_inc(latT_hi_ready, 1)
                act.wait_ge(sums_ready, 1)
                nc.scalar.activation(gs[:, 64:96], y[:, 1, 0:32], ACT.Copy).then_inc(sums_kept, 1)
                for n in range(4):
                    ahead(n0 + N_Z + n)
                used(N_UQ)
                nc.scalar.activation(z_gate[:, :, :], y[:, :, 0:BANK], ACT.Silu).then_inc(z_in, 1)
                act.wait_ge(dec_args, 1)
                nc.scalar.activation(gs[:, 96:128], gs[:, 160:192], ACT.Exp).then_inc(dec_ready, 1)
                act.wait_ge(wide_sums, 1)
                nc.scalar.activation(cross[:, :, :].rearrange("p m c -> p (m c)"), q_flat[:, 0:1024], ACT.Exp) \
                    .then_inc(grown, 1)
                act.wait_ge(decay_args, 1)
                for m in range(TT * GH):
                    nc.scalar.activation(attnT[:, m, :], attnT[:, m, :], ACT.Exp, bias=gs[:, 192 + m:193 + m])
                    nc.scalar.activation(lmat[:, m, :], lmat[:, m, :], ACT.Exp, bias=gs[:, 64 + m:65 + m],
                                         scale=-1.0).then_inc(decay_ready, 1)
                for n in range(3):
                    ahead(n0 + N_UQ + n)
                act.wait_ge(qn_made, 1)
                for hd in range(GH):
                    nc.scalar.activation(q_nopeT[:, hd, :], q[:, hd, 0:SEQ], ACT.Copy).then_inc(q_nope_kept, 1)
                used(N_UKV)
                nc.scalar.activation(rope_in[:, :, 0:4, :].rearrange("p t h c -> p t (h c)"),
                                     y[:, :, BANK:BANK + 256], ACT.Copy).then_inc(rope_kept, 1)
                for n in range(2):
                    ahead(n0 + N_UKV + n)
                act.wait_ge(kn_made, 1)
                for hd in range(GH):
                    nc.scalar.activation(k_nopeT[:, hd, :], q[:, hd, 0:SEQ], ACT.Copy).then_inc(k_nope_kept, 1)
                used(N_OUT)
                nc.scalar.activation(m_val[:, :, :], y[:, :, BANK:2 * BANK], ACT.Copy).then_inc(m_val_kept, 1)
                act.wait_ge(rope_turned, 1)
                nc.scalar.activation(ropeT[:, 0:2, :].rearrange("p r c -> p (r c)"), y[:, 0, BANK:2 * BANK], ACT.Copy)
                nc.scalar.activation(ropeT[:, 2:4, :].rearrange("p r c -> p (r c)"), y[:, 1, BANK:2 * BANK], ACT.Copy) \
                    .then_inc(ropeT_kept, 1)
                for t in range(TT):
                    act.wait_ge(m_max, t + 1)
                    for hd in range(GH):
                        ins = nc.scalar.activation(m_prob_of(t)[:, hd, :], m_scores_of(t)[:, hd, :], ACT.Exp,
                                                   bias=m_soft[:, 1, 4 * t + hd:4 * t + hd + 1], scale=M_SCALE,
                                                   accum_out=m_soft[:, 2, 4 * t + hd:4 * t + hd + 1])
                    ins.then_inc(m_exp, 1)
                act.wait_ge(m_turned, 1)
                nc.scalar.activation(m_probT[:, 0:BANK], y[:, 0, 0:BANK], ACT.Copy).then_inc(m_probT_act, 1)
                act.wait_ge(m_turned, 2)
                nc.scalar.activation(m_probT[:, BANK:2 * BANK], y[:, 1, 0:BANK], ACT.Copy).then_inc(m_probT_act, 1)
                act.wait_ge(m_mixed, 1)
                for j in range(2):
                    nc.scalar.activation(xT_hi[:, 4 + 2 * j:6 + 2 * j, :].rearrange("p m c -> p (m c)"),
                                         y[:, 0, j * BANK:(j + 1) * BANK], ACT.Copy).then_inc(emix_hi, 1)
                for s_, place in ((0, inv_t), (1, inv_u)):
                    for t in range(TT):
                        act.wait_ge(tok_turned, 2 * s_ + t + 1)
                        nc.scalar.activation(place[:, 4 * t:4 * t + 4, :].rearrange("p h c -> p (h c)"),
                                             q[:, 2 * (1 - s_) + t, :], ACT.Square).then_inc(tok_sq, 1)
                for s_, place in ((0, knT), (1, qnT)):
                    act.wait_ge(back_turned, s_ + 1)
                    nc.scalar.activation(place[:, :, :].rearrange("p h c -> p (h c)"),
                                         q_flat[:, s_ * 1024:(s_ + 1) * 1024], ACT.Copy).then_inc(back_kept, 1)
                act.wait_ge(solved, 1)
                nc.scalar.activation(u_tok[:, :, :].rearrange("p t c -> p (t c)"), q_flat[:, 0:1024], ACT.Copy) \
                    .then_inc(solved_kept, 1)
                act.wait_ge(solved, 2)
                nc.scalar.activation(wT[:, :, :].rearrange("p m c -> p (m c)"), q_flat[:, 1024:2048], ACT.Copy) \
                    .then_inc(solved_kept, 1)
                for t in range(TT):
                    act.wait_ge(o_made, t + 1)
                    nc.scalar.activation(k_dec_free(t), q[:, 1 + 2 * t, :], ACT.Square).then_inc(o_sq, 1)
                act.wait_ge(o_turned, 1)
                for j in range(2):
                    nc.scalar.activation(xT_hi[:, 2 * j:2 * j + 2, :].rearrange("p m c -> p (m c)"), q[:, j, :],
                                         ACT.Copy).then_inc(emix_hi, 1)
                for k in range(KD):
                    ahead(n0 + N_OUT + k)
                squares_y(name)

            norm(mains[0])
            act.wait_ge(cols_turned, 1)
            nc.scalar.activation(cols[:, :], q[:, 3, 0:P], ACT.Copy).then_inc(cols_ready, 1)
            act.wait_ge(bias_loaded, 16 * n_bias_loads)
            nc.scalar.activation(bias_hi[:, :], bias[:, :], ACT.Copy).then_inc(bias_hi_ready, 1)
            act.wait_ge(ones_set, 1)
            nc.scalar.activation(ones_r[:, :], ones[:, :], ACT.Copy).then_inc(ones_r_set, 1)
            for n in range(AHEAD):
                split_hi(n)
            turned(mains[0])
            for j, name in enumerate(mains):
                if j:
                    norm(name)
                    turned(name)
                if name.startswith("ffn"):
                    ffn(name)
                elif name.startswith("gate"):
                    gate(name)
                elif name == "mix1":
                    odd(name)
                elif name == "mix0":
                    even(name)

        @block.vector
        def _(dve):
            steps = [0]

            def link(ins):
                steps[0] += 1
                ins.then_inc(dve_step, 1)
                dve.wait_ge(dve_step, steps[0])

            def rsqrt(to, ms, half, scratch, wide, done, by=1):
                link(nc.vector.tensor_scalar(to.bitcast(I32), ms.bitcast(I32), -0.5, RSQRT_MAGIC,
                                             ALU.mult, ALU.add))
                for s in range(3):
                    if wide:
                        link(nc.vector.tensor_tensor(scratch, to, to, ALU.mult))
                        link(nc.vector.tensor_tensor(scratch, scratch, half, ALU.mult))
                        last = nc.vector.scalar_tensor_tensor(to, scratch, 1.5, to, ALU.add, ALU.mult)
                    else:
                        link(nc.vector.tensor_scalar(scratch, to, half, to, ALU.mult, ALU.mult))
                        last = nc.vector.tensor_scalar(to, scratch, 1.5, to, ALU.add, ALU.mult)
                    if s < 2 or done is None:
                        link(last)
                    else:
                        last.then_inc(done, by)

            def mean_rsqrt(to, ss, n, done=None, wide=False, at_=32):
                w = ss.shape[1]
                ms, half, scratch = (st[:, at_ + w * i:at_ + w * (i + 1)] for i in range(3))
                link(nc.vector.tensor_scalar(half, ss, -0.5 / n, -0.5 * EPS, ALU.mult, ALU.add))
                link(nc.vector.tensor_scalar(ms, ss, 1.0 / n, EPS, ALU.mult, ALU.add))
                rsqrt(to, ms, half, scratch, wide, done)

            def split_lo(m, i=None):
                parts, width = slabs.size[m]
                dve.wait_ge(hi_ready, at(i, m + 1, 6))
                nc.vector.tensor_tensor(lo[0:parts, m % RING, 0:width], raw[0:parts, m % RING, 0:width],
                                        hi[0:parts, m % RING, 0:width].bitcast(F32), ALU.subtract) \
                    .then_inc(lo_ready, 1)

            def ahead(n, i=None):
                if n + AHEAD < N:
                    split_lo(n + AHEAD, i)

            def scaled_y(name, t, to, done):
                u = gain_of[name][0]
                dve.wait_ge(y_sq, TT * squares_of[name] + t + 1)
                mean_rsqrt(st[:, 4 + t:5 + t], st[:, t:t + 1], D)
                if t == 0:
                    dve.wait_ge(gain_loaded[u % 2], 16 * (u // 2 + 1))
                scaled = nc.vector.scalar_tensor_tensor(to, y[:, t, :], st[:, 4 + t:5 + t], gain[:, u % 2, :],
                                                        ALU.mult, ALU.mult)
                if done is None:
                    link(scaled)
                else:
                    scaled.then_inc(done, 1)

            def update(name, c):
                for t in range(TT):
                    scaled_y(name, t, tmp[:, t, :], None)
                    nc.vector.scalar_tensor_tensor(x[:, t, :], tmp[:, t, :], c, x[:, t, :], ALU.mult, ALU.add) \
                        .then_inc(x_ready, 1)

            def norm(name):
                b = norm_of[name]
                for t in range(TT):
                    dve.wait_ge(x_sq, TT * b + t + 1)
                    mean_rsqrt(st[:, 6 + t:7 + t], st[:, 2 + t:3 + t], D, done=x_rms)

            def turned(name):
                b = norm_of[name]
                if b == 0:
                    dve.wait_ge(cols_ready, 1)
                for k in range(KD):
                    dve.wait_ge(xT_hi_ready, (KD * b + k) // 2 * 2 + 2)
                    nc.vector.scalar_tensor_tensor(
                        xT_lo[:, k, :], q[:, k // 2, (k % 2) * SEQ:(k % 2 + 1) * SEQ], gain_col(name, k),
                        xT_hi[:, k, :].bitcast(F32), ALU.mult, ALU.subtract).then_inc(xT_ready, 1)

            def unit(name, number, f, i=None):
                n, F = slab_of(name, f), TILES * number + f
                m = P if f < FULL else HALF
                ahead(n, i)
                if f == 0 and extra(name):
                    embeddings(name)
                    n += KP
                if f < FULL:
                    ahead(n + 1, i)
                dve.wait_ge(sil_ready, at(i, F + 1, 2))
                if F >= 2:
                    dve.wait_ge(h_lo_ready, at(i, F - 1, 2))
                up = q[0:P, f % 2, SEQ:2 * SEQ] if f < FULL else q[HALF:P, f % 2, 0:SEQ]
                nc.vector.tensor_tensor(h[0:m, f % 2, :], sil[0:m, f % 2, :], up, ALU.mult).then_inc(h_ready, 1)
                if f == FULL:
                    ahead(n + 1, i)
                elif f > 0:
                    ahead(n + 2, i)
                dve.wait_ge(h_hi_ready, at(i, F + 1, 2))
                nc.vector.tensor_tensor(h_lo[0:m, f % 2, :], h[0:m, f % 2, :],
                                        h_hi[0:m, f % 2, :].bitcast(F32), ALU.subtract).then_inc(h_lo_ready, 1)
                if f == FULL:
                    ahead(n + 2, i)

            def ffn(name):
                number = ffns[name][1]
                for f in range(LOOP0):
                    unit(name, number, f)
                with dve.Fori(0, TURNS) as i:
                    unit(name, number, LOOP0, i)
                    unit(name, number, LOOP0 + 1, i)
                for f in range(LOOP1, TILES):
                    unit(name, number, f)
                update(name, 0.5)

            def embeddings(name):
                dve.wait_ge(pT_hi_ready, int(name[-1]) + 1)
                nc.vector.tensor_tensor(pT_lo[:, :, :], y[:, 0, 0:BANK].rearrange("p (k c) -> p k c", k=KP),
                                        pT_hi[:, :, :].bitcast(F32), ALU.subtract).then_inc(pT_ready, 1)
                for k in range(KP):
                    ahead(ffns[name][0] + 1 + k)
                for t in range(TT):
                    scaled_y("p" + name, t, pn[:, t, :], p_scaled)

            def gate(name):
                l = int(name[-1])
                for k in range(KD):
                    ahead(toks[name] + k)
                for t in range(TT):
                    dve.wait_ge(gate_ready, TT * l + t + 1)
                    link(nc.vector.scalar_tensor_tensor(tmp[:, t, :], xn[:, t, :], 1.0, pn[:, t, :],
                                                        ALU.add, ALU.mult))
                    nc.vector.scalar_tensor_tensor(x[:, t, :], tmp[:, t, :], 0.5, x[:, t, :], ALU.mult, ALU.add) \
                        .then_inc(x_ready, 1)

            def mixed_lo(piece):
                b, bank, blocks, t = MIXED[piece]
                dve.wait_ge(mixT_hi_ready, piece + 1)
                nc.vector.tensor_tensor(xT_lo[:, blocks, t * P:(t + 1) * P],
                                        q[:, bank, :].rearrange("p (m c) -> p m c", m=4),
                                        xT_hi[:, blocks, t * P:(t + 1) * P].bitcast(F32), ALU.subtract) \
                    .then_inc(mixT_ready, 1)

            def odd(name):
                n0 = toks[name]
                for n in range(n0, n0 + 12):
                    ahead(n)

                def maxima(b):
                    t, h0, heads, place, key0, wide = BATCHES[b]
                    dve.wait_ge(scores_ready, b + 1)
                    if b == 0:
                        dve.wait_ge(sinks_loaded, 16)
                    s = place[:, 0:heads * wide].rearrange("p (h k) -> p h k", h=heads)
                    link(nc.vector.memset(s[0:CHUNK, :, wide - CHUNK:wide], -1e30))
                    if t:
                        link(nc.vector.memset(s[CHUNK:P, :, key0:key0 + CHUNK], -1e30))
                    link(nc.vector.reduce_max(soft_of(b, 0), scores_of(b), AX.X))
                    link(nc.vector.scalar_tensor_tensor(soft_of(b, 5), soft_of(b, 0), HD ** -0.5,
                                                        sink[:, h0:h0 + heads], ALU.mult, ALU.max))
                    link(nc.vector.tensor_tensor(soft_of(b, 1), sink[:, h0:h0 + heads], soft_of(b, 5), ALU.subtract))
                    nc.vector.tensor_scalar(soft_of(b, 2), soft_of(b, 5), -1.0, None, ALU.mult).then_inc(max_ready, 1)

                def normed(b):
                    dve.wait_ge(exp_done, b + 1)
                    link(nc.vector.tensor_tensor(soft_of(b, 3), soft_of(b, 3), soft_of(b, 4), ALU.add))
                    link(nc.vector.reciprocal(soft_of(b, 5), soft_of(b, 3)))
                    p = prob_of(b)
                    nc.vector.tensor_tensor(p, p, soft_of(b, 5).unsqueeze(2).to_broadcast(list(p.shape)),
                                            ALU.mult).then_inc(prob_ready, 1)

                def keep_turned(b):
                    dve.wait_ge(prob_turned, 2 * b + 2)
                    nc.vector.tensor_copy(probT[:, b % 2, 1024:2048], BATCHES[b][3][:, 1024:2048]) \
                        .then_inc(probT_dve, 1)

                maxima(0)
                maxima(1)
                normed(0)
                normed(1)
                keep_turned(0)
                keep_turned(1)
                maxima(2)
                for piece in range(3):
                    mixed_lo(piece)
                normed(2)
                keep_turned(2)
                mixed_lo(3)
                for k in range(KD):
                    ahead(n0 + 12 + k)
                update(name, 1.0)

            def even(name):
                n0 = toks[name]

                def per_head(v):
                    return v.unsqueeze(2).to_broadcast([P, v.shape[1], P])

                def heads(v):
                    return v.rearrange("p (h c) -> p h c", c=P)

                for n in range(N_TILE):
                    ahead(n0 + n)
                dve.wait_ge(lat_sq, 1)
                for c, n in ((64, Q_LORA), (66, KV_LORA)):
                    link(nc.vector.tensor_scalar(st[:, 72 + c - 64:74 + c - 64], st[:, c:c + 2], 1.0 / n, EPS,
                                                 ALU.mult, ALU.add))
                link(nc.vector.tensor_scalar(st[:, 76:80], st[:, 72:76], -0.5, None, ALU.mult))
                rsqrt(st[:, 68:72], st[:, 72:76], st[:, 76:80], st[:, 80:84], True, lat_rms)
                dve.wait_ge(gates_in, 1)
                z, ab = gs[:, 16:24], gs[:, 0:16].rearrange("p (t c) -> p t c", t=TT)
                link(nc.vector.tensor_tensor(z.rearrange("p (t h) -> p t h", t=TT), ab[:, :, 0:4],
                                             gs[:, 128:132].unsqueeze(1).to_broadcast([P, TT, 4]), ALU.add))
                link(nc.vector.tensor_scalar(gs[:, 24:32], z, -1.0, None, ALU.mult))
                nc.vector.tensor_tensor(gs[:, 24:32], gs[:, 24:32], z, ALU.max).then_inc(gates_raw, 1)
                dve.wait_ge(gates_exp, 2)
                link(nc.vector.scalar_tensor_tensor(gs[:, 40:48], z, 0.0, gs[:, 40:48], ALU.max, ALU.add))
                nc.vector.scalar_tensor_tensor(gs[:, 56:64].rearrange("p (t h) -> p t h", t=TT),
                                               gs[:, 40:48].rearrange("p (t h) -> p t h", t=TT), -1.0,
                                               gs[:, 136:140].unsqueeze(1).to_broadcast([P, TT, 4]),
                                               ALU.mult, ALU.mult).then_inc(gates_set, 1)
                link(nc.vector.tensor_scalar(gs[:, 48:56], gs[:, 48:56], 1.0, None, ALU.add))
                link(nc.vector.reciprocal(gs[:, 140:148], gs[:, 48:56]))
                beta = gs[:, 140:148]
                for j in range(3 * GH):
                    ahead(n0 + N_TILE + j)
                    dve.wait_ge(conv_first, j + 1)
                    for d in range(1, 4):
                        c = COL_CONV + 12 * (3 - d) + conv_col(j)
                        ins = nc.vector.scalar_tensor_tensor(convT[:, j, d:SEQ], q[:, j % 4, 0:SEQ - d],
                                                             cols[:, c:c + 1], convT[:, j, d:SEQ],
                                                             ALU.mult, ALU.add)
                        if d < 3:
                            link(ins)
                        else:
                            ins.then_inc(conv_done, 1)
                for k in range(KL):
                    dve.wait_ge(latT_hi_ready, min(k // 2 * 2 + 2, KL))
                    nc.vector.scalar_tensor_tensor(latT_lo[:, k, :], lat_bank(k), cols[:, COL_QN + k:COL_QN + k + 1],
                                                   latT_hi[:, k, :].bitcast(F32), ALU.mult, ALU.subtract) \
                        .then_inc(latT_ready, 1)
                dve.wait_ge(sums_kept, 1)
                gc, gl = gs[:, 64:72], gs[:, 72:80]
                link(nc.vector.tensor_copy(gs[:, 160:168], gc))
                link(nc.vector.tensor_tensor(gs[:, 168:176], gl, gc, ALU.subtract))
                link(nc.vector.tensor_scalar(gs[:, 192:200], gc, -1.0, None, ALU.mult))
                nc.vector.tensor_copy(gs[:, 176:192], gs[:, 80:96]).then_inc(dec_args, 1)
                for n in range(4):
                    ahead(n0 + N_Z + n)
                dve.wait_ge(grown, 1)
                wide = q_flat[:, 0:1024].rearrange("p (m c) -> p m c", m=TT * GH)
                for place, mask in ((attnT, "add_upto"), (lmat, "add_before")):
                    m = const[:, C_AT[mask]:C_AT[mask] + P].unsqueeze(1).to_broadcast([P, TT * GH, P])
                    ins = nc.vector.tensor_tensor(place[:, :, :], wide, m, ALU.add)
                    if place is attnT:
                        link(ins)
                    else:
                        ins.then_inc(decay_args, 1)
                for n in range(3):
                    ahead(n0 + N_UQ + n)
                for n in range(2):
                    ahead(n0 + N_UKV + n)
                dve.wait_ge(rope_kept, 1)
                dve.wait_ge(rope_key, 1)
                a, b = rope_in[:, :, :, 0:32], rope_in[:, :, :, 32:64]
                ra, rb = rope_out[:, :, 0:5, 0:32], rope_out[:, :, 0:5, 32:64]
                link(nc.vector.memset(rope_out[:, :, 5:7, :], 0.0))
                cos, sin = (const[:, c:c + 64].rearrange("p (t d) -> p t d", t=TT).unsqueeze(2)
                            .to_broadcast([P, TT, 5, 32]) for c in (C_COS, C_SIN))

                def rope_op(o, x0, x1, op, done=None):
                    for t in range(TT):
                        ins = nc.vector.tensor_tensor(o[:, t], x0[:, t], x1[:, t], op)
                        if done is None or t == 0:
                            link(ins)
                        else:
                            ins.then_inc(done, 1)

                rt = rope_tmp[:, :, :, :]
                rope_op(ra, a, cos, ALU.mult)
                rope_op(rt, b, sin, ALU.mult)
                rope_op(ra, ra, rt, ALU.subtract)
                rope_op(rb, b, cos, ALU.mult)
                rope_op(rt, a, sin, ALU.mult)
                rope_op(rb, rb, rt, ALU.add)
                nc.vector.tensor_copy(rope_out[:, :, 7, :], rope_out[:, :, 4, :]).then_inc(rope_ready, 1)
                for t in range(TT):
                    dve.wait_ge(m_scores, t + 1)
                    link(nc.vector.memset(m_scores_of(t)[0:CHUNK, :, (2 * t + 1) * CHUNK:], -1e30))
                    r = slice(4 * t, 4 * t + 4)
                    link(nc.vector.reduce_max(m_soft[:, 0, r], m_scores_of(t), AX.X))
                    nc.vector.tensor_scalar(m_soft[:, 1, r], m_soft[:, 0, r], -M_SCALE, None, ALU.mult) \
                        .then_inc(m_max, 1)
                for t in range(TT):
                    r = slice(4 * t, 4 * t + 4)
                    dve.wait_ge(m_exp, t + 1)
                    link(nc.vector.reciprocal(m_soft[:, 3, r], m_soft[:, 2, r]))
                    p = m_prob_of(t)
                    nc.vector.tensor_tensor(p, p, m_soft[:, 3, r].unsqueeze(2).to_broadcast(list(p.shape)),
                                            ALU.mult).then_inc(m_prob_ready, 1)
                dve.wait_ge(m_turned, 3)
                nc.vector.tensor_copy(m_probT[:, 2 * BANK:3 * BANK], y[:, 1, BANK:2 * BANK]).then_inc(m_probT_dve, 1)
                for j in range(2):
                    dve.wait_ge(emix_hi, j + 1)
                    nc.vector.tensor_tensor(xT_lo[:, 4 + 2 * j:6 + 2 * j, :].rearrange("p m c -> p (m c)"),
                                            y[:, 0, j * BANK:(j + 1) * BANK],
                                            xT_hi[:, 4 + 2 * j:6 + 2 * j, :].bitcast(F32)
                                            .rearrange("p m c -> p (m c)"), ALU.subtract).then_inc(emix_ready, 1)
                for s_, place in ((0, inv_t), (1, inv_u)):
                    for t in range(TT):
                        dve.wait_ge(tok_sq, 2 * s_ + t + 1)
                        link(nc.vector.reduce_sum(st[:, 96 + 8 * s_ + 4 * t:100 + 8 * s_ + 4 * t],
                                                  place[:, 4 * t:4 * t + 4, :], AX.X))
                    c = slice(96 + 8 * s_, 104 + 8 * s_)
                    to = slice(112 + 8 * s_, 120 + 8 * s_)
                    link(nc.vector.tensor_scalar(st[:, 128:136], st[:, c], EPS, None, ALU.add))
                    link(nc.vector.tensor_scalar(st[:, 136:144], st[:, 128:136], -0.5, None, ALU.mult))
                    rsqrt(st[:, to], st[:, 128:136], st[:, 136:144], st[:, 144:152], True, None)
                    if s_:
                        link(nc.vector.tensor_scalar(st[:, to], st[:, to], P ** -0.5, None, ALU.mult))
                    out_ = (k_tok, q_tok)[s_]
                    for t in range(TT):
                        nc.vector.tensor_tensor(heads(out_[:, t, :]), heads(q[:, 2 * (1 - s_) + t, :]),
                                                per_head(st[:, 112 + 8 * s_ + 4 * t:116 + 8 * s_ + 4 * t]),
                                                ALU.mult).then_inc(tok_ready, 1)
                for t in range(TT):
                    dve.wait_ge(tok_turned, 4 + t + 1)
                    nc.vector.tensor_tensor(rhs[:, 4 * t:4 * t + 4, 0:P], heads(q[:, 2 + t, :]),
                                            per_head(beta[:, 4 * t:4 * t + 4]), ALU.mult).then_inc(rhs_ready, 1)
                dve.wait_ge(dec_ready, 1)
                dve.wait_ge(tok_ready, 2)
                link(nc.vector.tensor_tensor(gs[:, 200:208], beta, gs[:, 96:104], ALU.mult))
                for t in range(TT):
                    r = slice(4 * t, 4 * t + 4)
                    nc.vector.tensor_tensor(rhs[:, r, P:2 * P], heads(k_tok[:, t, :]),
                                            per_head(gs[:, 200 + 4 * t:204 + 4 * t]), ALU.mult).then_inc(rhs_ready, 1)
                    nc.vector.tensor_tensor(heads(k_dec[:, t, :]), heads(k_tok[:, t, :]),
                                            per_head(gs[:, 104 + 4 * t:108 + 4 * t]), ALU.mult).then_inc(rhs_ready, 1)
                dve.wait_ge(decay_ready, TT * GH)
                link(nc.vector.tensor_tensor(lmat[:, :, :], lmat[:, :, :], per_head(beta), ALU.mult))
                eye = ident.unsqueeze(1).to_broadcast([P, TT * GH, P])
                nc.vector.tensor_copy(inv_t[:, :, :], eye).then_inc(inv_ready, 1)
                nc.vector.tensor_copy(inv_u[:, :, :], eye).then_inc(inv_ready, 2)
                dve.wait_ge(back_kept, 2)
                for t in range(TT):
                    nc.vector.tensor_tensor(qdT[:, :, t * P:(t + 1) * P], qnT[:, :, t * P:(t + 1) * P],
                                            cross[:, 4 * t:4 * t + 4, :], ALU.mult).then_inc(qd_ready, 1)
                dve.wait_ge(grams, 1)
                nc.vector.tensor_tensor(lmat[:, :, :].rearrange("p m c -> p (m c)"), q_flat[:, 0:1024],
                                        lmat[:, :, :].rearrange("p m c -> p (m c)"), ALU.mult).then_inc(l_ready, 1)
                dve.wait_ge(grams, 2)
                nc.vector.tensor_tensor(attnT[:, :, :].rearrange("p m c -> p (m c)"), q_flat[:, 1024:2048],
                                        attnT[:, :, :].rearrange("p m c -> p (m c)"), ALU.mult).then_inc(l_ready, 1)
                dve.wait_ge(qd_ready, TT)
                with dve.Fori(0, LEVELS) as i:
                    for t in range(TT):
                        r = slice(4 * t, 4 * t + 4)
                        mask = const[:, bass.ds(i * P + C_LEVEL, P)].unsqueeze(1).to_broadcast([P, 4, P])
                        dve.wait_ge(cross_made, i * TT + (t + 1))
                        nc.vector.tensor_tensor(cross[:, r, :], heads(q[:, t, :]), mask, ALU.mult) \
                            .then_inc(cross_ready, 1)
                    for t in range(TT):
                        r = slice(4 * t, 4 * t + 4)
                        dve.wait_ge(inv_made, i * 4 + (2 * t + 2))
                        for place, bank in ((inv_t, t), (inv_u, 2 + t)):
                            nc.vector.tensor_tensor(place[:, r, :], heads(q[:, bank, :]), place[:, r, :], ALU.add) \
                                .then_inc(inv_ready, 1)
                dve.wait_ge(solved_kept, 2)
                for n in range(4):
                    t, r = n // 2, slice((n % 2) * CHUNK, (n % 2 + 1) * CHUNK)
                    dve.wait_ge(read_out, n) if n else None
                    if n:
                        nc.vector.tensor_tensor(v_new[r, t, :], u_tok[r, t, :], q[r, 0, :], ALU.subtract) \
                            .then_inc(v_new_ready, 1)
                    if n == 3:
                        break
                    dve.wait_ge(kv_made, n + 1)
                    if n == 0:
                        nc.vector.tensor_copy(states[1][:, :, :].rearrange("p h c -> p (h c)"), q[:, 2, :]) \
                            .then_inc(state_ready, 4)
                    else:
                        for hd in range(GH):
                            c = 112 + 8 * (n % 2) + 4 * t + hd
                            nc.vector.scalar_tensor_tensor(states[(n + 1) % 2][:, hd, :], states[n % 2][:, hd, :], gs[:, c:c + 1],
                                                           q[:, 2, hd * P:(hd + 1) * P], ALU.mult, ALU.add) \
                                .then_inc(state_ready, 1)
                dve.wait_ge(z_ready, 1)
                for t in range(TT):
                    dve.wait_ge(o_sq, t + 1)
                    link(nc.vector.reduce_sum(st[:, 152 + 4 * t:156 + 4 * t], heads(k_dec_free(t)), AX.X))
                    mean_rsqrt(st[:, 160 + 4 * t:164 + 4 * t], st[:, 152 + 4 * t:156 + 4 * t], P, wide=True, at_=168)
                    link(nc.vector.tensor_tensor(heads(o_tok[:, t, :]), heads(q[:, 1 + 2 * t, :]),
                                                 per_head(st[:, 160 + 4 * t:164 + 4 * t]), ALU.mult))
                    nc.vector.tensor_tensor(o_tok[:, t, :], o_tok[:, t, :], z_gate[:, t, :], ALU.mult) \
                        .then_inc(o_ready, 1)
                for j in range(2):
                    dve.wait_ge(emix_hi, 2 + j + 1)
                    nc.vector.tensor_tensor(xT_lo[:, 2 * j:2 * j + 2, :].rearrange("p m c -> p (m c)"), q[:, j, :],
                                            xT_hi[:, 2 * j:2 * j + 2, :].bitcast(F32)
                                            .rearrange("p m c -> p (m c)"), ALU.subtract).then_inc(emix_ready, 1)
                for k in range(KD):
                    ahead(n0 + N_OUT + k)
                update(name, 1.0)

            nc.vector.memset(rows[:, :], 1.0).then_inc(rows_clear, 1)
            nc.vector.memset(bias[:, :], 0.0).then_inc(bias_clear, 1)
            nc.vector.memset(ones[:, :], 1.0).then_inc(ones_set, 1)
            norm(mains[0])
            dve.wait_ge(bias_hi_ready, 1)
            nc.vector.tensor_tensor(bias_lo[:, :], bias[:, :], bias_hi[:, :].bitcast(F32), ALU.subtract) \
                .then_inc(bias_ready, 1)
            for n in range(AHEAD):
                split_lo(n)
            turned(mains[0])
            for j, name in enumerate(mains):
                if j:
                    norm(name)
                    turned(name)
                if name.startswith("ffn"):
                    ffn(name)
                elif name.startswith("gate"):
                    gate(name)
                elif name == "mix1":
                    odd(name)
                elif name == "mix0":
                    even(name)

        @block.tensor
        def _(pe):
            def split_product(to, a_hi, a_lo, b_hi, b_lo, start, stop):
                nc.tensor.matmul(to, a_hi, b_hi, start=start, stop=False)
                nc.tensor.matmul(to, a_hi, b_lo, start=False, stop=False)
                return nc.tensor.matmul(to, a_lo, b_hi, start=False, stop=stop)

            def norm(name):
                b = norm_of[name]
                for t in range(TT):
                    pe.wait_ge(xn_ready, TT * b + t + 1)
                    for k in range(KD):
                        c = (k % 2) * SEQ + t * P
                        mm = nc.tensor.transpose(q[:, k // 2, c:c + P], xn[:, t, k * P:(k + 1) * P], ident)
                        if t == TT - 1 and k % 2:
                            mm.then_inc(xn_turned, 1)

            def token_major(n0, count, aT_hi, aT_lo, ready, bias_row=None):
                started = bias_row is not None
                if started:
                    r = bias_row
                    for t in range(TT):
                        for half in range(2):
                            c = slice(half * BANK, (half + 1) * BANK)
                            nc.tensor.matmul(y[:, t, c], ones_r[r:r + 1, :], bias_hi[r:r + 1, c],
                                             start=True, stop=False)
                            nc.tensor.matmul(y[:, t, c], ones_r[r:r + 1, :], bias_lo[r:r + 1, c],
                                             start=False, stop=False)
                for k in range(count):
                    n = n0 + k
                    ready(k)
                    pe.wait_ge(lo_ready, n + 1)
                    for t in range(TT):
                        for half in range(2):
                            c = slice(half * BANK, (half + 1) * BANK)
                            a = slice(t * P, (t + 1) * P)
                            mm = split_product(y[:, t, c], aT_hi[:, k, a], aT_lo[:, k, a],
                                               hi[:, n % RING, c], lo[:, n % RING, c],
                                               k == 0 and not started, k == count - 1)
                        if k == count - 1 and t == 0:
                            mm.then_inc(y_first, 1)
                    mm.then_inc(slab_used, 1)

            def xT(name):
                b = norm_of[name]
                return lambda k: pe.wait_ge(xT_ready, (KD * b + k) // 2 * 2 + 2)

            def column_tile(to, n, ready=None, m=slice(0, P)):
                for k in range(KD):
                    if ready:
                        ready(k)
                    w = slice(k * P, (k + 1) * P)
                    mm = split_product(to, hi[:, n % RING, w], lo[:, n % RING, w],
                                       xT_hi[:, k, :], xT_lo[:, k, :], k == 0, k == KD - 1)
                mm.then_inc(slab_used, 1)
                return mm

            def down(n, F, f, i=None, start=False, stop=False):
                m = P if f < FULL else HALF
                pe.wait_ge(lo_ready, at(i, n + 1, 6))
                pe.wait_ge(h_lo_ready, at(i, F + 1, 2))
                for t in range(TT):
                    a = slice(t * P, (t + 1) * P)
                    for half in range(2):
                        c = slice(half * BANK, (half + 1) * BANK)
                        mm = split_product(y[:, t, c], h_hi[0:m, f % 2, a], h_lo[0:m, f % 2, a],
                                           hi[0:m, n % RING, c], lo[0:m, n % RING, c], start, stop)
                    if stop and t == 0:
                        mm.then_inc(y_first, 1)
                mm.then_inc(slab_used, 1)

            def unit(name, number, f, i=None, ready=None):
                n, F = slab_of(name, f), TILES * number + f
                if F >= 2:
                    pe.wait_ge(h_ready, at(i, F - 1, 2))
                if f == 0 and extra(name):
                    turn_embeddings(name)
                pe.wait_ge(lo_ready, at(i, n + 1, 6))
                column_tile(q[:, f % 2, 0:SEQ], n, ready)
                if f == 0 and extra(name):
                    pe.wait_ge(pT_ready, int(name[-1]) + 1)
                    token_major(n + 1, KP, pT_hi, pT_lo, lambda k: None)
                    n += KP
                if f == 1 and extra(name):
                    pe.wait_ge(p_scaled, TT * (int(name[-1]) + 1))
                if f < FULL:
                    pe.wait_ge(lo_ready, at(i, n + 2, 6))
                    column_tile(q[:, f % 2, SEQ:2 * SEQ], n + 1)
                if f == FULL:
                    down(n + 1, F - 1, f - 1, i)
                elif f > 0:
                    down(n + 2, F - 1, f - 1, i, start=f == 1)
                if f == FULL:
                    down(n + 2, F, f, i, stop=True)

            def turn_embeddings(name):
                pe.wait_ge(p_loaded, 16 * (int(name[-1]) + 1))
                for k in range(KP):
                    for t in range(TT):
                        c = k * SEQ + t * P
                        mm = nc.tensor.transpose(y[:, 0, c:c + P], p_in[:, t, k * P:(k + 1) * P], ident)
                mm.then_inc(p_turned, 1)

            def ffn(name):
                number = ffns[name][1]
                for f in range(LOOP0):
                    unit(name, number, f, ready=xT(name) if f == 0 else None)
                with pe.Fori(0, TURNS) as i:
                    unit(name, number, LOOP0, i)
                    unit(name, number, LOOP0 + 1, i)
                for f in range(LOOP1, TILES):
                    unit(name, number, f)

            def odd(name):
                n0 = toks[name]

                def tile(j, n, ready=None):
                    if j >= 4:
                        pe.wait_ge(qk_kept, j - 3)
                    pe.wait_ge(lo_ready, n + 1)
                    column_tile(q[:, j % 4, 0:SEQ], n, ready)

                tile(0, n0, xT(name))
                tile(1, n0 + 1)
                for t in range(TT):
                    nc.tensor.matmul(y[:, t, 0:256], ones_r[96:97, :], bias_hi[96:97, 0:256], start=True, stop=False)
                    nc.tensor.matmul(y[:, t, 0:256], ones_r[96:97, :], bias_lo[96:97, 0:256], start=False, stop=False)
                for j in range(2):
                    n = n0 + 2 + j
                    pe.wait_ge(lo_ready, n + 1)
                    for t in range(TT):
                        a = slice(t * P, (t + 1) * P)
                        for k in range(4):
                            w = slice(k * 256, (k + 1) * 256)
                            mm = split_product(y[:, t, 0:256], xT_hi[:, 4 * j + k, a], xT_lo[:, 4 * j + k, a],
                                               hi[:, n % RING, w], lo[:, n % RING, w], False, j == 1 and k == 3)
                    mm.then_inc(slab_used, 1)
                for j in range(2, 10):
                    tile(j, n0 + 2 + j)

                def scores(b):
                    t, h0, heads, place, key0, wide = BATCHES[b]
                    for j in range(heads):
                        hd = h0 + j
                        a, half = hd // 8, (hd // 4 % 2) * HD
                        r = slice(half, half + HD)
                        mm = nc.tensor.matmul(scores_of(b)[:, j, :], qkT[r, 2 + 4 * a + hd % 4, t * P:(t + 1) * P],
                                              qkT[r, a, key0:key0 + wide - key0], start=True, stop=True)
                    mm.then_inc(scores_ready, 1)

                def turn(b):
                    t, h0, heads, place, key0, wide = BATCHES[b]
                    pe.wait_ge(prob_ready, b + 1)
                    if b:
                        pe.wait_ge(zero_set, b)
                    for j in range(16):
                        c = slice(j * P, (j + 1) * P)
                        mm = nc.tensor.transpose(place[:, c], prob[:, b % 2, c], ident)
                        if j % 8 == 7:
                            mm.then_inc(prob_turned, 1)

                def mix(b):
                    t, h0, heads, place, key0, wide = BATCHES[b]
                    pe.wait_ge(probT_act, b + 1)
                    pe.wait_ge(probT_dve, b + 1)
                    for j in range(heads):
                        hd = h0 + j
                        g = hd // 4
                        c0 = (hd // 2) * P if t == 0 else 1024 + (hd // 2) * P
                        to = q_flat[(hd % 2) * HD:(hd % 2 + 1) * HD, c0:c0 + P]
                        for kt in range(t + 1):
                            c = j * wide + kt * P
                            mm = nc.tensor.matmul(to, val[:, kt, g * HD:(g + 1) * HD], probT[:, b % 2, c:c + P],
                                                  start=kt == 0, stop=kt == t)
                    mm.then_inc(mixed, 1)

                pe.wait_ge(val_kept, 1)
                pe.wait_ge(qk_kept, 10)
                scores(0)
                scores(1)
                turn(0)
                turn(1)
                pe.wait_ge(probT_act, 1)
                pe.wait_ge(probT_dve, 1)
                scores(2)
                pe.wait_ge(probT_act, 2)
                pe.wait_ge(probT_dve, 2)
                mix(0)
                mix(1)
                turn(2)
                mix(2)
                pe.wait_ge(mixT_ready, len(MIXED))
                token_major(n0 + 12, KD, xT_hi, xT_lo, lambda k: None, bias_row=64)

            def even(name):
                n0 = toks[name]
                ready = xT(name)
                for part, width, c0 in ((N_A, W_A, 0), (N_KV, W_KV, BANK)):
                    for j in range(4):
                        pair_slab(n0 + part + j, j, width, c0, ready if part == N_A else None)
                for j in range(3 * GH):
                    n = n0 + N_TILE + j
                    if j >= 4:
                        pe.wait_ge(conv_done, j - 3)
                    pe.wait_ge(lo_ready, n + 1)
                    column_tile(q[:, j % 4, 0:SEQ], n)
                pe.wait_ge(lat_ready, 1)
                pe.wait_ge(rope_key, 1)
                for k in range(KL):
                    for t in range(TT):
                        mm = nc.tensor.transpose(lat_bank(k)[:, t * P:(t + 1) * P], lat[:, t, k * P:(k + 1) * P],
                                                 ident)
                    if k % 2 or k == KL - 1:
                        mm.then_inc(lat_turned, 1)
                pe.wait_ge(gates_set, 1)
                for j, m in enumerate(("upto", "same", "first", "second")):
                    mm = nc.tensor.matmul(y[:, 1, 8 * j:8 * j + 8], const[:, C_AT[m]:C_AT[m] + P], gs[:, 56:64],
                                          start=True, stop=True)
                mm.then_inc(sums_ready, 1)
                pe.wait_ge(latT_ready, KL)
                pe.wait_ge(sums_kept, 1)
                for j in range(4):
                    pair_slab(n0 + N_Z + j, j, BANK, 0, None)
                pe.wait_ge(conv_done, 3 * GH)
                for m in range(TT * GH):
                    mm = nc.tensor.matmul(q_flat[:, m * P:(m + 1) * P], gs[:, 56 + m:57 + m].to_broadcast([P, P]),
                                          const[:, C_AT["upto"]:C_AT["upto"] + P], start=True, stop=True)
                mm.then_inc(wide_sums, 1)
                pe.wait_ge(decay_args, 1)

                for part, first, count, width, made in ((N_UQ, 0, 3, 192, qn_made), (N_UKV, 3, 2, 256, kn_made)):
                    if part == N_UKV:
                        pe.wait_ge(q_nope_kept, GH)
                    pe.wait_ge(lo_ready, n0 + part + count)
                    for hd in range(GH):
                        for k in range(count):
                            w = slice(hd * width, hd * width + P)
                            s_ = (n0 + part + k) % RING
                            mm = split_product(q[:, hd, 0:SEQ], hi[:, s_, w], lo[:, s_, w],
                                               latT_hi[:, first + k, :], latT_lo[:, first + k, :],
                                               k == 0, k == count - 1)
                    mm.then_inc(made, 1)
                    if part == N_UKV:
                        pe.wait_ge(rope_kept, 1)
                    for t in range(TT):
                        a = slice(t * P, (t + 1) * P)
                        for k in range(count):
                            s_ = (n0 + part + k) % RING
                            w_hi, w_lo = (v[:, s_, 0:GH * width].rearrange("p (h c) -> p h c", h=GH)[:, :, P:width]
                                          for v in (hi, lo))
                            mm = split_product(y[:, t, BANK:BANK + GH * (width - P)], latT_hi[:, first + k, a],
                                               latT_lo[:, first + k, a], w_hi, w_lo, k == 0, k == count - 1)
                            if t == TT - 1:
                                mm.then_inc(slab_used, 1)
                pe.wait_ge(rope_ready, 1)
                pe.wait_ge(m_val_kept, 1)
                for r in range(4):
                    for t in range(TT):
                        c = BANK + (r % 2) * SEQ + t * P
                        mm = nc.tensor.transpose(y[:, r // 2, c:c + P],
                                                 rope_out[:, t, 2 * r:2 * r + 2, :].rearrange("p h c -> p (h c)"),
                                                 ident)
                mm.then_inc(rope_turned, 1)
                pe.wait_ge(k_nope_kept, GH)
                pe.wait_ge(ropeT_kept, 1)
                pe.wait_ge(z_in, 1)
                for t in range(TT):
                    for hd in range(GH):
                        to, a, w = m_scores_of(t)[:, hd, :], slice(t * P, (t + 1) * P), (t + 1) * P
                        nc.tensor.matmul(to, q_nopeT[:, hd, a], k_nopeT[:, hd, 0:w], start=True, stop=False)
                        mm = nc.tensor.matmul(to, ropeT[:, hd // 2, a], ropeT[:, 2 + hd % 2, 0:w],
                                              start=False, stop=True)
                    mm.then_inc(m_scores, 1)
                for t in range(TT):
                    pe.wait_ge(m_prob_ready, t + 1)
                    for j in range(GH * (t + 1)):
                        c = slice(j * P, (j + 1) * P)
                        src = t * GH * P + j * P
                        mm = nc.tensor.transpose(y[:, t, c], m_prob[:, src:src + P], ident)
                        if j % 4 == 3:
                            mm.then_inc(m_turned, 1)
                pe.wait_ge(m_probT_act, 2)
                pe.wait_ge(m_probT_dve, 1)
                for hd in range(GH):
                    for t in range(TT):
                        c = hd * SEQ + t * P
                        for kt in range(t + 1):
                            src = (t * GH + hd * (t + 1) + kt) * P
                            mm = nc.tensor.matmul(y[:, 0, c:c + P], m_val[:, kt, hd * P:(hd + 1) * P],
                                                  m_probT[:, src:src + P], start=kt == 0, stop=kt == t)
                mm.then_inc(m_mixed, 1)
                pe.wait_ge(conv_ready, 3 * GH)
                for s_, banks in ((0, 2), (1, 0), (2, 2)):
                    if s_ == 2:
                        pe.wait_ge(tok_ready, 2)
                    for t in range(TT):
                        for hd in range(GH):
                            mm = nc.tensor.transpose(q[:, banks + t, hd * P:(hd + 1) * P],
                                                     convT[:, s_ * GH + hd, t * P:(t + 1) * P], ident)
                        mm.then_inc(tok_turned, 1)
                for s_, src in ((0, k_tok), (1, q_tok)):
                    pe.wait_ge(tok_ready, 4)
                    if s_:
                        pe.wait_ge(rhs_ready, 2)
                    for hd in range(GH):
                        for t in range(TT):
                            c = s_ * 1024 + hd * SEQ + t * P
                            mm = nc.tensor.transpose(q_flat[:, c:c + P], src[:, t, hd * P:(hd + 1) * P], ident)
                    mm.then_inc(back_turned, 1)
                for s_, b in ((0, knT), (1, qnT)):
                    pe.wait_ge(back_kept, s_ + 1)
                    for m in range(TT * GH):
                        t, hd = m // GH, m % GH
                        a = slice(t * P, (t + 1) * P)
                        c = s_ * 1024 + m * P
                        mm = nc.tensor.matmul(q_flat[:, c:c + P], knT[:, hd, a], b[:, hd, a], start=True, stop=True)
                    mm.then_inc(grams, 1)
                pe.wait_ge(l_ready, 2)
                pe.wait_ge(qd_ready, TT)
                pe.wait_ge(inv_ready, 3)
                with pe.Fori(0, LEVELS) as i:
                    for t in range(TT):
                        for m in range(4 * t, 4 * t + 4):
                            if m == 4 * t:
                                pe.wait_ge(inv_ready, i * 4 + 2 * t + 1)
                            c = (m % 4) * P
                            mm = nc.tensor.matmul(q[:, t, c:c + P], lmat[:, m, :], inv_u[:, m, :],
                                                  start=True, stop=True)
                        mm.then_inc(cross_made, 1)
                    for t in range(TT):
                        pe.wait_ge(cross_ready, i * TT + (t + 1))
                        for bank, left, right in ((t, cross, inv_t), (2 + t, inv_t, cross)):
                            for m in range(4 * t, 4 * t + 4):
                                c = (m % 4) * P
                                mm = nc.tensor.matmul(q[:, bank, c:c + P], left[:, m, :], right[:, m, :],
                                                      start=True, stop=True)
                            mm.then_inc(inv_made, 1)
                pe.wait_ge(inv_ready, 4 * LEVELS + 3)
                pe.wait_ge(rhs_ready, 6)
                for m in range(TT * GH):
                    mm = nc.tensor.matmul(q_flat[:, m * P:(m + 1) * P], inv_u[:, m, :], rhs[:, m, 0:P],
                                          start=True, stop=True)
                mm.then_inc(solved, 1)
                for m in range(TT * GH):
                    mm = nc.tensor.matmul(q_flat[:, 1024 + m * P:1024 + (m + 1) * P], rhs[:, m, P:2 * P],
                                          inv_u[:, m, :], start=True, stop=True)
                mm.then_inc(solved, 1)
                pe.wait_ge(solved_kept, 2)
                for n in range(4):
                    t, r = n // 2, slice((n % 2) * CHUNK, (n % 2 + 1) * CHUNK)
                    v = v_new if n else u_tok
                    if n:
                        pe.wait_ge(state_ready, 4 * n)
                        for hd in range(GH):
                            mm = nc.tensor.matmul(q[r, 0, hd * P:(hd + 1) * P], wT[:, 4 * t + hd, r],
                                                  states[n % 2][:, hd, :], start=True, stop=True)
                        mm.then_inc(read_out, 1)
                        pe.wait_ge(v_new_ready, n)
                    if n < 3:
                        for hd in range(GH):
                            c = slice(hd * P, (hd + 1) * P)
                            mm = nc.tensor.matmul(q[:, 2, c], k_dec[r, t, c], v[r, t, c], start=True, stop=True)
                        mm.then_inc(kv_made, 1)
                    for hd in range(GH):
                        c = slice(hd * P, (hd + 1) * P)
                        if n:
                            nc.tensor.matmul(q[r, 1 + 2 * t, c], qdT[:, hd, t * P + r.start:t * P + r.stop],
                                             states[n % 2][:, hd, :], start=True, stop=False)
                        mm = nc.tensor.matmul(q[r, 1 + 2 * t, c], attnT[r, 4 * t + hd, r], v[r, t, c],
                                              start=n == 0, stop=True)
                    if n % 2:
                        mm.then_inc(o_made, 1)
                pe.wait_ge(o_ready, TT)
                for hd in range(GH):
                    for t in range(TT):
                        c = hd * SEQ + t * P
                        mm = nc.tensor.transpose(q_flat[:, c:c + P], o_tok[:, t, hd * P:(hd + 1) * P], ident)
                mm.then_inc(o_turned, 1)
                pe.wait_ge(emix_ready, 4)
                token_major(n0 + N_OUT, KD, xT_hi, xT_lo, lambda k: None)

            def pair_slab(n, j, width, c0, ready):
                pe.wait_ge(lo_ready, n + 1)
                for kk in range(2):
                    k = 2 * j + kk
                    if ready:
                        ready(k)
                    w = slice(kk * width, (kk + 1) * width)
                    for t in range(TT):
                        a = slice(t * P, (t + 1) * P)
                        mm = split_product(y[:, t, c0:c0 + width], xT_hi[:, k, a], xT_lo[:, k, a],
                                           hi[:, n % RING, w], lo[:, n % RING, w], k == 0, k == KD - 1)
                mm.then_inc(slab_used, 1)

            pe.wait_ge(const_loaded, 16)
            pe.wait_ge(rows_loaded, 16 * n_row_loads)
            nc.tensor.transpose(q[:, 3, 0:P], rows[:, :], ident).then_inc(cols_turned, 1)
            pe.wait_ge(cols_ready, 1)
            norm(mains[0])
            for j, name in enumerate(mains):
                if j:
                    norm(name)
                if name.startswith("ffn"):
                    ffn(name)
                elif name.startswith("gate"):
                    pe.wait_ge(bias_ready, 1)
                    token_major(toks[name], KD, xT_hi, xT_lo, xT(name), bias_row=32 * int(name[-1]))
                elif name == "mix1":
                    odd(name)
                elif name == "mix0":
                    even(name)


_INS = ["x", "p", "ffn1_pre", "ffn1_wgu", "ffn1_wd", "ffn1_post", "mix_pre", "mix_post", "ffn2_pre", "ffn2_wgu",
        "ffn2_wd", "ffn2_post", "ple_gate_w", "ple_gate_b", "ple_proj", "ple_norm", "ab_w_in", "gdn_conv",
        "gdn_a_log", "gdn_dt_bias", "gdn_out_norm", "mla_q_norm", "mla_w_uq", "mla_kv_norm", "mla_w_ukv",
        "ab_w_out", "swa_w_qkv", "swa_b_qkv", "swa_sinks", "swa_w_o", "swa_b_o"]
PHASES = ["ffn1_0", "mix0", "ffn2_0", "gate0", "ffn1_1", "mix1", "ffn2_1", "gate1"]


def kernel(**inputs):
    import concourse.bacc as bacc
    from concourse.bass_utils import run_bass_kernel_spmd

    nc = bacc.Bacc("TRN2", target_bir_lowering=False, num_devices=1)
    arrays = {f"in_{n}": np.ascontiguousarray(inputs[n]) for n in _INS}
    arrays["in_const"] = shape_constants()
    io = {n[3:]: nc.dram_tensor(n, a.shape, mybir.dt.from_np(a.dtype), kind="ExternalInput").ap()
          for n, a in arrays.items()}
    out = nc.dram_tensor("out", (1, SEQ, D), F32, kind="ExternalOutput").ap()
    encoder(nc, io, out, PHASES)
    r = run_bass_kernel_spmd(nc, [arrays], core_ids=[0])
    return r.results[0]["out"]
```

```python
from contextlib import ExitStack

import numpy as np

import concourse.bass as bass
from concourse import mybir

F32 = mybir.dt.float32
F32R = mybir.dt.float32r
I32 = mybir.dt.int32
ALU = mybir.AluOpType
ACT = mybir.ActivationFunctionType
AX = mybir.AxisListType

P = 128
SEQ = 256
TT = SEQ // P
D = 1024
KD = D // P
BANK = 512
D_FF = 2752
FULL = D_FF // P
HALF = D_FF - FULL * P
TILES = FULL + 1
PLE = 256
KP = PLE // P
CHUNK = 64
EPS = 1e-6
RSQRT_MAGIC = float(0x5F3759DF)

WARM = 7
RING = 6
AHEAD = 4
SLAB = 1024

COL_FFN1, COL_MIX, COL_FFN2, COL_CONV = 0, 16, 32, 48
COL_QN, COL_KVN, COL_BQK, COL_ONE = 96, 99, 101, 111
CONSTS = ["ident", "upto", "same", "first", "second", "add_upto", "add_before", "pairs"]
C_AT = {name: P * i for i, name in enumerate(CONSTS)}
LEVELS = 6
C_LEVEL = P * len(CONSTS)
C_COS = C_LEVEL + P * LEVELS
C_SIN = C_COS + 64
C_ALL = C_SIN + 64


def shape_constants():
    r = np.arange(P)
    row, col = r[:, None], r[None, :]
    same = (row // CHUNK) == (col // CHUNK)
    blocks = {
        "ident": row == col,
        "upto": same & (row <= col),
        "same": same,
        "first": (row < CHUNK) & (col >= 0),
        "second": (row >= CHUNK) & (col >= 0),
        "add_upto": np.where(same & (row <= col), 0.0, -1e30),
        "add_before": np.where(same & (col < row), 0.0, 1e30),
        "pairs": np.where((row // 2 == col // 2) & (col < row), -1.0, 0.0),
    }
    out = [np.asarray(blocks[n], np.float32) for n in CONSTS]
    for level in range(LEVELS):
        b = 1 << level
        pair = (row // (2 * b) == col // (2 * b)) & ((row // b) % 2 == 0) & ((col // b) % 2 == 1)
        out.append(np.where(pair, -1.0, 0.0).astype(np.float32))
    half = 32
    inv = np.float32(10000.0) ** (-np.arange(half, dtype=np.float32) / np.float32(half))
    ang = np.arange(SEQ, dtype=np.float32)[:, None] * inv[None, :].astype(np.float32)
    for fn in (np.cos, np.sin):
        out.append(fn(ang).astype(np.float32).reshape(TT, P, half).transpose(1, 0, 2).reshape(P, TT * half))
    return np.ascontiguousarray(np.concatenate(out, axis=1))


class Slabs:

    def __init__(self):
        self.load = []
        self.size = []
        self.loaded = []
        self.total = [0] * RING

    def add(self, parts, width, pieces):
        n = len(self.load)
        self.load.append(pieces)
        self.size.append((parts, width))
        self.total[n % RING] += 16 * len(pieces)
        self.loaded.append(self.total[n % RING])
        return n


def encoder(nc, io, out, phases):
    ctx = ExitStack()
    with ctx:
        def sem(name):
            return ctx.enter_context(nc.semaphore(name))

        origin = -(-nc.sbuf_base // 32) * 32
        ctx.enter_context(nc.sbuf_tensor("fence", [P, 207 * 256], F32))

        def at_kb(name, kb, shape, dt=F32):
            return nc.alloc_sbuf_tensor_at(name, shape, dt, offset=origin + int(kb * 1024))

        raw = at_kb("raw", 0, [P, RING, SLAB])
        hi = at_kb("hi", 24, [P, RING, SLAB], F32R)
        lo = at_kb("lo", 48, [P, RING, SLAB], F32R)
        x = at_kb("x", 72, [P, TT, D])
        xn = at_kb("xn", 80, [P, TT, D])
        xT_hi = at_kb("xT_hi", 88, [P, KD, SEQ], F32R)
        xT_lo = at_kb("xT_lo", 96, [P, KD, SEQ], F32R)
        gain = at_kb("gain", 104, [P, 2, D])
        tmp = at_kb("tmp", 112, [P, TT, D])
        const = at_kb("const", 120, [P, C_ALL])
        bias_hi = at_kb("bias_hi", 128, [P, D], F32R)
        bias_lo = at_kb("bias_lo", 132, [P, D], F32R)
        ones = at_kb("ones", 136, [P, P])
        ones_r = at_kb("ones_r", 136.5, [P, P], F32R)
        rows = at_kb("rows", 137, [P, P])
        cols = at_kb("cols", 137.5, [P, P])
        st = at_kb("st", 138, [P, 192])
        SCOPE = 139
        sil = at_kb("sil", SCOPE, [P, 2, SEQ])
        h = at_kb("h", SCOPE + 2, [P, 3, SEQ])
        h_hi = at_kb("h_hi", SCOPE + 5, [P, 3, SEQ], F32R)
        h_lo = at_kb("h_lo", SCOPE + 8, [P, 3, SEQ], F32R)
        p_in = at_kb("p_in", SCOPE + 11, [P, TT, PLE])
        pT_hi = at_kb("pT_hi", SCOPE + 13, [P, KP, SEQ], F32R)
        pT_lo = at_kb("pT_lo", SCOPE + 15, [P, KP, SEQ], F32R)
        pn = at_kb("pn", SCOPE + 17, [P, TT, D])
        bias = at_kb("bias", SCOPE + 25, [P, D])
        qkT = at_kb("qkT", SCOPE, [P, 10, SEQ])
        val = at_kb("val", SCOPE + 10, [P, TT, 256])
        prob = at_kb("prob", SCOPE + 12, [P, 2, 2048])
        probT = at_kb("probT", SCOPE + 28, [P, 2, 2048])
        sink = at_kb("sink", SCOPE + 44, [P, 16])
        soft = at_kb("soft", SCOPE + 44.5, [P, 6, 32])
        GH = 4
        convT = at_kb("convT", SCOPE, [P, 3 * GH, SEQ])
        knT = at_kb("knT", SCOPE, [P, GH, SEQ])
        qnT = at_kb("qnT", SCOPE + 4, [P, GH, SEQ])
        qdT = at_kb("qdT", SCOPE + 8, [P, GH, SEQ])
        wT = at_kb("wT", SCOPE, [P, TT * GH, P])
        k_tok = at_kb("k_tok", SCOPE + 12, [P, TT, BANK])
        o_tok = at_kb("o_tok", SCOPE + 12, [P, TT, BANK])
        q_tok = at_kb("q_tok", SCOPE + 16, [P, TT, BANK])
        u_tok = at_kb("u_tok", SCOPE + 16, [P, TT, BANK])
        k_dec = at_kb("k_dec", SCOPE + 20, [P, TT, BANK])
        rhs = at_kb("rhs", SCOPE + 24, [P, TT * GH, 2 * P])
        attnT = at_kb("attnT", SCOPE + 32, [P, TT * GH, P])
        lmat = at_kb("lmat", SCOPE + 36, [P, TT * GH, P])
        inv_u = at_kb("inv_u", SCOPE + 40, [P, TT * GH, P])
        inv_t = at_kb("inv_t", SCOPE + 44, [P, TT * GH, P])
        cross = at_kb("cross", SCOPE + 48, [P, TT * GH, P])
        v_new = at_kb("v_new", SCOPE + 48, [P, TT, BANK])
        z_gate = at_kb("z_gate", SCOPE + 52, [P, TT, BANK])
        states = [at_kb("state0", SCOPE + 40, [P, GH, P]), at_kb("state1", SCOPE + 56, [P, GH, P])]
        gs = at_kb("gs", SCOPE + 58, [P, 256])
        o_gain = at_kb("o_gain", SCOPE + 59, [P, P])
        Q_LORA, KV_LORA, ROPE = 384, 256, 64
        KL = (Q_LORA + KV_LORA) // P
        lat = at_kb("lat", 80, [P, TT, Q_LORA + KV_LORA])
        rope_in = at_kb("rope_in", 85, [P, TT, 5, ROPE])
        m_prob = at_kb("m_prob", 80, [P, 12 * P])
        latT_hi = at_kb("latT_hi", 112, [P, KL, SEQ], F32R)
        rope_out = at_kb("rope_out", SCOPE + 40, [P, TT, 8, ROPE])
        m_probT = at_kb("m_probT", 112, [P, 12 * P])
        latT_lo = at_kb("latT_lo", SCOPE + 60, [P, KL, SEQ], F32R)
        rope_tmp = at_kb("rope_tmp", SCOPE + 65, [P, TT, 5, ROPE // 2])
        m_soft = at_kb("m_soft", SCOPE + 66.5, [P, 4, 8])
        q_nopeT = at_kb("q_nopeT", 88, [P, GH, SEQ])
        k_nopeT = at_kb("k_nopeT", 92, [P, GH, SEQ])
        m_val = at_kb("m_val", 96, [P, TT, BANK])
        ropeT = at_kb("ropeT", 100, [P, 4, SEQ])
        y = ctx.enter_context(nc.psum_tensor("y", [P, TT, D], F32))
        q = ctx.enter_context(nc.psum_tensor("q", [P, 4, BANK], F32))
        y_flat = y[:, :, :].rearrange("p t d -> p (t d)")
        q_flat = q[:, :, :].rearrange("p b c -> p (b c)")
        ident = const[:, 0:P]

        slabs = Slabs()

        def view(n, k=None):
            parts, width = slabs.size[n]
            v = raw[0:parts, n % RING, 0:width]
            return v if k is None else v.rearrange("p (k c) -> p k c", k=k)

        def add_rows(w, k, parts=P, c0=0, c1=None):
            c1 = w.shape[1] if c1 is None else c1
            return slabs.add(parts, c1 - c0, [lambda n: (view(n), w[k * P:k * P + parts, c0:c1])])

        def add_cols(w, at):
            wk = w.rearrange("(k p) c -> p k c", p=P)
            pieces, done = [], 0
            for c, m in at:
                pieces.append(lambda n, c=c, m=m, done=done:
                              (view(n, KD)[:, :, done:done + m], wk[:, :, c:c + m]))
                done += m
            return slabs.add(P, KD * P, pieces)

        SWA_H, SWA_KV, HD = 16, 4, 64
        KV0 = SWA_H * HD
        V0 = KV0 + SWA_KV * HD

        def odd_tiles():
            return [[(KV0 + a * P, P)] for a in range(2)] + \
                   [[((8 * a + i) * HD, HD), ((8 * a + 4 + i) * HD, HD)] for a in range(2) for i in range(4)]

        TILE_ORDER = [0, 2, 3, 4, 5, 1, 6, 7, 8, 9]

        def plan_odd():
            w = io["swa_w_qkv"][0]
            wk = w.rearrange("(k p) c -> p k c", p=P)
            for j in range(2):
                slabs.add(P, SLAB, [lambda n, j=j: (view(n, 4), wk[:, 4 * j:4 * j + 4, V0:V0 + 256])])
            for j in TILE_ORDER:
                add_cols(w, odd_tiles()[j])
            for k in range(KD):
                add_rows(io["swa_w_o"][0], k)

        Z0, A0, KV_IN = 1536, 2048, 2048 + 8 + Q_LORA
        W_A, W_KV = 8 + Q_LORA, KV_LORA + ROPE

        def out_block(i):
            return (i + KD // 2) % KD

        def plan_even():
            w = io["ab_w_in"][0]
            wk = w.rearrange("(k p) c -> p k c", p=P)

            def pairs(c0, width):
                for j in range(KD // 2):
                    slabs.add(P, 2 * width, [lambda n, j=j: (view(n, 2), wk[:, 2 * j:2 * j + 2, c0:c0 + width])])

            pairs(A0, W_A)
            pairs(KV_IN, W_KV)
            for c in (512, 0, 1024):
                for hd in range(GH):
                    add_cols(w, [(c + hd * P, P)])
            pairs(Z0, BANK)
            for k in range(Q_LORA // P):
                add_rows(io["mla_w_uq"][0], k)
            for k in range(KV_LORA // P):
                add_rows(io["mla_w_ukv"][0], k)
            for i in range(KD):
                add_rows(io["ab_w_out"][0], out_block(i))

        N_A, N_KV, N_TILE, N_Z, N_UQ, N_UKV, N_OUT = 0, 4, 8, 20, 24, 27, 29

        def ffn_slab(wgu, wd, kind, f):
            if kind == "d":
                return add_rows(wd, f, P if f < FULL else HALF)
            if f == FULL:
                return add_cols(wgu, [(f * P, HALF), (D_FF + f * P, HALF)])
            return add_cols(wgu, [((kind == "u") * D_FF + f * P, P)])

        ffns, toks, slab_at = {}, {}, {}
        y_of, squares_of, gain_of, norm_of = {}, {}, {}, {}
        y_last, xn_base, xT_base, act_base, n_xn, n_xT, n_act = {}, {}, {}, {}, 0, 0, 0

        def together(name):
            return name.startswith("ffn") or name == "mix1"

        n_row_loads = 3 + 6
        n_bias_loads = 4
        for name in phases:
            kind, layer = name[:-1], int(name[-1])
            if kind in ("ffn1_", "ffn2_"):
                wgu, wd = io[kind + "wgu"][layer], io[kind + "wd"][layer]
                seq = [("p", k) for k in range(KP) if kind == "ffn2_"]
                seq += [("g", 0), ("u", 0), ("g", 1), ("u", 1), ("d", 0), ("g", 2), ("u", 2), ("d", 1)]
                for f in range(3, FULL):
                    seq += [("g", f), ("u", f), ("d", f - 1)]
                i = seq.index(("d", FULL - 2))
                seq = seq[:i] + [("g", FULL)] + seq[i:] + [("d", FULL - 1), ("d", FULL)]
                ffns[name] = (len(slabs.load), len(ffns), wgu, wd)
                slab_at[name] = {kf: len(slabs.load) + j for j, kf in enumerate(seq)}
                for kd, f in seq:
                    if kd == "p":
                        add_rows(io["ple_proj"][layer], f)
                    else:
                        ffn_slab(wgu, wd, kd, f)
                if kind == "ffn2_":
                    gain_of["p" + name] = (len(gain_of), "ple_norm", layer)
            elif kind == "mix":
                toks[name] = len(slabs.load)
                plan_odd() if layer else plan_even()
            elif kind == "gate":
                toks[name] = len(slabs.load)
                for k in range(KD):
                    add_rows(io["ple_gate_w"][layer], k)
            y_last[name] = len(slabs.load) - 1
            y_of[name] = len(y_of)
            xn_base[name], xT_base[name], act_base[name] = n_xn, n_xT, n_act
            if together(name):
                n_xn, n_xT, n_act = n_xn + 2, n_xT + KD, n_act + 2
            else:
                n_xn, n_xT = n_xn + 4, n_xT + 2 * KD
            norm_of[name] = len(norm_of)
            if kind != "gate":
                squares_of[name] = len(squares_of)
                gain_of[name] = (len(gain_of), {"ffn1_": "ffn1_post", "ffn2_": "ffn2_post",
                                                "mix": "mix_post"}[kind], layer)
        N = len(slabs.load)

        mains = phases
        norm_col = {"ffn1_": COL_FFN1, "ffn2_": COL_FFN2, "mix": COL_MIX}

        def gain_col(name, k):
            kind, layer = name[:-1], int(name[-1])
            c = COL_ONE + k if kind == "gate" else norm_col[kind] + 8 * layer + k
            return cols[:, c:c + 1]

        loaded = [sem(f"loaded{i}") for i in range(RING)]
        hi_ready, lo_ready, slab_used = sem("hi_ready"), sem("lo_ready"), sem("slab_used")
        x_loaded = [sem("x_loaded0"), sem("x_loaded1")]
        ident_loaded, p_loaded, const_loaded, rows_loaded, bias_loaded = (
            sem(n) for n in ("ident_loaded", "p_loaded", "const_loaded", "rows_loaded", "bias_loaded"))
        rows_clear, bias_clear, ones_set, ones_r_set = (
            sem(n) for n in ("rows_clear", "bias_clear", "ones_set", "ones_r_set"))
        cols_turned, cols_ready = sem("cols_turned"), sem("cols_ready")
        bias_hi_ready, bias_ready = sem("bias_hi_ready"), sem("bias_ready")
        gain_loaded = [sem("gain_loaded0"), sem("gain_loaded1")]
        y_first, y_sq, p_scaled = sem("y_first"), sem("y_sq"), sem("p_scaled")
        x_ready, x_sq, x_rms, xn_ready = sem("x_ready"), sem("x_sq"), sem("x_rms"), sem("xn_ready")
        xn_turned, xT_hi_ready, xT_ready = sem("xn_turned"), sem("xT_hi_ready"), sem("xT_ready")
        p_turned, pT_hi_ready, pT_ready = sem("p_turned"), sem("pT_hi_ready"), sem("pT_ready")
        sil_ready, h_ready, h_hi_ready, h_lo_ready = (
            sem(n) for n in ("sil_ready", "h_ready", "h_hi_ready", "h_lo_ready"))
        gate_ready = sem("gate_ready")
        sinks_loaded, qk_kept, val_kept, scores_ready, max_ready, exp_done, prob_ready, zero_set = (
            sem(n) for n in ("sinks_loaded", "qk_kept", "val_kept", "scores_ready", "max_ready", "exp_done",
                             "prob_ready", "zero_set"))
        prob_turned, probT_act, probT_dve, mixed, mixT_hi_ready, mixT_ready = (
            sem(n) for n in ("prob_turned", "probT_act", "probT_dve", "mixed", "mixT_hi_ready", "mixT_ready"))
        inv_t_first, dve_step, pool_step = sem("inv_t_first"), sem("dve_step"), sem("pool_step")
        xn_act, yg_ready, y_rms, p_sq, p_made, p_kept = sem("xn_act"), sem("yg_ready"), sem("y_rms"), sem("p_sq"), \
            sem("p_made"), sem("p_kept")
        gate_rows, gates_in, lat_sq, lat_rms, lat_ready, rope_key = (
            sem(n) for n in ("gate_rows", "gates_in", "lat_sq", "lat_rms", "lat_ready", "rope_key"))
        gates_raw, gates_exp, gates_set, conv_first, conv_done, conv_ready = (
            sem(n) for n in ("gates_raw", "gates_exp", "gates_set", "conv_first", "conv_done",
                             "conv_ready"))
        lat_turned, latT_hi_ready, latT_ready = sem("lat_turned"), sem("latT_hi_ready"), sem("latT_ready")
        sums_ready, sums_kept, dec_args, dec_ready, wide_sums, decay_args, grown, decay_ready = (
            sem(n) for n in ("sums_ready", "sums_kept", "dec_args", "dec_ready", "wide_sums", "decay_args",
                             "grown", "decay_ready"))
        z_in, z_ready, qn_made, q_nope_kept, rope_kept, kn_made, k_nope_kept, m_val_kept = (
            sem(n) for n in ("z_in", "z_ready", "qn_made", "q_nope_kept", "rope_kept", "kn_made", "k_nope_kept",
                             "m_val_kept"))
        rope_ready, rope_turned, ropeT_kept, m_scores, m_max, m_exp, m_prob_ready, m_turned, m_probT_act, \
            m_probT_dve, m_mixed = (sem(n) for n in (
                "rope_ready", "rope_turned", "ropeT_kept", "m_scores", "m_max", "m_exp", "m_prob_ready",
                "m_turned", "m_probT_act", "m_probT_dve", "m_mixed"))
        tok_turned, tok_sq, tok_ready, back_turned, back_kept, qd_ready = (
            sem(n) for n in ("tok_turned", "tok_sq", "tok_ready", "back_turned", "back_kept", "qd_ready"))
        rhs_ready, grams, l_ready, cross_made, cross_ready, inv_made, inv_ready = (
            sem(n) for n in ("rhs_ready", "grams", "l_ready", "cross_made", "cross_ready", "inv_made", "inv_ready"))
        solved, solved_kept, read_out, v_new_ready, kv_made, state_ready, o_made, o_sq, o_ready, o_turned = (
            sem(n) for n in ("solved", "solved_kept", "read_out", "v_new_ready", "kv_made", "state_ready",
                             "o_made", "o_sq", "o_ready", "o_turned"))
        emix_hi, emix_ready = sem("emix_hi"), sem("emix_ready")
        stored = sem("stored")

        def conv_col(j):
            return (GH, 0, 2 * GH)[j // GH] + j % GH

        def lat_bank(k):
            t, c = ((0, BANK), (0, BANK + SEQ), (1, BANK), (1, BANK + SEQ), (0, 0))[k]
            return y[:, t, c:c + SEQ]

        M_SCALE = 192 ** -0.5

        def m_scores_of(t):
            w = (t + 1) * P
            return y[:, t, 0:GH * w].rearrange("p (h k) -> p h k", h=GH)

        def m_prob_of(t):
            w = (t + 1) * P
            return m_prob[:, t * GH * P:t * GH * P + GH * w].rearrange("p (h k) -> p h k", h=GH)

        def k_dec_free(t):
            return inv_t[:, 4 * t:4 * t + 4, :].rearrange("p h c -> p (h c)")

        BATCHES = [(1, 0, 8, y_flat, 64, 256), (0, 0, 8, q_flat[:, 0:1024], 0, 128),
                   (0, 8, 8, q_flat[:, 1024:2048], 0, 128), (1, 8, 8, y_flat, 64, 256)]
        TURNED = [0, 2, 3, 4]

        def scores_of(b):
            t, h0, heads, place, key0, wide = BATCHES[b]
            return place[:, 0:heads * wide].rearrange("p (h k) -> p h k", h=heads)[:, :, key0:wide]

        def batch_place(v, b):
            return (v[:, 0, :], v[:, 1, 0:1024], v[:, 1, 1024:2048], v[:, 0, :])[b]

        def prob_of(b):
            t, h0, heads, place, key0, wide = BATCHES[b]
            return batch_place(prob, b).rearrange("p (h k) -> p h k", h=heads)[:, :, key0:wide]

        def soft_of(b, row):
            t, h0, heads, place, key0, wide = BATCHES[b]
            s0 = 16 * t + h0
            return soft[:, row, s0:s0 + heads]

        MIXED = [(0, 2, slice(0, 4), 1), (1, 0, slice(0, 4), 0), (2, 1, slice(4, 8), 0), (3, 3, slice(4, 8), 1)]

        def at(i, base, step):
            return base if i is None else i * step + base

        LOOP0, LOOP1 = 3, 19
        TURNS = (LOOP1 - LOOP0) // 2

        def slab_of(name, kind, f):
            return slab_at[name][kind, f]

        def slot(f):
            return f % 2 if f < FULL else 2

        def extra(name):
            return KP if name.startswith("ffn2_") else 0

        block = ctx.enter_context(nc.Block())

        def newton(v, link, to, half, scratch, wide, done, by=1):
            for s in range(3):
                if wide:
                    link(v.tensor_tensor(scratch, to, to, ALU.mult))
                    link(v.tensor_tensor(scratch, scratch, half, ALU.mult))
                    last = v.scalar_tensor_tensor(to, scratch, 1.5, to, ALU.add, ALU.mult)
                else:
                    link(v.tensor_scalar(scratch, to, half, to, ALU.mult, ALU.mult))
                    last = v.tensor_scalar(to, scratch, 1.5, to, ALU.add, ALU.mult)
                if s < 2 or done is None:
                    link(last)
                else:
                    last.then_inc(done, by)

        def first_sum(v, link, a, at_):
            half = st[:, at_:at_ + 1]
            link(v.tensor_scalar(half, a, -0.5 / D, -0.5 * EPS, ALU.mult, ALU.add))

        def inv_rms(v, link, to, b, at_, done=None):
            half, scratch = (st[:, at_ + i:at_ + i + 1] for i in range(2))
            if b is not None:
                link(v.tensor_scalar(half, b, -0.5 / D, half, ALU.mult, ALU.add))
            link(v.tensor_scalar(to.bitcast(I32), half.bitcast(I32), -0.5, RSQRT_MAGIC - 2.0 ** 22 - 2.0 ** 30,
                                 ALU.mult, ALU.add))
            newton(v, link, to, half, scratch, False, done)

        def half_of(h_):
            return slice(h_ * BANK, (h_ + 1) * BANK)

        def turned_whole(name, k):
            place = y_flat if extra(name) else q_flat
            return place[:, k * SEQ:(k + 1) * SEQ]

        def turned_at(t, k):
            c = (k % 2) * P
            if k < 4:
                return y[:, t, (k // 2) * BANK + c:(k // 2) * BANK + c + P]
            return q[:, 2 + (k - 4) // 2, c:c + P]

        def ffn_order(name, engine, ahead, tile, tile_more, embeddings):
            number = ffns[name][1]
            at_ = slab_at[name]

            def unit(f, i=None, down=True):
                n = at_["g", f]
                ahead(n, i)
                ahead(n + 1, i)
                tile(name, number, f, i)
                if down:
                    ahead(n + 2, i)
                tile_more(name, number, f, i)

            if extra(name):
                ahead(at_["p", 0])
                ahead(at_["p", 1])
            unit(0, down=False)
            if extra(name):
                embeddings(name)
            unit(1, down=False)
            ahead(at_["d", 0])
            unit(2)
            with engine.Fori(0, TURNS) as i:
                unit(LOOP0, i)
                unit(LOOP0 + 1, i)
            unit(LOOP1)
            f = FULL - 1
            ahead(at_["g", f])
            ahead(at_["u", f])
            tile(name, number, f)
            ahead(at_["g", FULL])
            tile_more(name, number, f)
            tile(name, number, FULL)
            ahead(at_["d", f - 1])
            tile_more(name, number, FULL)
            ahead(at_["d", f])
            ahead(at_["d", FULL])

        @block.sync
        def _(sp):
            for t in range(TT):
                sp.dma_start(x[:, t, :], io["x"][0, t * P:(t + 1) * P, :]).then_inc(x_loaded[t], 16)
            sp.dma_start(ident, io["const"][:, 0:P]).then_inc(ident_loaded, 16)

            def load_rows():
                sp.wait_ge(rows_clear, 1)
                for c, name in ((COL_FFN1, "ffn1_pre"), (COL_MIX, "mix_pre"), (COL_FFN2, "ffn2_pre")):
                    sp.dma_start(rows[c:c + 2 * KD, :], io[name].rearrange("l (k p) -> (l k) p", p=P)) \
                        .then_inc(rows_loaded, 16)
                for row, name in ((COL_QN, "mla_q_norm"), (COL_KVN, "mla_kv_norm")):
                    v = io[name][0].rearrange("(k p) -> k p", p=P)
                    sp.dma_start(rows[row:row + v.shape[0], :], v).then_inc(rows_loaded, 16)
                sp.dma_start(rows[COL_CONV:COL_CONV + 48, :], io["gdn_conv"][0].rearrange("j (c p) -> (j c) p", p=P)) \
                    .then_inc(rows_loaded, 16)
                b_qkv = io["swa_b_qkv"]
                q_bias = b_qkv[0, 0:KV0].rearrange("(a b r) -> b a r", a=2, b=2)
                for b in range(2):
                    sp.dma_start(rows[COL_BQK + 2:COL_BQK + 10, b * HD:(b + 1) * HD],
                                 q_bias[b].rearrange("a (i d) -> a i d", d=HD)).then_inc(rows_loaded, 16)
                sp.dma_start(rows[COL_BQK:COL_BQK + 2, :], b_qkv[0, KV0:V0].rearrange("(k p) -> k p", p=P)) \
                    .then_inc(rows_loaded, 16)

            def load(n):
                if n >= RING:
                    sp.wait_ge(lo_ready, n - RING + 1)
                for piece in slabs.load[n]:
                    dst, src = piece(n)
                    sp.dma_start(dst, src).then_inc(loaded[n % RING], 16)

            def load_ffn(name, base, wgu, wd):
                for n in range(base, slab_of(name, "g", LOOP0)):
                    load(n)
                    if n == 1:
                        load_rows()
                    if n == RING - 1:
                        sp.dma_start(const[:, P:], io["const"][:, P:]).then_inc(const_loaded, 16)
                wk = wgu.rearrange("(k p) c -> p k c", p=P)
                with sp.Fori(0, TURNS) as i:
                    for j in range(2):
                        n = slab_of(name, "g", LOOP0 + j)
                        f = LOOP0 + j
                        for m, (c0, stride) in enumerate([(f * P, 2 * P), (D_FF + f * P, 2 * P)]):
                            src = wk[:, :, bass.ds(i * stride + c0, P)]
                            sp.wait_ge(lo_ready, i * 6 + (n + m - RING + 1))
                            sp.dma_start(view(n + m, KD), src).then_inc(loaded[(n + m) % RING], 16)
                        src = wd[bass.ds(i * (2 * P) + (f - 1) * P, P), :]
                        sp.wait_ge(lo_ready, i * 6 + (n + 2 - RING + 1))
                        sp.dma_start(view(n + 2), src).then_inc(loaded[(n + 2) % RING], 16)
                for n in range(slab_of(name, "g", LOOP1), base + 65 + extra(name)):
                    load(n)

            n = 0
            while n < N:
                hit = [(name, v) for name, v in ffns.items() if v[0] == n]
                if hit:
                    name, (base, _, wgu, wd) = hit[0]
                    load_ffn(name, base, wgu, wd)
                    n += 65 + extra(name)
                else:
                    load(n)
                    n += 1
            for t in range(TT):
                for half in range(2):
                    c = slice(half * BANK, (half + 1) * BANK)
                    sp.wait_ge(x_ready, 4 * (len(mains) - 1) + 2 * t + half + 1)
                    sp.dma_start(out[0, t * P:(t + 1) * P, c], x[:, t, c]).then_inc(stored, 16)
            sp.wait_ge(stored, 64)

        @block.gpsimd
        def _(pool):
            uses = list(gain_of)
            steps = [0]

            def link(ins):
                steps[0] += 1
                ins.then_inc(pool_step, 1)
                pool.wait_ge(pool_step, steps[0])

            def load_gain(u):
                _, name, layer = gain_of[uses[u]]
                pool.dma_start(gain[:, u % 2, :], io[name][layer:layer + 1, :].to_broadcast([P, D])) \
                    .then_inc(gain_loaded[u % 2], 16)

            def load_gain_after(use):
                u = gain_of[use][0] + 2
                if u < len(uses):
                    load_gain(u)

            def start_mix0():
                for c, src in ((128, "gdn_dt_bias"), (132, "gdn_a_log")):
                    pool.dma_start(gs[:, c:c + 4], io[src].to_broadcast([P, 4])).then_inc(gate_rows, 16)
                pool.dma_start(o_gain[:, :], io["gdn_out_norm"].to_broadcast([P, P])).then_inc(gate_rows, 16)
                pool.wait_ge(gate_rows, 48)
                pool.wait_ge(z_in, 1)
                v = z_gate[:, :, :].rearrange("p t (h c) -> p (t h) c", c=P)
                pool.tensor_tensor(v, v, o_gain[:, :].unsqueeze(1).to_broadcast([P, TT * GH, P]), ALU.mult) \
                    .then_inc(z_ready, 1)

                pool.wait_ge(l_ready, 1)
                pool.wait_ge(rope_turned, 1)
                pairs, eye = (const[:, C_AT[m]:C_AT[m] + P].unsqueeze(1).to_broadcast([P, TT * GH, P])
                              for m in ("pairs", "ident"))
                link(pool.tensor_tensor(inv_t[:, :, :], lmat[:, :, :], pairs, ALU.mult))
                pool.tensor_tensor(inv_t[:, :, :], inv_t[:, :, :], eye, ALU.add).then_inc(inv_t_first, 1)

            def start_mix1():
                pool.dma_start(sink[:, :], io["swa_sinks"].to_broadcast([P, SWA_H])).then_inc(sinks_loaded, 16)
                v = prob[:, 0, :].rearrange("p (h k) -> p h k", h=8)[:, :, 0:CHUNK]
                pool.memset(v, 0.0).then_inc(zero_set, 1)

            load_gain(0)
            for j, name in enumerate(mains):
                b = norm_of[name]
                if j and not mains[j - 1].startswith("gate"):
                    pool.wait_ge(y_sq, 3 * squares_of[mains[j - 1]] + 3)
                    first_sum(nc.gpsimd, link, st[:, 2:3], 48)
                    inv_rms(nc.gpsimd, link, st[:, 9:10], None, 48, done=y_rms)
                if together(name):
                    pool.wait_ge(x_sq, 4 * b + 1)
                    first_sum(nc.gpsimd, link, st[:, 4:5], 52)
                    pool.wait_ge(x_sq, 4 * b + 2)
                    inv_rms(nc.gpsimd, link, st[:, 10:11], st[:, 5:6], 52, done=x_rms)
                if j == 0:
                    if len(uses) > 1:
                        load_gain(1)
                    pool.wait_ge(bias_clear, 1)
                    for l in range(2):
                        pool.dma_start(bias[32 * l:32 * l + 1, :], io["ple_gate_b"][l:l + 1, :]) \
                            .then_inc(bias_loaded, 16)
                    pool.dma_start(bias[64:65, :], io["swa_b_o"]).then_inc(bias_loaded, 16)
                    pool.dma_start(bias[96:97, 0:256], io["swa_b_qkv"][0:1, V0:]).then_inc(bias_loaded, 16)
                if j:
                    pool.wait_ge(x_ready, 4 * b)
                    if mains[j - 1] in gain_of:
                        load_gain_after(mains[j - 1])
                if name == "mix0":
                    start_mix0()
                if name == "mix1":
                    start_mix1()
                if name.startswith("mix"):
                    l = int(name[-1])
                    if l:
                        pool.wait_ge(mixed, len(BATCHES))
                    else:
                        pool.wait_ge(o_turned, 1)
                    pool.dma_start(p_in[:, :, :], io["p"][l, 0].rearrange("(t p) c -> p t c", p=P)) \
                        .then_inc(p_loaded, 16)
                if name.startswith("ffn2_"):
                    pool.wait_ge(p_scaled, TT * (int(name[-1]) + 1))
                    load_gain_after("p" + name)
            if not mains[-1].startswith("gate"):
                pool.wait_ge(y_sq, 3 * squares_of[mains[-1]] + 3)
                first_sum(nc.gpsimd, link, st[:, 2:3], 48)
                inv_rms(nc.gpsimd, link, st[:, 9:10], None, 48, done=y_rms)

        @block.scalar
        def _(act):
            def split_hi(m, i=None):
                parts, width = slabs.size[m]
                act.wait_ge(loaded[m % RING], at(i, slabs.loaded[m], 16))
                if m >= RING:
                    act.wait_ge(slab_used, at(i, m - RING + 1, 6))
                nc.scalar.activation(hi[0:parts, m % RING, 0:width], raw[0:parts, m % RING, 0:width],
                                     ACT.Copy).then_inc(hi_ready, 1)

            def ahead(n, i=None):
                if n + AHEAD < N:
                    split_hi(n + AHEAD, i)

            def wait_y(name, t):
                if t == 0:
                    act.wait_ge(y_first, y_of[name] + 1)
                else:
                    act.wait_ge(slab_used, y_last[name] + 1)

            def square(to, of, c):
                return nc.scalar.activation(to, of, ACT.Square, accum_out=st[:, c:c + 1])

            def squares_y(name, t):
                wait_y(name, t)
                if t == 0:
                    square(xn[:, 0, half_of(0)], y[:, 0, half_of(0)], 0).then_inc(y_sq, 1)
                    act.wait_ge(yg_ready, squares_of[name] + 1)
                    square(xn[:, 0, half_of(1)], y[:, 0, half_of(1)], 1).then_inc(y_sq, 1)
                else:
                    square(xn[:, 1, :], y[:, 1, :], 2).then_inc(y_sq, 1)

            def squares_x(b, t):
                for j in range(2):
                    if b == 0:
                        act.wait_ge(x_loaded[t], 16)
                    else:
                        act.wait_ge(x_ready, 4 * (b - 1) + 2 * t + j + 1)
                    square(xn[:, t, half_of(j)], x[:, t, half_of(j)], 4 + 2 * t + j).then_inc(x_sq, 1)

            def turned(name, t):
                for k in range(KD):
                    act.wait_ge(xn_turned, xT_base[name] // 2 + 4 * t + k // 2 + 1)
                    nc.scalar.activation(xT_hi[:, k, t * P:(t + 1) * P], turned_at(t, k), ACT.Copy,
                                         scale=gain_col(name, k)).then_inc(xT_hi_ready, 1)

            def turned_all(name):
                for k in range(KD):
                    act.wait_ge(xn_turned, (xT_base[name] + k) // 2 + 1)
                    nc.scalar.activation(xT_hi[:, k, :], turned_whole(name, k), ACT.Copy, scale=gain_col(name, k)) \
                        .then_inc(xT_hi_ready, 1)

            def normed_x(name):
                act.wait_ge(x_rms, act_base[name] // 2 + 1)
                for j in range(2):
                    nc.scalar.activation(xn[:, 0, half_of(j)], x[:, 0, half_of(j)], ACT.Copy,
                                         scale=st[:, 10:11]).then_inc(xn_act, 1)

            def boundary(before, name):
                if before and not before.startswith("gate"):
                    squares_y(before, 0)
                    squares_y(before, 1)
                if name is None:
                    return
                b = norm_of[name]
                squares_x(b, 0)
                if extra(name):
                    act.wait_ge(p_made, int(name[-1]) + 1)
                    square(pn[:, 1, :], q_flat[:, 0:D], 12).then_inc(p_sq, 1)
                    nc.scalar.activation(pn[:, 0, :], q_flat[:, 0:D], ACT.Copy).then_inc(p_kept, 1)
                if together(name):
                    squares_x(b, 1)
                    normed_x(name)
                    turned_all(name)
                else:
                    turned(name, 0)
                    squares_x(b, 1)
                    turned(name, 1)

            def tile(name, number, f, i=None):
                n, F = slab_of(name, "g", f), TILES * number + f
                m = P if f < FULL else HALF
                act.wait_ge(slab_used, at(i, n + (2 if f < FULL else 1), 6))
                if F >= 2:
                    act.wait_ge(h_ready, at(i, F - 1, 2))
                nc.scalar.activation(sil[0:m, f % 2, :], q[0:m, f % 2, 0:SEQ], ACT.Silu).then_inc(sil_ready, 1)

            def tile_hi(name, number, f, i=None):
                F, m = TILES * number + f, P if f < FULL else HALF
                act.wait_ge(h_ready, at(i, F + 1, 2))
                if 2 <= f < FULL:
                    act.wait_ge(slab_used, at(i, slab_of(name, "d", f - 2) + 1, 6))
                nc.scalar.activation(h_hi[0:m, slot(f), :], h[0:m, slot(f), :], ACT.Copy).then_inc(h_hi_ready, 1)

            def ffn(name):
                ffn_order(name, act, ahead, tile, tile_hi, embeddings)

            def embeddings_turned(l):
                act.wait_ge(p_turned, l + 1)
                nc.scalar.activation(pT_hi[:, :, :], q[:, 2, :].rearrange("p (k c) -> p k c", k=KP), ACT.Copy) \
                    .then_inc(pT_hi_ready, 1)

            def embeddings(name):
                act.wait_ge(slab_used, slab_of(name, "p", KP - 1) + 1)
                square(xn[:, 1, :], q_flat[:, D:2 * D], 13).then_inc(p_sq, 1)

            def gate(name):
                for k in range(KD):
                    ahead(toks[name] + k)
                for t in range(TT):
                    wait_y(name, t)
                    for j in range(2):
                        nc.scalar.activation(xn[:, t, half_of(j)], y[:, t, half_of(j)], ACT.Tanh, scale=0.5) \
                            .then_inc(gate_ready, 1)

            def mixed_hi(piece):
                b, bank, blocks, t = MIXED[piece]
                act.wait_ge(mixed, b + 1)
                nc.scalar.activation(xT_hi[:, blocks, t * P:(t + 1) * P],
                                     q[:, bank, :].rearrange("p (m c) -> p m c", m=4), ACT.Copy) \
                    .then_inc(mixT_hi_ready, 1)

            def odd(name):
                n0 = toks[name]

                def exps(b):
                    act.wait_ge(max_ready, b + 1)
                    for j in range(BATCHES[b][2]):
                        nc.scalar.activation(prob_of(b)[:, j, :], scores_of(b)[:, j, :], ACT.Exp,
                                             bias=soft_of(b, 2)[:, j:j + 1], scale=HD ** -0.5,
                                             accum_out=soft_of(b, 3)[:, j:j + 1])
                    nc.scalar.activation(soft_of(b, 4), soft_of(b, 1), ACT.Exp).then_inc(exp_done, 1)

                def keep_turned(b):
                    act.wait_ge(prob_turned, TURNED[b] + 1)
                    nc.scalar.activation(batch_place(probT, b)[:, 0:1024], BATCHES[b][3][:, 0:1024], ACT.Copy) \
                        .then_inc(probT_act, 1)

                ahead(n0)
                ahead(n0 + 1)
                act.wait_ge(slab_used, n0 + 2)
                nc.scalar.activation(val[:, :, :], y[:, :, 0:256], ACT.Copy).then_inc(val_kept, 1)
                for p, j in enumerate(TILE_ORDER):
                    ahead(n0 + 2 + p)
                    act.wait_ge(slab_used, n0 + 2 + p + 1)
                    nc.scalar.activation(qkT[:, j, :], q[:, p % 4, 0:SEQ], ACT.Identity,
                                         bias=cols[:, COL_BQK + j:COL_BQK + j + 1]).then_inc(qk_kept, 1)
                    if p == 6:
                        exps(0)
                keep_turned(0)
                exps(1)
                exps(2)
                keep_turned(1)
                keep_turned(2)
                exps(3)
                for piece in range(3):
                    mixed_hi(piece)
                keep_turned(3)
                ahead(n0 + 12)
                mixed_hi(3)
                for k in range(1, KD):
                    if k == 6:
                        embeddings_turned(1)
                    ahead(n0 + 12 + k)

            def even(name):
                n0 = toks[name]

                def used(n):
                    act.wait_ge(slab_used, n0 + n)

                def latents_turned():
                    for k in range(KL):
                        act.wait_ge(lat_turned, k // 2 + 1)
                        nc.scalar.activation(latT_hi[:, k, :], lat_bank(k), ACT.Copy,
                                             scale=cols[:, COL_QN + k:COL_QN + k + 1]).then_inc(latT_hi_ready, 1)
                    act.wait_ge(sums_ready, 1)
                    nc.scalar.activation(gs[:, 64:96], y[:, 1, 0:32], ACT.Copy).then_inc(sums_kept, 1)

                def back(s_):
                    act.wait_ge(back_turned, s_ + 1)
                    nc.scalar.activation((knT, qnT)[s_][:, :, :].rearrange("p h c -> p (h c)"),
                                         q_flat[:, s_ * 1024:(s_ + 1) * 1024], ACT.Copy).then_inc(back_kept, 1)

                for n in range(N_TILE):
                    ahead(n0 + n)
                used(N_TILE)
                for t in range(TT):
                    nc.scalar.activation(lat[:, t, 0:Q_LORA], y[:, t, 8:W_A], ACT.Square,
                                         accum_out=st[:, 64 + t:65 + t])
                    ins = nc.scalar.activation(lat[:, t, Q_LORA:], y[:, t, BANK:BANK + KV_LORA], ACT.Square,
                                               accum_out=st[:, 66 + t:67 + t])
                ins.then_inc(lat_sq, 1)
                act.wait_ge(gate_rows, 48)
                nc.scalar.activation(gs[:, 0:16].rearrange("p (t c) -> p t c", t=TT), y[:, :, 0:8], ACT.Copy) \
                    .then_inc(gates_in, 1)
                nc.scalar.activation(rope_in[:, :, 4, :], y[:, :, BANK + KV_LORA:BANK + W_KV], ACT.Copy) \
                    .then_inc(rope_key, 1)
                act.wait_ge(gates_raw, 1)
                nc.scalar.activation(gs[:, 32:40], gs[:, 24:32], ACT.Exp, scale=-1.0).then_inc(gates_exp, 1)
                nc.scalar.activation(gs[:, 136:140], gs[:, 132:136], ACT.Exp)
                act.wait_ge(gates_in, 1)
                nc.scalar.activation(gs[:, 48:56].rearrange("p (t c) -> p t c", t=TT),
                                     gs[:, 0:16].rearrange("p (t c) -> p t c", t=TT)[:, :, 4:8], ACT.Exp, scale=-1.0)
                act.wait_ge(gates_exp, 1)
                nc.scalar.activation(gs[:, 40:48], gs[:, 32:40], ACT.Ln, bias=1.0).then_inc(gates_exp, 1)
                act.wait_ge(lat_rms, 1)
                for t in range(TT):
                    nc.scalar.activation(lat[:, t, 0:Q_LORA], y[:, t, 8:W_A], ACT.Copy, scale=st[:, 68 + t:69 + t])
                    ins = nc.scalar.activation(lat[:, t, Q_LORA:], y[:, t, BANK:BANK + KV_LORA], ACT.Copy,
                                               scale=st[:, 70 + t:71 + t])
                ins.then_inc(lat_ready, 1)
                for j in range(3 * GH):
                    ahead(n0 + N_TILE + j)
                    if j == GH:
                        latents_turned()
                    used(N_TILE + j + 1)
                    c = COL_CONV + 36 + conv_col(j)
                    nc.scalar.activation(convT[:, j, :], q[:, j % 4, 0:SEQ], ACT.Copy, scale=cols[:, c:c + 1]) \
                        .then_inc(conv_first, 1)
                    if j:
                        act.wait_ge(conv_done, j)
                        nc.scalar.activation(convT[:, j - 1, :], convT[:, j - 1, :], ACT.Silu).then_inc(conv_ready, 1)
                act.wait_ge(conv_done, 3 * GH)
                nc.scalar.activation(convT[:, 3 * GH - 1, :], convT[:, 3 * GH - 1, :], ACT.Silu) \
                    .then_inc(conv_ready, 1)
                act.wait_ge(wide_sums, 1)
                nc.scalar.activation(cross[:, :, :].rearrange("p m c -> p (m c)"), y[:, 0, :], ACT.Exp) \
                    .then_inc(grown, 1)
                act.wait_ge(dec_args, 1)
                nc.scalar.activation(gs[:, 96:128], gs[:, 160:192], ACT.Exp).then_inc(dec_ready, 1)
                ahead(n0 + N_Z)
                ahead(n0 + N_Z + 1)
                for s_, place in ((0, inv_t), (1, inv_u)):
                    for t in range(TT):
                        act.wait_ge(tok_turned, 2 * s_ + t + 1)
                        nc.scalar.activation(place[:, 4 * t:4 * t + 4, :].rearrange("p h c -> p (h c)"),
                                             q[:, 2 * (1 - s_) + t, :], ACT.Square).then_inc(tok_sq, 1)
                ahead(n0 + N_Z + 2)
                used(N_UQ)
                nc.scalar.activation(z_gate[:, :, :].rearrange("p t c -> p (t c)"), y[:, 1, :], ACT.Silu) \
                    .then_inc(z_in, 1)
                ahead(n0 + N_Z + 3)
                act.wait_ge(decay_args, 1)
                for m in range(TT * GH):
                    nc.scalar.activation(attnT[:, m, :], attnT[:, m, :], ACT.Exp, bias=gs[:, 192 + m:193 + m])
                    nc.scalar.activation(lmat[:, m, :], lmat[:, m, :], ACT.Exp, bias=gs[:, 64 + m:65 + m],
                                         scale=-1.0).then_inc(decay_ready, 1)
                ahead(n0 + N_UQ)
                act.wait_ge(qn_made, 1)
                nc.scalar.activation(q_nopeT[:, :, :].rearrange("p h c -> p (h c)"), y[:, 0, :], ACT.Copy) \
                    .then_inc(q_nope_kept, 1)
                used(N_UKV)
                nc.scalar.activation(rope_in[:, :, 0:4, :].rearrange("p t h c -> p t (h c)"),
                                     y[:, 1, 0:BANK].rearrange("p (t c) -> p t c", t=TT), ACT.Copy) \
                    .then_inc(rope_kept, 1)
                back(0)
                ahead(n0 + N_UQ + 1)
                ahead(n0 + N_UQ + 2)
                act.wait_ge(kn_made, 1)
                nc.scalar.activation(k_nopeT[:, :, :].rearrange("p h c -> p (h c)"), y[:, 0, :], ACT.Copy) \
                    .then_inc(k_nope_kept, 1)
                back(1)
                used(N_OUT)
                nc.scalar.activation(m_val[:, :, :].rearrange("p t c -> p (t c)"), y[:, 1, :], ACT.Copy) \
                    .then_inc(m_val_kept, 1)
                act.wait_ge(rope_turned, 1)
                nc.scalar.activation(ropeT[:, :, :].rearrange("p r c -> p (r c)"), y[:, 0, :], ACT.Copy) \
                    .then_inc(ropeT_kept, 1)
                for n in range(2):
                    ahead(n0 + N_UKV + n)
                for t in range(TT):
                    act.wait_ge(m_max, t + 1)
                    for hd in range(GH):
                        ins = nc.scalar.activation(m_prob_of(t)[:, hd, :], m_scores_of(t)[:, hd, :], ACT.Exp,
                                                   bias=m_soft[:, 1, 4 * t + hd:4 * t + hd + 1], scale=M_SCALE,
                                                   accum_out=m_soft[:, 2, 4 * t + hd:4 * t + hd + 1])
                    ins.then_inc(m_exp, 1)
                act.wait_ge(solved, 1)
                nc.scalar.activation(u_tok[:, :, :].rearrange("p t c -> p (t c)"), q_flat[:, 0:1024], ACT.Copy) \
                    .then_inc(solved_kept, 1)
                act.wait_ge(solved, 2)
                nc.scalar.activation(wT[:, :, :].rearrange("p m c -> p (m c)"), q_flat[:, 1024:2048], ACT.Copy) \
                    .then_inc(solved_kept, 1)
                for t in range(TT):
                    act.wait_ge(m_turned, t + 1)
                    nc.scalar.activation(m_probT[:, t * BANK:(t + 1) * BANK], y[:, t, 0:BANK], ACT.Copy) \
                        .then_inc(m_probT_act, 1)
                act.wait_ge(m_mixed, 1)
                for j in range(2):
                    nc.scalar.activation(xT_hi[:, 4 + 2 * j:6 + 2 * j, :].rearrange("p m c -> p (m c)"),
                                         y[:, 0, j * BANK:(j + 1) * BANK], ACT.Copy).then_inc(emix_hi, 1)
                ahead(n0 + N_OUT)
                ahead(n0 + N_OUT + 1)
                ahead(n0 + N_OUT + 2)
                for t in range(TT):
                    act.wait_ge(o_made, t + 1)
                    nc.scalar.activation(k_dec_free(t), q[:, 1 + 2 * t, :], ACT.Square).then_inc(o_sq, 1)
                ahead(n0 + N_OUT + 3)
                ahead(n0 + N_OUT + 4)
                act.wait_ge(o_turned, 1)
                for j in range(2):
                    nc.scalar.activation(xT_hi[:, 2 * j:2 * j + 2, :].rearrange("p m c -> p (m c)"), q[:, j, :],
                                         ACT.Copy).then_inc(emix_hi, 1)
                ahead(n0 + N_OUT + 5)
                embeddings_turned(0)
                for k in range(6, KD):
                    ahead(n0 + N_OUT + k)

            squares_x(0, 0)
            squares_x(0, 1)
            split_hi(0)
            normed_x(mains[0])
            split_hi(1)
            act.wait_ge(cols_turned, 1)
            nc.scalar.activation(cols[:, :], q[:, 3, 0:P], ACT.Copy).then_inc(cols_ready, 1)
            act.wait_ge(cols_ready, 1)
            turned_all(mains[0])
            for n in range(2, AHEAD):
                split_hi(n)
            act.wait_ge(bias_loaded, 16 * n_bias_loads)
            nc.scalar.activation(bias_hi[:, :], bias[:, :], ACT.Copy).then_inc(bias_hi_ready, 1)
            act.wait_ge(ones_set, 1)
            nc.scalar.activation(ones_r[:, :], ones[:, :], ACT.Copy).then_inc(ones_r_set, 1)
            for j, name in enumerate(mains):
                if j:
                    boundary(mains[j - 1], name)
                if name.startswith("ffn"):
                    ffn(name)
                elif name.startswith("gate"):
                    gate(name)
                elif name == "mix1":
                    odd(name)
                elif name == "mix0":
                    even(name)
            boundary(mains[-1], None)

        @block.vector
        def _(dve):
            steps = [0]

            def link(ins):
                steps[0] += 1
                ins.then_inc(dve_step, 1)
                dve.wait_ge(dve_step, steps[0])

            def rsqrt(to, ms, half, scratch, wide, done, by=1):
                link(nc.vector.tensor_scalar(to.bitcast(I32), ms.bitcast(I32), -0.5, RSQRT_MAGIC,
                                             ALU.mult, ALU.add))
                newton(nc.vector, link, to, half, scratch, wide, done, by)

            def mean_rsqrt(to, ss, n, done=None, wide=False, at_=32):
                w = ss.shape[1]
                ms, half, scratch = (st[:, at_ + w * i:at_ + w * (i + 1)] for i in range(3))
                link(nc.vector.tensor_scalar(half, ss, -0.5 / n, -0.5 * EPS, ALU.mult, ALU.add))
                link(nc.vector.tensor_scalar(ms, ss, 1.0 / n, EPS, ALU.mult, ALU.add))
                rsqrt(to, ms, half, scratch, wide, done)

            def split_lo(m, i=None):
                parts, width = slabs.size[m]
                dve.wait_ge(hi_ready, at(i, m + 1, 6))
                nc.vector.tensor_tensor(lo[0:parts, m % RING, 0:width], raw[0:parts, m % RING, 0:width],
                                        hi[0:parts, m % RING, 0:width].bitcast(F32), ALU.subtract) \
                    .then_inc(lo_ready, 1)

            def ahead(n, i=None):
                if n + AHEAD < N:
                    split_lo(n + AHEAD, i)

            def gained(name, t, half, c):
                u = gain_of[name][0]
                return nc.vector.scalar_tensor_tensor(tmp[:, t, half_of(half)], y[:, t, half_of(half)], c,
                                                      gain[:, u % 2, half_of(half)], ALU.mult, ALU.mult)

            def add_scaled(t):
                for j in range(2):
                    c = half_of(j)
                    nc.vector.scalar_tensor_tensor(x[:, t, c], tmp[:, t, c], st[:, 8 + t:9 + t], x[:, t, c],
                                                   ALU.mult, ALU.add).then_inc(x_ready, 1)

            def add_gated(name, t):
                l = int(name[-1])
                for j in range(2):
                    c = half_of(j)
                    dve.wait_ge(gate_ready, 4 * l + 2 * t + j + 1)
                    link(nc.vector.scalar_tensor_tensor(tmp[:, t, c], xn[:, t, c], 1.0, pn[:, t, c],
                                                        ALU.add, ALU.mult))
                    nc.vector.tensor_tensor(x[:, t, c], tmp[:, t, c], x[:, t, c], ALU.add).then_inc(x_ready, 1)

            def normed_x(b, t):
                c = 4 + 2 * t
                dve.wait_ge(x_sq, 4 * b + 2 * t + 1)
                first_sum(nc.vector, link, st[:, c:c + 1], 32)
                dve.wait_ge(x_sq, 4 * b + 2 * t + 2)
                inv_rms(nc.vector, link, st[:, 10 + t:11 + t], st[:, c + 1:c + 2], 32)
                for j in range(2):
                    nc.vector.tensor_scalar(xn[:, t, half_of(j)], x[:, t, half_of(j)], st[:, 10 + t:11 + t], None,
                                            ALU.mult).then_inc(xn_ready, 1)

            def turned(name, t):
                for k in range(KD):
                    dve.wait_ge(xT_hi_ready, xT_base[name] + 8 * t + k // 2 * 2 + 2)
                    nc.vector.scalar_tensor_tensor(
                        xT_lo[:, k, t * P:(t + 1) * P], turned_at(t, k), gain_col(name, k),
                        xT_hi[:, k, t * P:(t + 1) * P].bitcast(F32), ALU.mult, ALU.subtract).then_inc(xT_ready, 1)

            def turned_all(name):
                for k in range(KD):
                    dve.wait_ge(xT_hi_ready, xT_base[name] + k // 2 * 2 + 2)
                    nc.vector.scalar_tensor_tensor(xT_lo[:, k, :], turned_whole(name, k), gain_col(name, k),
                                                   xT_hi[:, k, :].bitcast(F32), ALU.mult, ALU.subtract) \
                        .then_inc(xT_ready, 1)

            def boundary(before, name):
                gated = before.startswith("gate")
                b = norm_of[name] if name else None
                if gated:
                    add_gated(before, 0)
                else:
                    u, s_ = gain_of[before][0], squares_of[before]
                    c = 0.5 if before.startswith("ffn") else 1.0
                    dve.wait_ge(gain_loaded[u % 2], 16 * (u // 2 + 1))
                    dve.wait_ge(y_first, y_of[before] + 1)
                    gained(before, 0, 1, c).then_inc(yg_ready, 1)
                    dve.wait_ge(y_sq, 3 * s_ + 1)
                    first_sum(nc.vector, link, st[:, 0:1], 32)
                    link(gained(before, 0, 0, c))
                    dve.wait_ge(y_sq, 3 * s_ + 2)
                    inv_rms(nc.vector, link, st[:, 8:9], st[:, 1:2], 32)
                    add_scaled(0)
                    dve.wait_ge(y_sq, 3 * s_ + 3)
                    gained(before, 1, 0, c).then_inc(dve_step, 1)
                    steps[0] += 1
                ahead_first = name and not together(name)
                if ahead_first:
                    normed_x(b, 0)
                if not gated:
                    link(gained(before, 1, 1, c))
                if ahead_first:
                    turned(name, 0)
                if gated:
                    add_gated(before, 1)
                else:
                    dve.wait_ge(y_rms, s_ + 1)
                    add_scaled(1)
                if ahead_first:
                    normed_x(b, 1)
                    turned(name, 1)
                elif name:
                    normed_x(b, 1)
                    turned_all(name)

            def tile(name, number, f, i=None):
                F, m = TILES * number + f, P if f < FULL else HALF
                dve.wait_ge(sil_ready, at(i, F + 1, 2))
                if F >= 2:
                    dve.wait_ge(h_lo_ready, at(i, F - 1, 2))
                up = q[0:P, f % 2, SEQ:2 * SEQ] if f < FULL else q[HALF:P, f % 2, 0:SEQ]
                nc.vector.tensor_tensor(h[0:m, slot(f), :], sil[0:m, f % 2, :], up, ALU.mult).then_inc(h_ready, 1)

            def tile_lo(name, number, f, i=None):
                F, m = TILES * number + f, P if f < FULL else HALF
                dve.wait_ge(h_hi_ready, at(i, F + 1, 2))
                nc.vector.tensor_tensor(h_lo[0:m, slot(f), :], h[0:m, slot(f), :],
                                        h_hi[0:m, slot(f), :].bitcast(F32), ALU.subtract).then_inc(h_lo_ready, 1)

            def ffn(name):
                ffn_order(name, dve, ahead, tile, tile_lo, embeddings)

            def embeddings_turned(l):
                dve.wait_ge(pT_hi_ready, l + 1)
                nc.vector.tensor_tensor(pT_lo[:, :, :], q[:, 2, :].rearrange("p (k c) -> p k c", k=KP),
                                        pT_hi[:, :, :].bitcast(F32), ALU.subtract).then_inc(pT_ready, 1)

            def embeddings(name):
                l = int(name[-1])
                u = gain_of["p" + name][0]
                dve.wait_ge(gain_loaded[u % 2], 16 * (u // 2 + 1))
                dve.wait_ge(p_kept, l + 1)
                dve.wait_ge(p_sq, TT * (l + 1))
                for t, src in enumerate((pn[:, 0, :], q_flat[:, D:2 * D])):
                    nc.vector.scalar_tensor_tensor(pn[:, t, :], src, 0.5, gain[:, u % 2, :],
                                                   ALU.mult, ALU.mult).then_inc(p_scaled, 1)
                dve.wait_ge(p_scaled, TT * (l + 1))
                mean_rsqrt(st[:, 14:16], st[:, 12:14], D, wide=True)
                for t in range(TT):
                    link(nc.vector.tensor_scalar(pn[:, t, :], pn[:, t, :], st[:, 14 + t:15 + t], None, ALU.mult))

            def gate(name):
                for k in range(KD):
                    ahead(toks[name] + k)

            def mixed_lo(piece):
                b, bank, blocks, t = MIXED[piece]
                dve.wait_ge(mixT_hi_ready, piece + 1)
                nc.vector.tensor_tensor(xT_lo[:, blocks, t * P:(t + 1) * P],
                                        q[:, bank, :].rearrange("p (m c) -> p m c", m=4),
                                        xT_hi[:, blocks, t * P:(t + 1) * P].bitcast(F32), ALU.subtract) \
                    .then_inc(mixT_ready, 1)

            def odd(name):
                n0 = toks[name]

                def maxima(b):
                    t, h0, heads, place, key0, wide = BATCHES[b]
                    dve.wait_ge(scores_ready, b + 1)
                    if b == 0:
                        dve.wait_ge(sinks_loaded, 16)
                    s = place[:, 0:heads * wide].rearrange("p (h k) -> p h k", h=heads)
                    link(nc.vector.memset(s[0:CHUNK, :, wide - CHUNK:wide], -1e30))
                    if t:
                        link(nc.vector.memset(s[CHUNK:P, :, key0:key0 + CHUNK], -1e30))
                    link(nc.vector.reduce_max(soft_of(b, 0), scores_of(b), AX.X))
                    link(nc.vector.scalar_tensor_tensor(soft_of(b, 5), soft_of(b, 0), HD ** -0.5,
                                                        sink[:, h0:h0 + heads], ALU.mult, ALU.max))
                    link(nc.vector.tensor_tensor(soft_of(b, 1), sink[:, h0:h0 + heads], soft_of(b, 5), ALU.subtract))
                    nc.vector.tensor_scalar(soft_of(b, 2), soft_of(b, 5), -1.0, None, ALU.mult).then_inc(max_ready, 1)

                def normed(b):
                    dve.wait_ge(exp_done, b + 1)
                    link(nc.vector.tensor_tensor(soft_of(b, 3), soft_of(b, 3), soft_of(b, 4), ALU.add))
                    link(nc.vector.reciprocal(soft_of(b, 5), soft_of(b, 3)))
                    p = prob_of(b)
                    nc.vector.tensor_tensor(p, p, soft_of(b, 5).unsqueeze(2).to_broadcast(list(p.shape)),
                                            ALU.mult).then_inc(prob_ready, 1)

                def keep_turned(b):
                    dve.wait_ge(prob_turned, TURNED[b] + 2)
                    nc.vector.tensor_copy(batch_place(probT, b)[:, 1024:2048], BATCHES[b][3][:, 1024:2048]) \
                        .then_inc(probT_dve, 1)

                for n in range(8):
                    ahead(n0 + n)
                maxima(0)
                ahead(n0 + 8)
                ahead(n0 + 9)
                normed(0)
                maxima(1)
                keep_turned(0)
                maxima(2)
                normed(1)
                normed(2)
                maxima(3)
                ahead(n0 + 10)
                ahead(n0 + 11)
                for piece in range(3):
                    mixed_lo(piece)
                normed(3)
                keep_turned(3)
                ahead(n0 + 12)
                mixed_lo(3)
                for k in range(1, KD):
                    if k == 6:
                        embeddings_turned(1)
                    ahead(n0 + 12 + k)

            def even(name):
                n0 = toks[name]

                def per_head(v):
                    return v.unsqueeze(2).to_broadcast([P, v.shape[1], P])

                def heads(v):
                    return v.rearrange("p (h c) -> p h c", c=P)

                for n in range(N_TILE):
                    ahead(n0 + n)
                dve.wait_ge(lat_sq, 1)
                for c, n in ((64, Q_LORA), (66, KV_LORA)):
                    link(nc.vector.tensor_scalar(st[:, 72 + c - 64:74 + c - 64], st[:, c:c + 2], 1.0 / n, EPS,
                                                 ALU.mult, ALU.add))
                link(nc.vector.tensor_scalar(st[:, 76:80], st[:, 72:76], -0.5, None, ALU.mult))
                rsqrt(st[:, 68:72], st[:, 72:76], st[:, 76:80], st[:, 80:84], True, lat_rms)
                dve.wait_ge(gates_in, 1)
                z, ab = gs[:, 16:24], gs[:, 0:16].rearrange("p (t c) -> p t c", t=TT)
                link(nc.vector.tensor_tensor(z.rearrange("p (t h) -> p t h", t=TT), ab[:, :, 0:4],
                                             gs[:, 128:132].unsqueeze(1).to_broadcast([P, TT, 4]), ALU.add))
                link(nc.vector.tensor_scalar(gs[:, 24:32], z, -1.0, None, ALU.mult))
                nc.vector.tensor_tensor(gs[:, 24:32], gs[:, 24:32], z, ALU.max).then_inc(gates_raw, 1)
                dve.wait_ge(gates_exp, 2)
                link(nc.vector.scalar_tensor_tensor(gs[:, 40:48], z, 0.0, gs[:, 40:48], ALU.max, ALU.add))
                nc.vector.scalar_tensor_tensor(gs[:, 56:64].rearrange("p (t h) -> p t h", t=TT),
                                               gs[:, 40:48].rearrange("p (t h) -> p t h", t=TT), -1.0,
                                               gs[:, 136:140].unsqueeze(1).to_broadcast([P, TT, 4]),
                                               ALU.mult, ALU.mult).then_inc(gates_set, 1)
                link(nc.vector.tensor_scalar(gs[:, 48:56], gs[:, 48:56], 1.0, None, ALU.add))
                link(nc.vector.reciprocal(gs[:, 140:148], gs[:, 48:56]))
                beta = gs[:, 140:148]
                def latents_turned():
                    for k in range(KL):
                        dve.wait_ge(latT_hi_ready, min(k // 2 * 2 + 2, KL))
                        nc.vector.scalar_tensor_tensor(latT_lo[:, k, :], lat_bank(k),
                                                       cols[:, COL_QN + k:COL_QN + k + 1],
                                                       latT_hi[:, k, :].bitcast(F32), ALU.mult, ALU.subtract) \
                            .then_inc(latT_ready, 1)
                    dve.wait_ge(sums_kept, 1)
                    gc, gl = gs[:, 64:72], gs[:, 72:80]
                    link(nc.vector.tensor_copy(gs[:, 160:168], gc))
                    link(nc.vector.tensor_tensor(gs[:, 168:176], gl, gc, ALU.subtract))
                    link(nc.vector.tensor_scalar(gs[:, 192:200], gc, -1.0, None, ALU.mult))
                    nc.vector.tensor_copy(gs[:, 176:192], gs[:, 80:96]).then_inc(dec_args, 1)

                for j in range(3 * GH):
                    ahead(n0 + N_TILE + j)
                    if j == GH:
                        latents_turned()
                    dve.wait_ge(conv_first, j + 1)
                    for d in range(1, 4):
                        c = COL_CONV + 12 * (3 - d) + conv_col(j)
                        ins = nc.vector.scalar_tensor_tensor(convT[:, j, d:SEQ], q[:, j % 4, 0:SEQ - d],
                                                             cols[:, c:c + 1], convT[:, j, d:SEQ],
                                                             ALU.mult, ALU.add)
                        if d < 3:
                            link(ins)
                        else:
                            ins.then_inc(conv_done, 1)
                dve.wait_ge(grown, 1)
                wide = y[:, 0, :].rearrange("p (m c) -> p m c", m=TT * GH)
                for place, mask in ((attnT, "add_upto"), (lmat, "add_before")):
                    m = const[:, C_AT[mask]:C_AT[mask] + P].unsqueeze(1).to_broadcast([P, TT * GH, P])
                    ins = nc.vector.tensor_tensor(place[:, :, :], wide, m, ALU.add)
                    if place is attnT:
                        link(ins)
                    else:
                        ins.then_inc(decay_args, 1)

                def scaled_rows(s_):
                    place = (inv_t, inv_u)[s_]
                    for t in range(TT):
                        dve.wait_ge(tok_sq, 2 * s_ + t + 1)
                        link(nc.vector.reduce_sum(st[:, 96 + 8 * s_ + 4 * t:100 + 8 * s_ + 4 * t],
                                                  place[:, 4 * t:4 * t + 4, :], AX.X))
                    c = slice(96 + 8 * s_, 104 + 8 * s_)
                    to = slice(112 + 8 * s_, 120 + 8 * s_)
                    link(nc.vector.tensor_scalar(st[:, 128:136], st[:, c], EPS, None, ALU.add))
                    link(nc.vector.tensor_scalar(st[:, 136:144], st[:, 128:136], -0.5, None, ALU.mult))
                    rsqrt(st[:, to], st[:, 128:136], st[:, 136:144], st[:, 144:152], True, None)
                    if s_:
                        link(nc.vector.tensor_scalar(st[:, to], st[:, to], P ** -0.5, None, ALU.mult))
                    out_ = (k_tok, q_tok)[s_]
                    for t in range(TT):
                        nc.vector.tensor_tensor(heads(out_[:, t, :]), heads(q[:, 2 * (1 - s_) + t, :]),
                                                per_head(st[:, 112 + 8 * s_ + 4 * t:116 + 8 * s_ + 4 * t]),
                                                ALU.mult).then_inc(tok_ready, 1)

                scaled_rows(0)
                ahead(n0 + N_Z)
                ahead(n0 + N_Z + 1)
                ahead(n0 + N_Z + 2)
                scaled_rows(1)
                for t in range(TT):
                    dve.wait_ge(tok_turned, 4 + t + 1)
                    nc.vector.tensor_tensor(rhs[:, 4 * t:4 * t + 4, 0:P], heads(q[:, 2 + t, :]),
                                            per_head(beta[:, 4 * t:4 * t + 4]), ALU.mult).then_inc(rhs_ready, 1)
                ahead(n0 + N_Z + 3)
                ahead(n0 + N_UQ)
                dve.wait_ge(rope_kept, 1)
                dve.wait_ge(rope_key, 1)
                a, b = rope_in[:, :, :, 0:32], rope_in[:, :, :, 32:64]
                ra, rb = rope_out[:, :, 0:5, 0:32], rope_out[:, :, 0:5, 32:64]
                link(nc.vector.memset(rope_out[:, :, 5:7, :], 0.0))
                cos, sin = (const[:, c:c + 64].rearrange("p (t d) -> p t d", t=TT).unsqueeze(2)
                            .to_broadcast([P, TT, 5, 32]) for c in (C_COS, C_SIN))

                def rope_op(o, x0, x1, op):
                    for t in range(TT):
                        link(nc.vector.tensor_tensor(o[:, t], x0[:, t], x1[:, t], op))

                rt = rope_tmp[:, :, :, :]
                rope_op(ra, a, cos, ALU.mult)
                rope_op(rt, b, sin, ALU.mult)
                rope_op(ra, ra, rt, ALU.subtract)
                rope_op(rb, b, cos, ALU.mult)
                rope_op(rt, a, sin, ALU.mult)
                rope_op(rb, rb, rt, ALU.add)
                nc.vector.tensor_copy(rope_out[:, :, 7, :], rope_out[:, :, 4, :]).then_inc(rope_ready, 1)
                ahead(n0 + N_UQ + 1)
                ahead(n0 + N_UQ + 2)
                dve.wait_ge(decay_ready, TT * GH)
                link(nc.vector.tensor_tensor(lmat[:, :, :], lmat[:, :, :], per_head(beta), ALU.mult))
                dve.wait_ge(grams, 1)
                nc.vector.tensor_tensor(lmat[:, :, :].rearrange("p m c -> p (m c)"), q_flat[:, 0:1024],
                                        lmat[:, :, :].rearrange("p m c -> p (m c)"), ALU.mult).then_inc(l_ready, 1)
                dve.wait_ge(back_kept, 2)
                for t in range(TT):
                    nc.vector.tensor_tensor(qdT[:, :, t * P:(t + 1) * P], qnT[:, :, t * P:(t + 1) * P],
                                            cross[:, 4 * t:4 * t + 4, :], ALU.mult).then_inc(qd_ready, 1)
                dve.wait_ge(rope_turned, 1)
                eye = ident.unsqueeze(1).to_broadcast([P, 4, P])
                level0 = const[:, C_LEVEL:C_LEVEL + P].unsqueeze(1).to_broadcast([P, 4, P])
                for t in range(TT):
                    r = slice(4 * t, 4 * t + 4)
                    dve.wait_ge(cross_made, t + 1)
                    link(nc.vector.tensor_tensor(inv_u[:, r, :], heads(q[:, t, :]), level0, ALU.mult))
                    nc.vector.tensor_tensor(inv_u[:, r, :], inv_u[:, r, :], eye, ALU.add).then_inc(inv_ready, 2)
                dve.wait_ge(grams, 2)
                nc.vector.tensor_tensor(attnT[:, :, :].rearrange("p m c -> p (m c)"), q_flat[:, 1024:2048],
                                        attnT[:, :, :].rearrange("p m c -> p (m c)"), ALU.mult).then_inc(l_ready, 1)
                for t in range(TT):
                    dve.wait_ge(m_scores, t + 1)
                    link(nc.vector.memset(m_scores_of(t)[0:CHUNK, :, (2 * t + 1) * CHUNK:], -1e30))
                    r = slice(4 * t, 4 * t + 4)
                    link(nc.vector.reduce_max(m_soft[:, 0, r], m_scores_of(t), AX.X))
                    nc.vector.tensor_scalar(m_soft[:, 1, r], m_soft[:, 0, r], -M_SCALE, None, ALU.mult) \
                        .then_inc(m_max, 1)

                def masked_cross(t, made, mask):
                    dve.wait_ge(cross_made, made)
                    nc.vector.tensor_tensor(cross[:, 4 * t:4 * t + 4, :], heads(q[:, t, :]), mask, ALU.mult) \
                        .then_inc(cross_ready, 1)

                dve.wait_ge(qd_ready, TT)
                dve.wait_ge(inv_t_first, 1)
                with dve.Fori(0, LEVELS - 2) as i:
                    for t in range(TT):
                        mask = const[:, bass.ds(i * P + (C_LEVEL + P), P)].unsqueeze(1).to_broadcast([P, 4, P])
                        masked_cross(t, i * TT + (TT + t + 1), mask)
                    for t in range(TT):
                        r = slice(4 * t, 4 * t + 4)
                        dve.wait_ge(inv_made, i * 4 + (2 * t + 2))
                        for place, bank in ((inv_t, t), (inv_u, 2 + t)):
                            nc.vector.tensor_tensor(place[:, r, :], heads(q[:, bank, :]), place[:, r, :], ALU.add) \
                                .then_inc(inv_ready, 1)
                c = C_LEVEL + (LEVELS - 1) * P
                for t in range(TT):
                    masked_cross(t, TT * (LEVELS - 1) + t + 1,
                                 const[:, c:c + P].unsqueeze(1).to_broadcast([P, 4, P]))
                dve.wait_ge(dec_ready, 1)
                dve.wait_ge(tok_ready, 2)
                link(nc.vector.tensor_tensor(gs[:, 200:208], beta, gs[:, 96:104], ALU.mult))
                for t in range(TT):
                    r = slice(4 * t, 4 * t + 4)
                    dve.wait_ge(inv_made, 4 * (LEVELS - 2) + t + 1)
                    nc.vector.tensor_tensor(inv_u[:, r, :], heads(q[:, 2 + t, :]), inv_u[:, r, :], ALU.add) \
                        .then_inc(inv_ready, 1)
                for t in range(TT):
                    r = slice(4 * t, 4 * t + 4)
                    nc.vector.tensor_tensor(rhs[:, r, P:2 * P], heads(k_tok[:, t, :]),
                                            per_head(gs[:, 200 + 4 * t:204 + 4 * t]), ALU.mult).then_inc(rhs_ready, 1)
                for t in range(TT):
                    r = slice(4 * t, 4 * t + 4)
                    dve.wait_ge(m_exp, t + 1)
                    link(nc.vector.reciprocal(m_soft[:, 3, r], m_soft[:, 2, r]))
                    p = m_prob_of(t)
                    nc.vector.tensor_tensor(p, p, m_soft[:, 3, r].unsqueeze(2).to_broadcast(list(p.shape)),
                                            ALU.mult).then_inc(m_prob_ready, 1)
                for t in range(TT):
                    nc.vector.tensor_tensor(heads(k_dec[:, t, :]), heads(k_tok[:, t, :]),
                                            per_head(gs[:, 104 + 4 * t:108 + 4 * t]), ALU.mult).then_inc(rhs_ready, 1)
                for n in range(2):
                    ahead(n0 + N_UKV + n)
                dve.wait_ge(m_turned, 3)
                nc.vector.tensor_copy(m_probT[:, 2 * BANK:3 * BANK], y[:, 1, BANK:2 * BANK]).then_inc(m_probT_dve, 1)

                def mixed_lo(j, block, place):
                    dve.wait_ge(emix_hi, j + 1)
                    nc.vector.tensor_tensor(xT_lo[:, block:block + 2, :].rearrange("p m c -> p (m c)"), place,
                                            xT_hi[:, block:block + 2, :].bitcast(F32)
                                            .rearrange("p m c -> p (m c)"), ALU.subtract).then_inc(emix_ready, 1)

                dve.wait_ge(solved_kept, 2)
                for n in range(4):
                    t, r = n // 2, slice((n % 2) * CHUNK, (n % 2 + 1) * CHUNK)
                    if n:
                        dve.wait_ge(read_out, n)
                        nc.vector.tensor_tensor(v_new[r, t, :], u_tok[r, t, :], q[r, 0, :], ALU.subtract) \
                            .then_inc(v_new_ready, 1)
                    if n == 3:
                        break
                    dve.wait_ge(kv_made, n + 1)
                    if n == 0:
                        nc.vector.tensor_copy(states[1][:, :, :].rearrange("p h c -> p (h c)"), q[:, 2, :]) \
                            .then_inc(state_ready, 4)
                    else:
                        if n == 1:
                            for j in range(2):
                                mixed_lo(j, 4 + 2 * j, y[:, 0, j * BANK:(j + 1) * BANK])
                        for hd in range(GH):
                            c = 112 + 8 * (n % 2) + 4 * t + hd
                            nc.vector.scalar_tensor_tensor(states[(n + 1) % 2][:, hd, :], states[n % 2][:, hd, :],
                                                           gs[:, c:c + 1], q[:, 2, hd * P:(hd + 1) * P],
                                                           ALU.mult, ALU.add).then_inc(state_ready, 1)
                        if n == 1:
                            ahead(n0 + N_OUT)
                dve.wait_ge(z_ready, 1)
                for t in range(TT):
                    dve.wait_ge(o_sq, t + 1)
                    link(nc.vector.reduce_sum(st[:, 152 + 4 * t:156 + 4 * t], heads(k_dec_free(t)), AX.X))
                mean_rsqrt(st[:, 160:168], st[:, 152:160], P, wide=True, at_=168)
                for t in range(TT):
                    link(nc.vector.tensor_tensor(heads(o_tok[:, t, :]), heads(q[:, 1 + 2 * t, :]),
                                                 per_head(st[:, 160 + 4 * t:164 + 4 * t]), ALU.mult))
                    nc.vector.tensor_tensor(o_tok[:, t, :], o_tok[:, t, :], z_gate[:, t, :], ALU.mult) \
                        .then_inc(o_ready, 1)
                for k in range(1, 3):
                    ahead(n0 + N_OUT + k)
                for j in range(2):
                    mixed_lo(2 + j, 2 * j, q[:, j, :])
                for k in range(3, 6):
                    ahead(n0 + N_OUT + k)
                embeddings_turned(0)
                for k in range(6, KD):
                    ahead(n0 + N_OUT + k)

            nc.vector.memset(ones[:, :], 1.0).then_inc(ones_set, 1)
            nc.vector.memset(rows[:, :], 1.0).then_inc(rows_clear, 1)
            nc.vector.memset(bias[:, :], 0.0).then_inc(bias_clear, 1)
            normed_x(0, 1)
            split_lo(0)
            split_lo(1)
            dve.wait_ge(cols_ready, 1)
            turned_all(mains[0])
            for n in range(2, AHEAD):
                split_lo(n)
            dve.wait_ge(bias_hi_ready, 1)
            nc.vector.tensor_tensor(bias_lo[:, :], bias[:, :], bias_hi[:, :].bitcast(F32), ALU.subtract) \
                .then_inc(bias_ready, 1)
            for j, name in enumerate(mains):
                if j:
                    boundary(mains[j - 1], name)
                if name.startswith("ffn"):
                    ffn(name)
                elif name.startswith("gate"):
                    gate(name)
                elif name == "mix1":
                    odd(name)
                elif name == "mix0":
                    even(name)
            boundary(mains[-1], None)

        @block.tensor
        def _(pe):
            def split_product(to, a_hi, a_lo, b_hi, b_lo, start, stop):
                nc.tensor.matmul(to, a_hi, b_hi, start=start, stop=False)
                nc.tensor.matmul(to, a_hi, b_lo, start=False, stop=False)
                return nc.tensor.matmul(to, a_lo, b_hi, start=False, stop=stop)

            def stay_warm(name):
                b = norm_of[name]
                if extra(name):
                    return
                if b == 0:
                    steps = [(ones_set, 1), (x_sq, 2), (x_sq, 4)]
                else:
                    steps = [(x_ready, 4 * b - 2)]
                    if mains[b - 1] in squares_of:
                        steps = [(y_sq, 3 * squares_of[mains[b - 1]] + 3)] + steps
                    if together(name):
                        steps.append((x_ready, 4 * b))
                for signal, count in steps:
                    pe.wait_ge(signal, count)
                    for _ in range(WARM):
                        nc.tensor.matmul(q[:, 3, 0:P], ones[:, :], ones[:, :], start=True, stop=True)

            def turn(name, t):
                for k in range(KD):
                    if k % 4 == 0:
                        pe.wait_ge(xn_ready, xn_base[name] + 2 * t + k // 4 + 1)
                    if k == 4 and t:
                        pe.wait_ge(xT_ready, xT_base[name] + 8)
                    mm = nc.tensor.transpose(turned_at(t, k), xn[:, t, k * P:(k + 1) * P], ident)
                    if k % 2:
                        mm.then_inc(xn_turned, 1)

            def turn_all(name):
                if extra(name):
                    pe.wait_ge(x_ready, 4 * norm_of[name])
                for t in range(TT):
                    for k in range(KD):
                        if k % 4 == 0 and t == 0:
                            pe.wait_ge(xn_act, act_base[name] + k // 4 + 1)
                        elif k % 4 == 0:
                            pe.wait_ge(xn_ready, xn_base[name] + k // 4 + 1)
                        mm = nc.tensor.transpose(turned_whole(name, k)[:, t * P:(t + 1) * P],
                                                 xn[:, t, k * P:(k + 1) * P], ident)
                        if t and k % 2:
                            mm.then_inc(xn_turned, 1)

            def wait_xT(name, t, k):
                pe.wait_ge(xT_ready, xT_base[name] + 8 * t + k // 2 * 2 + 2)

            def lead(name, product, count):
                turn(name, 0)
                for j in range(count - 1):
                    product(j, 0)
                turn(name, 1)
                product(count - 1, 0)
                for j in range(count):
                    product(j, 1)

            def bias_rows(t, r):
                for half in range(2):
                    c = half_of(half)
                    nc.tensor.matmul(y[:, t, c], ones_r[r:r + 1, :], bias_hi[r:r + 1, c], start=True, stop=False)
                    nc.tensor.matmul(y[:, t, c], ones_r[r:r + 1, :], bias_lo[r:r + 1, c], start=False, stop=False)

            def row_slab(n, k, t, aT_hi, aT_lo, start, stop):
                a = slice(t * P, (t + 1) * P)
                for half in range(2):
                    c = half_of(half)
                    mm = split_product(y[:, t, c], aT_hi[:, k, a], aT_lo[:, k, a],
                                       hi[:, n % RING, c], lo[:, n % RING, c], start, stop)
                return mm

            def row_slabs(n0, i0, i1, aT_hi, aT_lo, first, last, block=lambda i: i, more=False):
                body = i1 - 2 if last else i1
                for i in range(i0, body):
                    pe.wait_ge(lo_ready, n0 + i + 1)
                    for t in range(TT):
                        mm = row_slab(n0 + i, block(i), t, aT_hi, aT_lo, first and i == i0,
                                      not last and not more and i == i1 - 1)
                    mm.then_inc(slab_used, 1)
                if last:
                    for t in range(TT):
                        for i in range(body, i1):
                            pe.wait_ge(lo_ready, n0 + i + 1)
                            mm = row_slab(n0 + i, block(i), t, aT_hi, aT_lo, False, i == i1 - 1)
                            if t:
                                mm.then_inc(slab_used, 1)
                        if t == 0:
                            mm.then_inc(y_first, 1)

            def column_tile(to, n, name=None):
                for k in range(KD):
                    if name and k % 2 == 0:
                        wait_xT(name, 0, k)
                    w = slice(k * P, (k + 1) * P)
                    mm = split_product(to, hi[:, n % RING, w], lo[:, n % RING, w],
                                       xT_hi[:, k, :], xT_lo[:, k, :], k == 0, k == KD - 1)
                mm.then_inc(slab_used, 1)

            def down(n, t, F, f, i=None, start=False, stop=False):
                m = P if f < FULL else HALF
                pe.wait_ge(lo_ready, at(i, n + 1, 6))
                pe.wait_ge(h_lo_ready, at(i, F + 1, 2))
                a = slice(t * P, (t + 1) * P)
                for half in range(2):
                    c = half_of(half)
                    mm = split_product(y[:, t, c], h_hi[0:m, slot(f), a], h_lo[0:m, slot(f), a],
                                       hi[0:m, n % RING, c], lo[0:m, n % RING, c], start, stop)
                if stop and t == 0:
                    mm.then_inc(y_first, 1)
                return mm

            def ffn(name):
                number = ffns[name][1]
                n_of = slab_at[name]
                F0 = TILES * number

                def gu(f, i=None):
                    n, F = n_of["g", f], F0 + f
                    if F >= 2:
                        pe.wait_ge(h_ready, at(i, F - 1, 2))
                    pe.wait_ge(lo_ready, at(i, n + 1, 6))
                    column_tile(q[:, f % 2, 0:SEQ], n, None if f else name)
                    if f < FULL:
                        pe.wait_ge(lo_ready, at(i, n + 2, 6))
                        column_tile(q[:, f % 2, SEQ:2 * SEQ], n + 1)

                def d(f, i=None):
                    for t in range(TT):
                        mm = down(n_of["d", f], t, F0 + f, f, i, start=f == 0)
                    mm.then_inc(slab_used, 1)

                turn_all(name)
                if extra(name):
                    pe.wait_ge(p_kept, int(name[-1]) + 1)
                gu(0)
                gu(1)
                d(0)
                gu(2)
                d(1)
                with pe.Fori(0, TURNS) as i:
                    for f in (LOOP0, LOOP0 + 1):
                        gu(f, i)
                        d(f - 1, i)
                gu(LOOP1)
                d(LOOP1 - 1)
                gu(FULL - 1)
                gu(FULL)
                d(FULL - 2)
                for t in range(TT):
                    for f in (FULL - 1, FULL):
                        mm = down(n_of["d", f], t, F0 + f, f, stop=f == FULL)
                        if t:
                            mm.then_inc(slab_used, 1)

            def turn_embeddings(l):
                pe.wait_ge(p_loaded, 16 * (l + 1))
                for k in range(KP):
                    for t in range(TT):
                        c = k * SEQ + t * P
                        mm = nc.tensor.transpose(q[:, 2, c:c + P], p_in[:, t, k * P:(k + 1) * P], ident)
                mm.then_inc(p_turned, 1)

            def project_embeddings(l):
                pe.wait_ge(pT_ready, l + 1)
                for t in range(TT):
                    a = slice(t * P, (t + 1) * P)
                    for k in range(KP):
                        n = slab_at[f"ffn2_{l}"]["p", k]
                        pe.wait_ge(lo_ready, n + 1)
                        for half in range(2):
                            c = half_of(half)
                            mm = split_product(q[:, 2 * t + half, :], pT_hi[:, k, a], pT_lo[:, k, a],
                                               hi[:, n % RING, c], lo[:, n % RING, c], k == 0, k == KP - 1)
                        if t:
                            mm.then_inc(slab_used, 1)
                    if t == 0:
                        mm.then_inc(p_made, 1)

            def gate(name):
                n0 = toks[name]

                def first(j, t):
                    pe.wait_ge(lo_ready, n0 + j + 1)
                    if j == 0:
                        wait_xT(name, t, 3)
                        bias_rows(t, 32 * int(name[-1]))
                    mm = row_slab(n0 + j, j, t, xT_hi, xT_lo, False, False)
                    if t:
                        mm.then_inc(slab_used, 1)

                lead(name, first, 4)
                wait_xT(name, 1, KD - 1)
                row_slabs(n0, 4, KD, xT_hi, xT_lo, False, True)

            def odd(name):
                n0 = toks[name]

                def tile(p):
                    if p >= 4:
                        pe.wait_ge(qk_kept, p - 3)
                    pe.wait_ge(lo_ready, n0 + 2 + p + 1)
                    column_tile(q[:, p % 4, 0:SEQ], n0 + 2 + p)

                def first(j, t):
                    n = n0 + j
                    pe.wait_ge(lo_ready, n + 1)
                    if j == 0:
                        nc.tensor.matmul(y[:, t, 0:256], ones_r[96:97, :], bias_hi[96:97, 0:256],
                                         start=True, stop=False)
                        nc.tensor.matmul(y[:, t, 0:256], ones_r[96:97, :], bias_lo[96:97, 0:256],
                                         start=False, stop=False)
                    a = slice(t * P, (t + 1) * P)
                    for k in range(4):
                        wait_xT(name, 0, 4 * j + k)
                        w = slice(k * 256, (k + 1) * 256)
                        mm = split_product(y[:, t, 0:256], xT_hi[:, 4 * j + k, a], xT_lo[:, 4 * j + k, a],
                                           hi[:, n % RING, w], lo[:, n % RING, w], False, j == 1 and k == 3)
                    if t:
                        mm.then_inc(slab_used, 1)

                turn_all(name)
                for j in range(2):
                    for t in range(TT):
                        first(j, t)

                def scores(b):
                    t, h0, heads, place, key0, wide = BATCHES[b]
                    for j in range(heads):
                        hd = h0 + j
                        a, half = hd // 8, (hd // 4 % 2) * HD
                        r = slice(half, half + HD)
                        mm = nc.tensor.matmul(scores_of(b)[:, j, :], qkT[r, 2 + 4 * a + hd % 4, t * P:(t + 1) * P],
                                              qkT[r, a, key0:key0 + wide - key0], start=True, stop=True)
                    mm.then_inc(scores_ready, 1)

                def turn(b):
                    t, h0, heads, place, key0, wide = BATCHES[b]
                    pe.wait_ge(prob_ready, b + 1)
                    if t:
                        pe.wait_ge(zero_set, 1)
                    for j in range(heads * (t + 1)):
                        c = slice(j * P, (j + 1) * P)
                        mm = nc.tensor.transpose(place[:, c], batch_place(prob, b)[:, c], ident)
                        if j % 8 == 7:
                            mm.then_inc(prob_turned, 1)

                def kept(b):
                    pe.wait_ge(probT_act, b + 1)
                    if BATCHES[b][0]:
                        pe.wait_ge(probT_dve, 1 if b == 0 else 2)

                def mix(b):
                    t, h0, heads, place, key0, wide = BATCHES[b]
                    kept(b)
                    for j in range(heads):
                        hd = h0 + j
                        g = hd // 4
                        c0 = (hd // 2) * P if t == 0 else 1024 + (hd // 2) * P
                        to = q_flat[(hd % 2) * HD:(hd % 2 + 1) * HD, c0:c0 + P]
                        for kt in range(t + 1):
                            c = j * wide + kt * P
                            mm = nc.tensor.matmul(to, val[:, kt, g * HD:(g + 1) * HD], batch_place(probT, b)[:, c:c + P],
                                                  start=kt == 0, stop=kt == t)
                    mm.then_inc(mixed, 1)

                for p in range(5):
                    tile(p)
                pe.wait_ge(val_kept, 1)
                pe.wait_ge(qk_kept, 5)
                scores(0)
                for p in range(5, 10):
                    tile(p)
                pe.wait_ge(qk_kept, 10)
                scores(1)
                turn(0)
                scores(2)
                kept(0)
                scores(3)
                turn(1)
                turn(2)
                kept(2)
                for b in range(3):
                    mix(b)
                turn(3)
                kept(3)
                pe.wait_ge(mixT_ready, 3)
                for t in range(TT):
                    bias_rows(t, 64)
                row_slabs(n0 + 12, 0, 1, xT_hi, xT_lo, False, False, more=True)
                mix(3)
                row_slabs(n0 + 12, 1, 4, xT_hi, xT_lo, False, False, more=True)
                pe.wait_ge(mixT_ready, len(MIXED))
                row_slabs(n0 + 12, 4, KD - 2, xT_hi, xT_lo, False, False, more=True)
                turn_embeddings(1)
                row_slabs(n0 + 12, KD - 2, KD, xT_hi, xT_lo, False, True)
                project_embeddings(1)

            def even(name):
                n0 = toks[name]
                pe.wait_ge(const_loaded, 16)

                def turn_latents():
                    pe.wait_ge(lat_ready, 1)
                    pe.wait_ge(rope_key, 1)
                    for k in range(KL):
                        for t in range(TT):
                            mm = nc.tensor.transpose(lat_bank(k)[:, t * P:(t + 1) * P],
                                                     lat[:, t, k * P:(k + 1) * P], ident)
                        if k % 2 or k == KL - 1:
                            mm.then_inc(lat_turned, 1)
                    pe.wait_ge(gates_set, 1)
                    for j, m in enumerate(("upto", "same", "first", "second")):
                        mm = nc.tensor.matmul(y[:, 1, 8 * j:8 * j + 8], const[:, C_AT[m]:C_AT[m] + P], gs[:, 56:64],
                                              start=True, stop=True)
                    mm.then_inc(sums_ready, 1)

                def first(j, t):
                    mm = pair_slab(n0 + N_A + j, j, t, W_A, 0, name)
                    if t:
                        mm.then_inc(slab_used, 1)

                lead(name, first, 4)
                for j in range(4):
                    for t in range(TT):
                        mm = pair_slab(n0 + N_KV + j, j, t, W_KV, BANK)
                    mm.then_inc(slab_used, 1)
                for j in range(3 * GH):
                    if j == GH:
                        turn_latents()
                    n = n0 + N_TILE + j
                    if j >= 4:
                        pe.wait_ge(conv_done, j - 3)
                    pe.wait_ge(lo_ready, n + 1)
                    column_tile(q[:, j % 4, 0:SEQ], n)
                pe.wait_ge(latT_ready, KL)
                pe.wait_ge(sums_kept, 1)
                for m in range(TT * GH):
                    mm = nc.tensor.matmul(y[:, 0, m * P:(m + 1) * P], gs[:, 56 + m:57 + m].to_broadcast([P, P]),
                                          const[:, C_AT["upto"]:C_AT["upto"] + P], start=True, stop=True)
                mm.then_inc(wide_sums, 1)

                def z_slab(j):
                    for t in range(TT):
                        mm = pair_slab(n0 + N_Z + j, j, t, BANK, 0, to=y[:, 1, t * BANK:(t + 1) * BANK])
                    mm.then_inc(slab_used, 1)

                def by_token(s_, banks):
                    for t in range(TT):
                        for hd in range(GH):
                            mm = nc.tensor.transpose(q[:, banks + t, hd * P:(hd + 1) * P],
                                                     convT[:, s_ * GH + hd, t * P:(t + 1) * P], ident)
                        mm.then_inc(tok_turned, 1)

                def back(s_, src):
                    for hd in range(GH):
                        for t in range(TT):
                            c = s_ * 1024 + hd * SEQ + t * P
                            mm = nc.tensor.transpose(q_flat[:, c:c + P], src[:, t, hd * P:(hd + 1) * P], ident)
                    mm.then_inc(back_turned, 1)

                def gram(s_, b):
                    pe.wait_ge(back_kept, s_ + 1)
                    for m in range(TT * GH):
                        t, hd = m // GH, m % GH
                        a = slice(t * P, (t + 1) * P)
                        c = s_ * 1024 + m * P
                        mm = nc.tensor.matmul(q_flat[:, c:c + P], knT[:, hd, a], b[:, hd, a], start=True, stop=True)
                    mm.then_inc(grams, 1)

                def project(part, first, count, width, made, wide_at):
                    pe.wait_ge(lo_ready, n0 + part + count)
                    for hd in range(GH):
                        for k in range(count):
                            w = slice(hd * width, hd * width + P)
                            s_ = (n0 + part + k) % RING
                            mm = split_product(y[:, 0, hd * SEQ:(hd + 1) * SEQ], hi[:, s_, w], lo[:, s_, w],
                                               latT_hi[:, first + k, :], latT_lo[:, first + k, :],
                                               k == 0, k == count - 1)
                    mm.then_inc(made, 1)
                    for t in range(TT):
                        a = slice(t * P, (t + 1) * P)
                        for k in range(count):
                            s_ = (n0 + part + k) % RING
                            w_hi, w_lo = (v[:, s_, 0:GH * width].rearrange("p (h c) -> p h c", h=GH)[:, :, P:width]
                                          for v in (hi, lo))
                            mm = split_product(y[:, 1, t * wide_at:(t + 1) * wide_at], latT_hi[:, first + k, a],
                                               latT_lo[:, first + k, a], w_hi, w_lo, k == 0, k == count - 1)
                            if t == TT - 1:
                                mm.then_inc(slab_used, 1)

                z_slab(0)
                z_slab(1)
                pe.wait_ge(conv_ready, 3 * GH)
                by_token(0, 2)
                by_token(1, 0)
                z_slab(2)
                z_slab(3)
                pe.wait_ge(tok_ready, 2)
                by_token(2, 2)
                pe.wait_ge(decay_args, 1)
                pe.wait_ge(z_in, 1)
                project(N_UQ, 0, 3, 192, qn_made, 256)
                pe.wait_ge(tok_ready, 4)
                back(0, k_tok)
                pe.wait_ge(q_nope_kept, 1)
                pe.wait_ge(rope_kept, 1)
                project(N_UKV, 3, 2, 256, kn_made, BANK)
                pe.wait_ge(rhs_ready, 2)
                back(1, q_tok)
                gram(0, knT)
                pe.wait_ge(rope_ready, 1)
                pe.wait_ge(k_nope_kept, 1)
                for r in range(4):
                    for t in range(TT):
                        c = r * SEQ + t * P
                        mm = nc.tensor.transpose(y[:, 0, c:c + P],
                                                 rope_out[:, t, 2 * r:2 * r + 2, :].rearrange("p h c -> p (h c)"),
                                                 ident)
                mm.then_inc(rope_turned, 1)
                gram(1, qnT)
                pe.wait_ge(l_ready, 1)
                for t in range(TT):
                    for m in range(4 * t, 4 * t + 4):
                        c = (m % 4) * P
                        mm = nc.tensor.transpose(q[:, t, c:c + P], lmat[:, m, :], ident)
                    mm.then_inc(cross_made, 1)
                pe.wait_ge(ropeT_kept, 1)
                pe.wait_ge(m_val_kept, 1)
                for t in range(TT):
                    for hd in range(GH):
                        to, a, w = m_scores_of(t)[:, hd, :], slice(t * P, (t + 1) * P), (t + 1) * P
                        nc.tensor.matmul(to, q_nopeT[:, hd, a], k_nopeT[:, hd, 0:w], start=True, stop=False)
                        mm = nc.tensor.matmul(to, ropeT[:, hd // 2, a], ropeT[:, 2 + hd % 2, 0:w],
                                              start=False, stop=True)
                    mm.then_inc(m_scores, 1)

                def cross_product(t):
                    for m in range(4 * t, 4 * t + 4):
                        c = (m % 4) * P
                        mm = nc.tensor.matmul(q[:, t, c:c + P], lmat[:, m, :], inv_u[:, m, :], start=True, stop=True)
                    mm.then_inc(cross_made, 1)

                def inverse_product(t, bank, left, right):
                    for m in range(4 * t, 4 * t + 4):
                        c = (m % 4) * P
                        mm = nc.tensor.matmul(q[:, bank, c:c + P], left[:, m, :], right[:, m, :],
                                              start=True, stop=True)
                    mm.then_inc(inv_made, 1)

                pe.wait_ge(l_ready, 2)
                pe.wait_ge(inv_t_first, 1)
                with pe.Fori(0, LEVELS - 2) as i:
                    for t in range(TT):
                        pe.wait_ge(inv_ready, i * 4 + (2 * t + 2))
                        cross_product(t)
                    for t in range(TT):
                        pe.wait_ge(cross_ready, i * TT + (t + 1))
                        inverse_product(t, t, cross, inv_t)
                        inverse_product(t, 2 + t, inv_t, cross)
                for t in range(TT):
                    pe.wait_ge(inv_ready, 4 * (LEVELS - 2) + 2 * t + 2)
                    cross_product(t)
                for t in range(TT):
                    pe.wait_ge(cross_ready, TT * (LEVELS - 2) + t + 1)
                    inverse_product(t, 2 + t, inv_t, cross)
                pe.wait_ge(inv_ready, 4 * (LEVELS - 1) + TT)
                for m in range(TT * GH):
                    mm = nc.tensor.matmul(q_flat[:, m * P:(m + 1) * P], inv_u[:, m, :], rhs[:, m, 0:P],
                                          start=True, stop=True)
                mm.then_inc(solved, 1)
                pe.wait_ge(rhs_ready, 4)
                for m in range(TT * GH):
                    mm = nc.tensor.matmul(q_flat[:, 1024 + m * P:1024 + (m + 1) * P], rhs[:, m, P:2 * P],
                                          inv_u[:, m, :], start=True, stop=True)
                mm.then_inc(solved, 1)
                for t in range(TT):
                    pe.wait_ge(m_prob_ready, t + 1)
                    for j in range(GH * (t + 1)):
                        c = slice(j * P, (j + 1) * P)
                        src = t * GH * P + j * P
                        mm = nc.tensor.transpose(y[:, t, c], m_prob[:, src:src + P], ident)
                        if j % 4 == 3:
                            mm.then_inc(m_turned, 1)

                def chunk(n):
                    t, r = n // 2, slice((n % 2) * CHUNK, (n % 2 + 1) * CHUNK)
                    v = v_new if n else u_tok
                    if n:
                        pe.wait_ge(state_ready, 4 * n)
                        for hd in range(GH):
                            mm = nc.tensor.matmul(q[r, 0, hd * P:(hd + 1) * P], wT[:, 4 * t + hd, r],
                                                  states[n % 2][:, hd, :], start=True, stop=True)
                        mm.then_inc(read_out, 1)
                        pe.wait_ge(v_new_ready, n)
                    if n < 3:
                        for hd in range(GH):
                            c = slice(hd * P, (hd + 1) * P)
                            mm = nc.tensor.matmul(q[:, 2, c], k_dec[r, t, c], v[r, t, c], start=True, stop=True)
                        mm.then_inc(kv_made, 1)
                    for hd in range(GH):
                        c = slice(hd * P, (hd + 1) * P)
                        if n:
                            nc.tensor.matmul(q[r, 1 + 2 * t, c], qdT[:, hd, t * P + r.start:t * P + r.stop],
                                             states[n % 2][:, hd, :], start=True, stop=False)
                        mm = nc.tensor.matmul(q[r, 1 + 2 * t, c], attnT[r, 4 * t + hd, r], v[r, t, c],
                                              start=n == 0, stop=True)
                    if n % 2:
                        mm.then_inc(o_made, 1)

                pe.wait_ge(solved_kept, 2)
                pe.wait_ge(rhs_ready, 6)
                chunk(0)
                pe.wait_ge(m_probT_act, 2)
                pe.wait_ge(m_probT_dve, 1)
                for hd in range(GH):
                    for t in range(TT):
                        c = hd * SEQ + t * P
                        for kt in range(t + 1):
                            src = (t * GH + hd * (t + 1) + kt) * P
                            mm = nc.tensor.matmul(y[:, 0, c:c + P], m_val[:, kt, hd * P:(hd + 1) * P],
                                                  m_probT[:, src:src + P], start=kt == 0, stop=kt == t)
                mm.then_inc(m_mixed, 1)
                chunk(1)
                pe.wait_ge(emix_ready, 2)
                row_slabs(n0 + N_OUT, 0, 1, xT_hi, xT_lo, True, False, block=out_block, more=True)
                chunk(2)
                chunk(3)
                row_slabs(n0 + N_OUT, 1, 4, xT_hi, xT_lo, False, False, block=out_block, more=True)
                pe.wait_ge(o_ready, TT)
                for hd in range(GH):
                    for t in range(TT):
                        c = hd * SEQ + t * P
                        mm = nc.tensor.transpose(q_flat[:, c:c + P], o_tok[:, t, hd * P:(hd + 1) * P], ident)
                mm.then_inc(o_turned, 1)
                pe.wait_ge(emix_ready, 4)
                row_slabs(n0 + N_OUT, 4, KD - 2, xT_hi, xT_lo, False, False, block=out_block, more=True)
                turn_embeddings(0)
                row_slabs(n0 + N_OUT, KD - 2, KD, xT_hi, xT_lo, False, True, block=out_block)
                project_embeddings(0)

            def pair_slab(n, j, t, width, c0, name=None, to=None):
                pe.wait_ge(lo_ready, n + 1)
                if name:
                    wait_xT(name, t, 2 * j)
                a = slice(t * P, (t + 1) * P)
                for k in (2 * j, 2 * j + 1):
                    w = slice((k % 2) * width, (k % 2 + 1) * width)
                    mm = split_product(y[:, t, c0:c0 + width] if to is None else to, xT_hi[:, k, a], xT_lo[:, k, a],
                                       hi[:, n % RING, w], lo[:, n % RING, w], k == 0, k == KD - 1)
                return mm

            stay_warm(mains[0])
            pe.wait_ge(ident_loaded, 16)
            pe.wait_ge(rows_loaded, 16 * n_row_loads)
            nc.tensor.transpose(q[:, 3, 0:P], rows[:, :], ident).then_inc(cols_turned, 1)
            pe.wait_ge(cols_ready, 1)
            for name in mains:
                if norm_of[name]:
                    stay_warm(name)
                if name.startswith("ffn"):
                    ffn(name)
                elif name.startswith("gate"):
                    pe.wait_ge(bias_ready, 1)
                    gate(name)
                elif name == "mix1":
                    odd(name)
                elif name == "mix0":
                    even(name)


_INS = ["x", "p", "ffn1_pre", "ffn1_wgu", "ffn1_wd", "ffn1_post", "mix_pre", "mix_post", "ffn2_pre", "ffn2_wgu",
        "ffn2_wd", "ffn2_post", "ple_gate_w", "ple_gate_b", "ple_proj", "ple_norm", "ab_w_in", "gdn_conv",
        "gdn_a_log", "gdn_dt_bias", "gdn_out_norm", "mla_q_norm", "mla_w_uq", "mla_kv_norm", "mla_w_ukv",
        "ab_w_out", "swa_w_qkv", "swa_b_qkv", "swa_sinks", "swa_w_o", "swa_b_o"]
PHASES = ["ffn1_0", "mix0", "ffn2_0", "gate0", "ffn1_1", "mix1", "ffn2_1", "gate1"]


def kernel(**inputs):
    import concourse.bacc as bacc
    from concourse.bass_utils import run_bass_kernel_spmd

    nc = bacc.Bacc("TRN2", target_bir_lowering=False, num_devices=1)
    arrays = {f"in_{n}": np.ascontiguousarray(inputs[n]) for n in _INS}
    arrays["in_const"] = shape_constants()
    io = {n[3:]: nc.dram_tensor(n, a.shape, mybir.dt.from_np(a.dtype), kind="ExternalInput").ap()
          for n, a in arrays.items()}
    out = nc.dram_tensor("out", (1, SEQ, D), F32, kind="ExternalOutput").ap()
    encoder(nc, io, out, PHASES)
    r = run_bass_kernel_spmd(nc, [arrays], core_ids=[0])
    return r.results[0]["out"]
```
